# Optimizing a Trainium2 kernel written in Bass

```python
import jax, jax.numpy as jnp
from jax import lax
import numpy as np

D_MODEL = 1024
BATCH = 1
SEQ = 512
DEPTH = 1
DEC_BATCH = 8
DEC_SEQ = 4
PAST_LEN = 1024
PAGE_SIZE = 128

N_HEADS = 8
HEAD_DIM = D_MODEL // 16
ATT_WIDTH = N_HEADS * HEAD_DIM
CONV_CH = D_MODEL // 2
CONV_WIDTH = 31
D_FF = ((8 * D_MODEL // 3 + 255) // 256) * 256
Q_BLOCK = 128
EPS = 1e-6
ATT_BIAS_INIT = -7.0
IN_WIDTH = 2 * CONV_CH + 3 * ATT_WIDTH + 2 * D_MODEL

kernel_name = "conformer_conv_stickbreaking_gated_hybrid_step"

def rms_norm(x, g):
    xf = x.astype(jnp.float32)
    y = xf * lax.rsqrt(jnp.mean(xf * xf, axis=-1, keepdims=True) + EPS)
    return (y * g.astype(jnp.float32)).astype(x.dtype)

def layer_norm(x, g, b):
    xf = x.astype(jnp.float32)
    mu = jnp.mean(xf, axis=-1, keepdims=True)
    var = jnp.mean(jnp.square(xf - mu), axis=-1, keepdims=True)
    y = (xf - mu) * lax.rsqrt(var + EPS)
    return (y * g.astype(jnp.float32) + b.astype(jnp.float32)).astype(x.dtype)

def stick_breaking_block(q, k, v, bias, q_pos, k_pos):
    z = jnp.einsum('bqhd,bshd->bhqs', q.astype(jnp.float32), k.astype(jnp.float32)) * (HEAD_DIM ** -0.5)
    z = z + bias.astype(jnp.float32)[None, :, None, None]
    mask = k_pos[None, :] < q_pos[:, None]
    c = jnp.where(mask, jax.nn.softplus(z), 0.0)
    rev = lax.cumsum(c, axis=3, reverse=True)
    log_a = jax.nn.log_sigmoid(z) - (rev - c)
    a = jnp.where(mask, jnp.exp(log_a), 0.0)
    o = jnp.einsum('bhqs,bshd->bqhd', a, v.astype(jnp.float32))
    return o.astype(v.dtype)

def stick_breaking(q, k, v, bias, q_pos, k_pos):
    b, t = q.shape[0], q.shape[1]
    if t > Q_BLOCK and t % Q_BLOCK == 0:
        nb = t // Q_BLOCK
        qb = q.reshape(b, nb, Q_BLOCK, N_HEADS, HEAD_DIM).transpose(1, 0, 2, 3, 4)
        pb = q_pos.reshape(nb, Q_BLOCK)
        ob = lax.map(lambda a: stick_breaking_block(a[0], k, v, bias, a[1], k_pos), (qb, pb))
        return ob.transpose(1, 0, 2, 3, 4).reshape(b, t, N_HEADS, HEAD_DIM)
    return stick_breaking_block(q, k, v, bias, q_pos, k_pos)

def conv_branch(u, buf, w_dw, b_dw, ln_g, ln_b, w_out):
    full = jnp.concatenate([buf.astype(u.dtype), u], axis=1)
    y = lax.conv_general_dilated(full, w_dw[:, None, :], window_strides=(1,), padding='VALID',
                                 dimension_numbers=('NWC', 'WIO', 'NWC'),
                                 feature_group_count=CONV_CH) + b_dw
    y = jax.nn.silu(layer_norm(y, ln_g, ln_b))
    return y @ w_out, full[:, -(CONV_WIDTH - 1):]

def layer(x, conv_buf, past_k, past_v, q_pos, k_pos,
          g_pre_mix, g_post_mix, g_pre_ffn, g_post_ffn, w_in, conv_dw, conv_b,
          conv_ln_g, conv_ln_b, w_conv_out, att_bias, w_att_out, w_o, w_ffn_in, w_ffn_out):
    b, t, _ = x.shape
    h = rms_norm(x, g_pre_mix)
    proj = h @ w_in
    o1 = 2 * CONV_CH
    o2 = o1 + 3 * ATT_WIDTH
    glu = proj[..., :o1]
    qkv = proj[..., o1:o2]
    gates = proj[..., o2:]
    u = glu[..., :CONV_CH] * jax.nn.sigmoid(glu[..., CONV_CH:])
    conv_d, new_buf = conv_branch(u, conv_buf, conv_dw, conv_b, conv_ln_g, conv_ln_b, w_conv_out)
    q, k, v = jnp.split(qkv, 3, axis=-1)
    q = q.reshape(b, t, N_HEADS, HEAD_DIM)
    k = k.reshape(b, t, N_HEADS, HEAD_DIM)
    v = v.reshape(b, t, N_HEADS, HEAD_DIM)
    if past_k is None:
        k_all, v_all = k, v
    else:
        k_all = jnp.concatenate([past_k.astype(k.dtype), k], axis=1)
        v_all = jnp.concatenate([past_v.astype(v.dtype), v], axis=1)
    att = stick_breaking(q, k_all, v_all, att_bias, q_pos, k_pos).reshape(b, t, ATT_WIDTH)
    att_d = att @ w_att_out
    merged = jax.nn.sigmoid(gates[..., :D_MODEL]) * conv_d + jax.nn.sigmoid(gates[..., D_MODEL:]) * att_d
    x = x + rms_norm(merged @ w_o, g_post_mix)
    hf = rms_norm(x, g_pre_ffn) @ w_ffn_in
    ff = (jax.nn.silu(hf[..., :D_FF]) * hf[..., D_FF:]) @ w_ffn_out
    x = x + rms_norm(ff, g_post_ffn)
    return x, k, v, new_buf

def setup_inputs(seed: int = 0) -> dict:
    key = jax.random.key(seed)
    ks = jax.random.split(key, 24)
    n_pages = PAST_LEN // PAGE_SIZE
    n_used = DEC_BATCH * n_pages
    n_phys = n_used + (n_used + 3) // 4
    nrm = lambda k, shape, s: jax.random.normal(k, shape, jnp.float32) * s
    page_table = jax.random.permutation(ks[5], n_phys)[:n_used].reshape(DEC_BATCH, n_pages).astype(jnp.int32)
    return {
        "x_prompt": nrm(ks[0], (BATCH, SEQ, D_MODEL), 1.0),
        "x_sample": nrm(ks[1], (DEC_BATCH, DEC_SEQ, D_MODEL), 1.0),
        "cache_k": nrm(ks[2], (DEPTH, n_phys, PAGE_SIZE, N_HEADS, HEAD_DIM), 1.0),
        "cache_v": nrm(ks[3], (DEPTH, n_phys, PAGE_SIZE, N_HEADS, HEAD_DIM), 1.0),
        "state_conv": nrm(ks[4], (DEPTH, DEC_BATCH, CONV_WIDTH - 1, CONV_CH), 0.5),
        "page_table": page_table,
        "norm_pre_mix": 1.0 + nrm(ks[6], (DEPTH, D_MODEL), 0.05),
        "norm_post_mix": 1.0 + nrm(ks[7], (DEPTH, D_MODEL), 0.05),
        "norm_pre_ffn": 1.0 + nrm(ks[8], (DEPTH, D_MODEL), 0.05),
        "norm_post_ffn": 1.0 + nrm(ks[9], (DEPTH, D_MODEL), 0.05),
        "w_in": nrm(ks[10], (DEPTH, D_MODEL, IN_WIDTH), D_MODEL ** -0.5),
        "conv_dw": nrm(ks[11], (DEPTH, CONV_WIDTH, CONV_CH), CONV_WIDTH ** -0.5),
        "conv_b": nrm(ks[12], (DEPTH, CONV_CH), 0.01),
        "conv_ln_g": 1.0 + nrm(ks[13], (DEPTH, CONV_CH), 0.05),
        "conv_ln_b": nrm(ks[14], (DEPTH, CONV_CH), 0.01),
        "w_conv_out": nrm(ks[15], (DEPTH, CONV_CH, D_MODEL), CONV_CH ** -0.5),
        "att_bias": ATT_BIAS_INIT + nrm(ks[20], (DEPTH, N_HEADS), 0.1),
        "w_att_out": nrm(ks[16], (DEPTH, ATT_WIDTH, D_MODEL), ATT_WIDTH ** -0.5),
        "w_o": nrm(ks[17], (DEPTH, D_MODEL, D_MODEL), D_MODEL ** -0.5),
        "w_ffn_in": nrm(ks[18], (DEPTH, D_MODEL, 2 * D_FF), D_MODEL ** -0.5),
        "w_ffn_out": nrm(ks[19], (DEPTH, D_FF, D_MODEL), D_FF ** -0.5),
    }

def reference(x_prompt, x_sample, cache_k, cache_v, state_conv, page_table,
              norm_pre_mix, norm_post_mix, norm_pre_ffn, norm_post_ffn, w_in, conv_dw, conv_b,
              conv_ln_g, conv_ln_b, w_conv_out, att_bias, w_att_out, w_o, w_ffn_in, w_ffn_out):
    t_p = x_prompt.shape[1]
    t_s = x_sample.shape[1]
    dec_b = x_sample.shape[0]
    n_pages = PAST_LEN // PAGE_SIZE
    pos_p = jnp.arange(t_p, dtype=jnp.int32)
    q_pos_s = PAST_LEN + jnp.arange(t_s, dtype=jnp.int32)
    k_pos_s = jnp.arange(PAST_LEN + t_s, dtype=jnp.int32)
    zero_buf = jnp.zeros((x_prompt.shape[0], CONV_WIDTH - 1, CONV_CH), x_prompt.dtype)

    hp, hs = x_prompt, x_sample
    kp_l, vp_l, cp_l, ks_l, vs_l, cs_l = [], [], [], [], [], []
    for l in range(DEPTH):
        params = (norm_pre_mix[l], norm_post_mix[l], norm_pre_ffn[l], norm_post_ffn[l], w_in[l],
                  conv_dw[l], conv_b[l], conv_ln_g[l], conv_ln_b[l], w_conv_out[l], att_bias[l],
                  w_att_out[l], w_o[l], w_ffn_in[l], w_ffn_out[l])
        hp, kp, vp, cp = layer(hp, zero_buf, None, None, pos_p, pos_p, *params)
        past_k = cache_k[l][page_table].reshape(dec_b, n_pages * PAGE_SIZE, N_HEADS, HEAD_DIM)
        past_v = cache_v[l][page_table].reshape(dec_b, n_pages * PAGE_SIZE, N_HEADS, HEAD_DIM)
        hs, kn, vn, cn = layer(hs, state_conv[l], past_k, past_v, q_pos_s, k_pos_s, *params)
        kp_l.append(kp); vp_l.append(vp); cp_l.append(cp)
        ks_l.append(kn); vs_l.append(vn); cs_l.append(cn)

    k_prompt = jnp.stack(kp_l)
    v_prompt = jnp.stack(vp_l)
    conv_prompt = jnp.stack(cp_l)
    k_sample = jnp.stack(ks_l)
    v_sample = jnp.stack(vs_l)
    conv_sample = jnp.stack(cs_l)
    return (hp, hs, k_prompt, v_prompt, conv_prompt, k_sample, v_sample, conv_sample)


_drawn_inputs = setup_inputs


def setup_inputs(seed=0):
    import zlib

    import numpy as np

    out = dict(_drawn_inputs(seed))
    spreads = {}
    factors = {'conv_b': 3.485, 'conv_ln_b': 7.182, 'att_bias': 8.0}
    for name, (base, spread) in spreads.items():
        noise = np.random.default_rng([zlib.crc32(name.encode()), seed]).standard_normal(out[name].shape)
        drawn = base * np.exp(spread * noise) if base else spread * noise
        out[name] = __import__('jax').numpy.asarray(drawn.astype(out[name].dtype))
    for name, factor in factors.items():
        out[name] = (out[name] * factor).astype(out[name].dtype)
    return out
```

```python
from contextlib import ExitStack

import numpy as np

import concourse.bass as bass
from concourse import mybir

F32 = mybir.dt.float32
F32R = mybir.dt.float32r
I32 = mybir.dt.int32
ALU = mybir.AluOpType
ACT = mybir.ActivationFunctionType
AX = mybir.AxisListType

P = 128
D = 1024
S = 512
NB, NT = 8, 4
NS = NB * NT
T = S + NS
HT = T // 2
S1 = S - HT
H, DH = 8, 64
C = 512
CW = 31
HIST = CW - 1
PAGES, PAGE = 8, 128
PAST = PAGES * PAGE
FF = 2816
KD, KC, KF = D // P, C // P, FF // P
EPS = 1e-6
SCALE = DH ** -0.5
UC = 256
UK = 8
MT = UC // P
RING = 2
GB = 4
GROUPS = NB // GB

COL_GLU_A, COL_GLU_B, COL_Q, COL_K, COL_V, COL_GC, COL_GA = 0, 512, 1024, 1536, 2048, 2560, 3584
FIRST_UNITS = [COL_GLU_B, COL_GLU_A, COL_GLU_B + UC, COL_GLU_A + UC, COL_Q, COL_Q + UC,
               COL_K, COL_K + UC, COL_V, COL_V + UC]
U_IN, U_MERGE, U_WO, U_FFI, U_FFO = 0, 10, 22, 26, 48
A_IN, A_MERGE, A_WO, A_FFI = 0, 20, 52, 60

K_ID, K_TRI, K_ONE, K_NEW, K_SEL, K_HEAD, K_EPS = 0, 128, 256, 384, 448, 464, 976
K_COLS = 977


def constants():
    c = np.zeros((P, K_COLS), np.float32)
    r = np.arange(P)
    b, h, q = r // 32, r // NT % H, r % NT
    c[:, K_ID:K_ID + P] = np.eye(P)
    c[:, K_TRI:K_TRI + P] = r[None, :] < r[:, None]
    c[:, K_ONE:K_ONE + P] = 1.0
    n = np.arange(NS)
    for g in range(GROUPS):
        c[:, K_NEW + NS * g:K_NEW + NS * (g + 1)] = (n[None] // NT == GB * g + b[:, None]) & (n[None] % NT < q[:, None])
    m = np.arange(GB * NT)
    c[:, K_SEL:K_SEL + GB * NT] = (m[None] // NT == b[:, None]) & (m[None] % NT == q[:, None])
    c[:, K_HEAD:K_HEAD + H * DH] = np.arange(H * DH)[None] // DH == h[:, None]
    c[:, K_EPS] = EPS
    return c


def attention_steps():
    prompt = [(k, h) for h in range(H) for k in ("PS", "PT", "PO")]
    steps, n = [], 0

    def piece():
        nonlocal n
        if n < len(prompt):
            steps.append(prompt[n])
            n += 1

    for g in range(GROUPS):
        for j in range(PAGES):
            steps.append(("KT", g, j))
            if j:
                steps.append(("SC", g, j - 1))
            if j % 4 != 1:
                piece()
        steps += [("SC", g, PAGES - 1), ("ZN", g)]
        piece()
        steps.append(("AT", g))
        for j in range(PAGES):
            steps.append(("PV", g, j))
            if j % 4 != 1 and j != 7:
                piece()
        steps += [("PN", g)]
        if g == GROUPS - 1:
            while n < len(prompt):
                piece()
        steps += [("SO", g)]
    assert n == len(prompt)
    return steps


class Semaphores:

    def __init__(self, new):
        self.ld_const = new("ld_const")
        self.ld_par = new("ld_par")
        self.ld_x0 = new("ld_x0")
        self.ld_x1 = new("ld_x1")
        self.ld_state = new("ld_state")
        self.ld_table = new("ld_table")
        self.stored = new("stored")
        self.kv_stored = new("kv_stored")
        self.hi_done = new("hi_done")
        self.split_done = new("split_done")
        self.unit_used = new("unit_used")
        self.par_done = new("par_done")
        self.par_read = new("par_read")
        self.bias_ready = new("bias_ready")
        self.st_done = new("st_done")
        self.st_read = new("st_read")
        self.xt_done = new("xt_done")
        self.x_copied = new("x_copied")
        self.sq_ready = new("sq_ready")
        self.ssq_done = new("ssq_done")
        self.std_ready = new("std_ready")
        self.norm_t = new("norm_t")
        self.norm_h = new("norm_h")
        self.norm_l = new("norm_l")
        self.zeroed = new("zeroed")
        self.sconv_done = new("sconv_done")
        self.conv_done = new("conv_done")
        self.dconv_done = new("dconv_done")
        self.conv_tap = new("conv_tap")
        self.vt_done = new("vt_done")
        self.vt_read = new("vt_read")
        self.ktok_done = new("ktok_done")
        self.ktok_read = new("ktok_read")
        self.cout_done = new("cout_done")
        self.cout_read = new("cout_read")
        self.page_used = new("page_used")
        self.kt_done = new("kt_done")
        self.score_done = new("score_done")
        self.z_read = new("z_read")
        self.weight_s = new("weight_s")
        self.own_done = new("own_done")
        self.own_ready = new("own_ready")
        self.attT_done = new("attT_done")
        self.attT_hi = new("attT_hi")
        self.pscore_done = new("pscore_done")
        self.pscore_read = new("pscore_read")
        self.pweight = new("pweight")
        self.ptr_done = new("ptr_done")
        self.ptr_read = new("ptr_read")
        self.pv_done = new("pv_done")
        self.pv_hi = new("pv_hi")
        self.pv_read = new("pv_read")
        self.ln_sum = new("ln_sum")
        self.ln_cent = new("ln_cent")
        self.ln_sq = new("ln_sq")
        self.ln_sqsum = new("ln_sqsum")
        self.ln_t = new("ln_t")
        self.ln_sig = new("ln_sig")
        self.ln_y = new("ln_y")
        self.ln_hi = new("ln_hi")
        self.ln_lo = new("ln_lo")
        self.dve_step = new("dve_step")
        self.merged_t = new("merged_t")
        self.merged_hi = new("merged_hi")
        self.merged_lo = new("merged_lo")
        self.wo_sum = new("wo_sum")
        self.silu_ready = new("silu_ready")
        self.act_hi = new("act_hi")
        self.act_lo = new("act_lo")
        self.x1_ready = new("x1_ready")
        self.sq_ready2 = new("sq_ready2")
        self.out_acc_done = new("out_acc_done")
        self.out_acc_read = new("out_acc_read")
        self.y_ready = new("y_ready")
        self.yt_done = new("yt_done")
        self.yt_read = new("yt_read")
        self.raw_loaded = [new("raw_loaded0"), new("raw_loaded1")]
        self.pages_loaded = [new("pages_loaded0"), new("pages_loaded1")]
        self.acc_done = [new("acc_done0"), new("acc_done1")]
        self.acc_read = [new("acc_read0"), new("acc_read1")]
        self.kt_read = [new("kt_read0"), new("kt_read1")]


class Count:

    def __init__(self):
        self.n = 0

    def up(self):
        self.n = self.n + 1
        return 1


def layer_kernel(nc, x_prompt, x_sample, cache_k, cache_v, state_conv, page_table, g_pre_mix, g_post_mix,
                 g_pre_ffn, g_post_ffn, w_in, conv_dw, conv_b, conv_ln_g, conv_ln_b, w_conv_out, att_bias,
                 w_att_out, w_o, w_ffn_in, w_ffn_out, consts,
                 y_prompt, y_sample, k_prompt, v_prompt, conv_prompt, k_sample, v_sample, conv_sample):
    n_phys = cache_k.shape[1]
    rows = lambda w: w[0].rearrange("(k p) c -> p k c", p=P)
    win_v, wconv_v, watt_v, wo_v, wfi_v, wfo_v = map(rows, (w_in, w_conv_out, w_att_out, w_o, w_ffn_in, w_ffn_out))
    STEPS = attention_steps()

    with ExitStack() as ctx:
        arena_bytes = 212768
        arena = ctx.enter_context(nc.sbuf_tensor("arena", [P, arena_bytes // 4], F32))
        base = nc.sbuf_base - arena_bytes

        def at(name, shape, dt, offset):
            size = 4 * int(np.prod(shape[1:]))
            assert offset % 32 == 0 and offset + size <= arena_bytes, (name, offset, size)
            return nc.alloc_sbuf_tensor_at(name, shape, dt, offset=base + offset)

        kc = at("consts", [P, K_COLS], F32, 0)
        vec = at("vec", [P, 44], F32, 3936)
        dw = at("dw", [P, KC, CW], F32, 4128)
        bias_h = at("bias_h", [P, H], F32, 4640)
        bias_r = at("bias_r", [P, 1], F32, 4672)
        ptab = at("ptab", [1, NB * PAGES], I32, 4704)
        O = 4960
        ident, tri, ones = kc[:, K_ID:K_ID + P], kc[:, K_TRI:K_TRI + P], kc[:, K_ONE:K_ONE + P]
        newmask = lambda g: kc[:, K_NEW + NS * g:K_NEW + NS * (g + 1)]
        selq, headmask, eps = kc[:, K_SEL:K_SEL + GB * NT], kc[:, K_HEAD:K_HEAD + C], kc[:, K_EPS:K_EPS + 1]
        gain = lambda n, k: vec[:, 8 * n + k:8 * n + k + 1]
        cvec = lambda n, k: vec[:, 32 + KC * n + k:33 + KC * n + k]

        TB = 4 * T
        xT = at("xT", [P, KD, T], F32, O)
        hH = at("hH", [P, KD, T], F32R, O + KD * TB)
        hL = at("hL", [P, KD, T], F32R, O + 2 * KD * TB)
        pout = at("pout", [P, KD, T], F32, O + KD * TB)
        W0 = O + 3 * KD * TB
        w_raw = at("w_raw", [P, RING, UK, UC], F32, W0)
        w_hi = at("w_hi", [P, RING, UK, UC], F32R, W0 + 16384)
        w_lo = at("w_lo", [P, RING, UK, UC], F32R, W0 + 32768)
        pages = at("pages", [P, RING, GB, C], F32, W0)
        keysT = at("keysT", [P, RING, GB, KC, P], F32, W0 + 16384)
        LS = PAST + NS
        beta_s = at("beta_s", [P, LS], F32, W0 + 32768)
        stick_s = at("stick_s", [P, LS + 1], F32, W0 + 36992)
        wgtT_s = at("wgtT_s", [P, PAGES + 1, P], F32, W0 + 41248)
        own_s = at("own_s", [P, C], F32, W0 + 45856)
        B = W0 + 49152
        acH = at("acH", [P, 2 * KC, T], F32R, B)
        acL = at("acL", [P, 2 * KC, T], F32R, B + 17408)
        yc = at("yc", [P, KC, T], F32, B + 17408 + KC * TB)
        q_even = at("q_even", [P, KC, S], F32, B + 34816)
        q_odd = at("q_odd", [P, KC, S], F32, B + 43008)
        q_s = at("q_s", [P, NB, KC, H, NT], F32, B + 51200)
        kT = at("kT", [P, KC, T], F32, B + 55296)
        vT = at("vT", [P, KC, T], F32, B + 64000)
        k_tok = at("k_tok", [P, S // P, C], F32, B + 72704)
        ks_tok = at("ks_tok", [NS, C], F32, B + 80896)
        v_tok = at("v_tok", [P, S // P, C], F32, B + 82944)
        vs_tok = at("vs_tok", [P, C], F32, B + 91136)
        uP = at("uP", [P, KC, HIST + S], F32, B + 93184)
        uS = at("uS", [P, KC, NB, HIST + NT], F32, B + 101856)
        x_tok = at("x_tok", [P, S // P, D], F32, B)
        xs_tok = at("xs_tok", [NS, D], F32, B + 16384)
        st_tok = at("st_tok", [GB * HIST, GROUPS, C], F32, B + 20480)
        par = at("par", [44, P], F32, B + 24576)
        dw_tok = at("dw_tok", [CW, C], F32, B + 25088)
        ab_tok = at("ab_tok", [1, H], F32, B + 27136)
        sq0 = at("sq0", [P, RING, T], F32, B + 55296)
        std0 = at("std0", [P, T], F32, B + 59648)
        tmp0 = at("tmp0", [P, RING, T], F32, B + 64000)
        sig_u = at("sig_u", [P, MT, T], F32, B + 72704)
        prod = at("prod", [P, NT, NB, CW], F32, B + 72704 + 4352)
        u_new = at("u_new", [P, KC, NS], F32, B + 72704 + 8320)
        conv_tail = at("conv_tail", [HIST, C], F32, B + 8704)
        conv_new = at("conv_new", [NS, C], F32, B + 10752)
        tap_prod = at("tap_prod", [P, 2, S], F32, B + 12800)
        WID = [P * (i + 1) for i in range(S // P)]
        POS = [sum(WID[:i]) for i in range(S // P)]
        beta_p = at("beta_p", [P, sum(WID)], F32, B + 64000)
        stick_p = at("stick_p", [P, RING, 516], F32, B + 69120)
        wgtT_p = at("wgtT_p", [P, sum(WID)], F32, B + 73248)
        sq1 = at("sq1", [P, RING, T], F32, B + 82944)
        std1 = at("std1", [P, T], F32, B + 87296)
        tmp1 = at("tmp1", [P, RING, T], F32, B + 89472)
        sig1 = at("sig1", [P, RING, T], F32, B + 93824)
        mH = at("mH", [P, KD, T], F32R, B + 34816)
        mL = at("mL", [P, KD, T], F32R, B + 52224)
        sig_c = at("sig_c", [P, MT, T], F32, B + 69632)
        sig_a = at("sig_a", [P, MT, T], F32, B + 73984)
        part = at("part", [P, MT, T], F32, B + 78336)
        both = at("both", [P, MT, T], F32, B + 82688)
        actH = at("actH", [P, KF, T], F32R, B)
        actL = at("actL", [P, KF, T], F32R, B + KF * TB)
        tmp2 = at("tmp2", [P, RING, T], F32, B + 87040)
        sig_f = at("sig_f", [P, MT, T], F32, B + 95744)
        up_f = at("up_f", [P, MT, T], F32, B + 100096)
        sq2 = at("sq2", [P, RING, T], F32, B + 95744)
        ssum = at("ssum", [P, T], F32, B + 100096)
        std2 = at("std2", [P, T], F32, B + 102272)
        y_tok = at("y_tok", [P, S // P + 1, D], F32, B)

        ps = ctx.enter_context(nc.psum_tensor("ps", [P, 8, 512], F32))

        s = Semaphores(lambda name: ctx.enter_context(nc.semaphore(name)))
        raw_loaded, acc_done, acc_read, pages_loaded, kt_read = s.raw_loaded, s.acc_done, s.acc_read, s.pages_loaded, s.kt_read



        halves = lambda a: a.rearrange("p (h t) -> p h t", h=2)
        acc = lambda c: ps[:, 2 * (c % 2):2 * (c % 2) + 2, 0:HT]
        block = ctx.enter_context(nc.Block())

        @block.sync
        def _(sp):
            sp.dma_start(kc[:], consts).then_inc(s.ld_const, 16)
            for n, g in enumerate((g_pre_mix, g_post_mix, g_pre_ffn, g_post_ffn)):
                sp.dma_start(par[8 * n:8 * n + 8, :], g[0].rearrange("(k p) -> k p", p=P)).then_inc(s.ld_par, 16)
            for n, g in enumerate((conv_b, conv_ln_g, conv_ln_b)):
                sp.dma_start(par[32 + KC * n:36 + KC * n, :], g[0].rearrange("(k p) -> k p", p=P)).then_inc(s.ld_par, 16)
            sp.dma_start(dw_tok[:], conv_dw[0]).then_inc(s.ld_par, 16)
            sp.dma_start(ab_tok[:], att_bias).then_inc(s.ld_par, 16)
            xp_v, xs_v = x_prompt[0].rearrange("(j p) d -> p j d", p=P), x_sample.rearrange("b t d -> (b t) d")
            for half, sem in enumerate((s.ld_x0, s.ld_x1)):
                cols = slice(512 * half, 512 * half + 512)
                sp.dma_start(x_tok[:, :, cols], xp_v[:, :, cols]).then_inc(sem, 16)
                sp.dma_start(xs_tok[:, cols], xs_v[:, cols]).then_inc(sem, 16)

            def load_unit(par_, lo, hi, need=None):
                if need is not None:
                    sp.wait_ge(s.split_done, need)
                sp.dma_start(w_raw[:, par_, 0:4], lo).then_inc(raw_loaded[par_], 16)
                sp.dma_start(w_raw[:, par_, 4:4 + hi.shape[1]], hi).then_inc(raw_loaded[par_], 16)

            def columns(v, c, k0=0, k1=UK):
                return v[:, k0:k0 + 4, bass.ds(c, UC)], v[:, k0 + 4:k1, bass.ds(c, UC)]

            load_unit(0, *columns(win_v, FIRST_UNITS[0]))
            sp.dma_start(st_tok[:], state_conv[0].rearrange("(g b) r c -> (b r) g c", g=GROUPS)).then_inc(s.ld_state, 16)
            sp.dma_start(ptab[:], page_table.rearrange("(o b) n -> o (b n)", o=1)).then_inc(s.ld_table, 16)
            load_unit(1, *columns(win_v, FIRST_UNITS[1]))
            sp.dma_start(conv_sample[0, :, 0:HIST - NT, :], state_conv[0, :, NT:HIST, :]).then_inc(s.stored, 16)
            for n in range(2, U_MERGE):
                load_unit(n % 2, *columns(win_v, FIRST_UNITS[n]), need=n - 1)

            sp.wait_ge(s.ld_table, 16)
            cache = (cache_k[0].rearrange("n r h d -> n r (h d)"), cache_v[0].rearrange("n r h d -> n r (h d)"))

            def load_pages(g, kv, j, slot):
                for b in range(GB):
                    page = sp.value_load(ptab[0:1, bass.ds((GB * g + b) * PAGES + j, 1)], min_val=0, max_val=n_phys - 1)
                    sp.dma_start(pages[:, slot, b, :], cache[kv][bass.ds(page, 1)].rearrange("n r c -> r (n c)"))\
                        .then_inc(pages_loaded[slot], 16)

            sp.wait_ge(s.split_done, U_MERGE)
            for slot in range(RING):
                load_pages(0, 0, slot, slot)
            sp.wait_ge(s.vt_read, KC + 1)
            sp.dma_start(v_prompt[0, 0].rearrange("(j p) h d -> p j (h d)", p=P), v_tok[:]).then_inc(s.kv_stored, 16)
            sp.dma_start(v_sample[0].rearrange("b t h d -> (b t) (h d)"), vs_tok[0:NS, :]).then_inc(s.kv_stored, 16)
            sp.wait_ge(s.ktok_read, KC + 1)
            sp.dma_start(k_prompt[0, 0].rearrange("(j p) h d -> p j (h d)", p=P), k_tok[:]).then_inc(s.kv_stored, 16)
            sp.dma_start(k_sample[0].rearrange("b t h d -> (b t) (h d)"), ks_tok[:]).then_inc(s.kv_stored, 16)
            sp.wait_ge(s.cout_read, 2)
            sp.dma_start(conv_prompt[0, 0], conv_tail[:]).then_inc(s.kv_stored, 16)
            for b in range(NB):
                sp.dma_start(conv_sample[0, b, HIST - NT:HIST, :], conv_new[NT * b:NT * b + NT, :]).then_inc(s.kv_stored, 16)

            def keys_used(g, j):
                return GB * (PAGES * g + j + 1) + 3 * g

            for g in range(GROUPS):
                for kv in range(2):
                    for slot in range(RING):
                        if kv:
                            sp.wait_ge(s.kt_done, keys_used(g, PAGES - RING + slot))
                        elif g:
                            sp.wait_ge(s.page_used, PAGES * g - RING + slot + 1)
                        if kv or g:
                            load_pages(g, kv, slot, slot)
                    with sp.Fori(1, PAGES // RING) as i:
                        for slot in range(RING):
                            if kv:
                                sp.wait_ge(s.page_used, i * RING + (PAGES * g + slot - RING + 1))
                            else:
                                sp.wait_ge(s.kt_done, i * (RING * GB) + keys_used(g, slot - RING))
                            load_pages(g, kv, i * RING + slot, slot)

            sp.wait_ge(s.page_used, GROUPS * PAGES)
            for mp in range(D // UC):
                for j in range(3):
                    n = U_MERGE + 3 * mp + j
                    if j < 2:
                        src = columns(win_v, (COL_GC, COL_GA)[j] + UC * mp)
                    else:
                        src = wconv_v[:, :, UC * mp:UC * mp + UC], watt_v[:, :, UC * mp:UC * mp + UC]
                    load_unit(n % 2, *src, need=n - 1)
            for m in range(D // UC):
                n = U_WO + m
                load_unit(n % 2, *columns(wo_v, UC * m), need=n - 1)
            with sp.Fori(0, FF // UC) as i:
                for j in range(2):
                    load_unit(j, *columns(wfi_v, i * UC + j * FF), need=i * 2 + (U_FFI + j - 1))
            for mp in range(D // UC):
                for j in range(3):
                    n = U_FFO + 3 * mp + j
                    load_unit(n % 2, *columns(wfo_v, UC * mp, 8 * j, min(8 * j + 8, KF)), need=n - 1)

            yp_v = y_prompt[0].rearrange("(j p) d -> p j d", p=P)
            for half in range(2):
                sp.wait_ge(s.yt_read, (KD // 2) * (half + 1))
                cols = slice(512 * half, 512 * half + 512)
                sp.dma_start(yp_v[:, :, cols], y_tok[:, 0:4, cols]).then_inc(s.stored, 16)
                sp.dma_start(y_sample.rearrange("b t d -> (b t) d")[:, cols], y_tok[0:NS, 4, cols]).then_inc(s.stored, 16)
            sp.wait_ge(s.kv_stored, 16 * (5 + NB))
            sp.wait_ge(s.stored, 16 * 5)

        @block.tensor
        def _(pe):
            def gemm_tile(slot, m, out, rh, rl, ks, start=True, stop=True, per_k=None):
                for n, (k, kk) in enumerate(ks):
                    if per_k is not None:
                        pe.wait_ge(s.norm_l, per_k + n + 1)
                    cols = slice(P * m, P * m + P)
                    for q, (w, r) in enumerate(((w_hi, rh), (w_hi, rl), (w_lo, rh))):
                        for half in range(2):
                            last = pe.matmul(out[:, half], w[:, slot, k, cols], r[:, kk, HT * half:HT * half + HT],
                                             start=start and n == 0 and q == 0, stop=stop and n == len(ks) - 1 and q == 2)
                return last

            all_k = [(k, k) for k in range(UK)]

            def acc_tile(c_half, c, slot, m, rh, rl, ks=all_k, per_k=None, wait=True):
                if wait:
                    pe.wait_ge(acc_read[c % 2], c_half)
                gemm_tile(slot, m, acc(c), rh, rl, ks, per_k=per_k).then_inc(acc_done[c % 2], 1)

            pe.wait_ge(s.ld_const, 16)
            pe.wait_ge(s.ld_par, 16 * 9)
            pe.transpose(ps[:, 6, 0:44], par[:, :], ident[0:44, 0:44])
            for k in range(KC):
                pe.transpose(ps[:, 6, 64 + CW * k:64 + CW * k + CW], dw_tok[:, P * k:P * k + P], ident[0:CW, 0:CW])
            pe.matmul(ps[:, 6, 192:200], ones[0:1, :], ab_tok[0:1, :], start=True, stop=True).then_inc(s.par_done, 1)
            def sum_squares(sq, k, bank=4, n=KD):
                for half in range(2):
                    last = pe.matmul(ps[:, bank + half, 0:HT], ones, sq[:, HT * half:HT * half + HT],
                                     start=(k == 0), stop=(k == n - 1))
                return last

            for k in range(KD + 1):
                if k < KD:
                    if k % 4 == 0:
                        pe.wait_ge((s.ld_x0, s.ld_x1)[k // 4], 32)
                    if k >= 2:
                        pe.wait_ge(s.x_copied, k - 1)
                    for j in range(S // P):
                        pe.transpose(ps[:, 2 * (k % 2), P * j:P * j + P], x_tok[:, j, P * k:P * k + P], ident)
                    pe.transpose(ps[:, 2 * (k % 2) + 1, 0:NS], xs_tok[:, P * k:P * k + P], ident[0:NS, 0:NS])\
                        .then_inc(s.xt_done, 1)
                if k >= 1:
                    pe.wait_ge(s.sq_ready, k)
                    sum_squares(sq0[:, (k - 1) % 2], k - 1).then_inc(s.ssq_done, 1)
            pe.wait_ge(s.ld_state, 16)
            pe.wait_ge(s.par_read, 1)
            for g in range(GROUPS):
                for k in range(KC):
                    last = pe.transpose(ps[:, 6 + g, GB * HIST * k:GB * HIST * (k + 1)], st_tok[:, g, P * k:P * k + P],
                                        ident[0:GB * HIST, 0:GB * HIST])
                last.then_inc(s.st_done, 1)

            def in_pair(i, peeled):
                for j in range(2):
                    pe.wait_ge(s.split_done, i * 2 + (j + 1))
                    for m in range(MT):
                        t = 2 * j + m
                        acc_tile(i * 2 + t // 2, t, j, m, hH, hL, per_k=0 if peeled and t == 0 else None,
                                 wait=not peeled or t >= 2)

            in_pair(0, True)
            with pe.Fori(1, U_MERGE // 2) as i:
                in_pair(i, False)

            n_in = U_MERGE
            pe.wait_ge(acc_read[0], n_in)
            pe.wait_ge(acc_read[1], n_in)
            pe.wait_ge(s.st_read, GROUPS)
            for k in range(KC):
                pe.transpose(ps[0:HIST, 0, P * k:P * k + P], uP[:, k, S:S + HIST], ident)
                last = pe.transpose(ps[0:NS, 1, P * k:P * k + P], u_new[:, k], ident)
            last.then_inc(s.cout_done, 1)
            for src, big, small, done, read in ((vT, 4, 6, s.vt_done, s.vt_read), (kT, 5, 7, s.ktok_done, s.ktok_read)):
                for k in range(KC):
                    if k:
                        pe.wait_ge(read, k)
                    for j in range(S // P):
                        last = pe.transpose(ps[:, big, P * j:P * j + P], src[:, k, P * j:P * j + P], ident)
                    last.then_inc(done, 1)
                for k in range(KC):
                    last = pe.transpose(ps[0:NS, small, P * k:P * k + P], src[:, k, S:T], ident)
                last.then_inc(done, 1)

            pe.wait_ge(s.cout_read, 2)
            pe.wait_ge(s.vt_read, KC + 1)
            pe.wait_ge(s.ktok_read, KC + 1)
            n_kt = n_z = n_ps = n_pt = n_pw = 0

            def next_kt():
                nonlocal n_kt
                if n_kt >= 2:
                    pe.wait_ge(kt_read[n_kt % 2], n_kt // 2)
                n_kt += 1
                return 2 + (n_kt - 1) % 2

            for st in STEPS:
                what, a = st[0], st[1:]
                if what == "KT":
                    g, j = a
                    r = 2 * PAGES * g + j
                    pe.wait_ge(pages_loaded[r % 2], 16 * GB * (r // 2 + 1))
                    for b in range(GB):
                        bank = next_kt()
                        for k in range(KC):
                            last = pe.transpose(ps[:, bank, P * k:P * k + P], pages[:, r % 2, b, P * k:P * k + P], ident)
                        last.then_inc(s.kt_done, 1)
                elif what == "SC":
                    g, j = a
                    ks = PAGES * g + j
                    upto = 4 * (ks + 1) + 3 * g
                    pe.wait_ge(kt_read[0], (upto + 1) // 2)
                    pe.wait_ge(kt_read[1], upto // 2)
                    if j % 4 == 0 and n_z:
                        pe.wait_ge(s.z_read, n_z)
                    for k in range(KC):
                        for b in range(GB):
                            last = pe.matmul(ps[32 * b:32 * b + 32, 4, P * (j % 4):P * (j % 4) + P],
                                             q_s[:, GB * g + b, k], keysT[:, ks % 2, b, k], start=(k == 0),
                                             stop=(k == KC - 1), skip_group_check=True)
                    last.then_inc(s.score_done, 1)
                    if j % 4 == 3:
                        n_z += 1
                elif what == "ZN":
                    g, = a
                    pe.wait_ge(s.z_read, n_z)
                    for k in range(KC):
                        for b in range(GB):
                            last = pe.matmul(ps[32 * b:32 * b + 32, 4, 0:NS], q_s[:, GB * g + b, k], kT[:, k, S:T],
                                             start=(k == 0), stop=(k == KC - 1), skip_group_check=True)
                    last.then_inc(s.score_done, 1)
                    n_z += 1
                elif what == "AT":
                    g, = a
                    pe.wait_ge(s.weight_s, g + 1)
                    for blocks in (range(0, 4), range(4, 8), range(8, 9)):
                        bank = next_kt()
                        for n, j in enumerate(blocks):
                            w = P if j < PAGES else NS
                            last = pe.transpose(ps[0:w, bank, P * n:P * n + P], beta_s[:, P * j:P * j + w], ident)
                        last.then_inc(s.kt_done, 1)
                    pe.wait_ge(kt_read[0], (n_kt + 1) // 2)
                    pe.wait_ge(kt_read[1], n_kt // 2)
                    pe.wait_ge(s.z_read, n_z)
                elif what in ("PV", "PN"):
                    g = a[0]
                    j = a[1] if what == "PV" else PAGES
                    r = 2 * PAGES * g + PAGES + j
                    if what == "PV":
                        pe.wait_ge(pages_loaded[r % 2], 16 * GB * (r // 2 + 1))
                    for b in range(GB):
                        v = pages[:, r % 2, b, :] if what == "PV" else vs_tok[:, :]
                        last = pe.matmul(ps[32 * b:32 * b + 32, 4, :], wgtT_s[:, j, 32 * b:32 * b + 32], v,
                                         start=(j == 0), stop=(j == PAGES), skip_group_check=True)
                    last.then_inc(s.page_used if what == "PV" else s.own_done, 1)
                elif what == "SO":
                    g, = a
                    pe.wait_ge(s.own_ready, g + 1)
                    for k in range(KC):
                        last = pe.matmul(ps[:, 4, GB * NT * k:GB * NT * (k + 1)], own_s[:, P * k:P * k + P], selq,
                                         start=True, stop=True, skip_group_check=True)
                    last.then_inc(s.attT_done, 1)
                    n_z += 1
                elif what == "PS":
                    h, = a
                    q = (q_even, q_odd)[h % 2]
                    for i in range(S // P):
                        if n_ps >= 2:
                            pe.wait_ge(s.pscore_read, n_ps - 1)
                        pe.matmul(ps[:, n_ps % 2, 0:WID[i]], q[:, h // 2, P * i:P * i + P], kT[:, h // 2, 0:WID[i]],
                                  start=True, stop=True).then_inc(s.pscore_done, 1)
                        n_ps += 1
                elif what == "PT":
                    h, = a
                    pe.wait_ge(s.pweight, 4 * (h + 1))
                    for j in range(S // P):
                        if n_pt >= 2:
                            pe.wait_ge(s.ptr_read, n_pt - 1)
                        for i in range(j, S // P):
                            last = pe.transpose(ps[:, 6 + n_pt % 2, P * (i - j):P * (i - j) + P],
                                                beta_p[:, POS[i] + P * j:POS[i] + P * j + P], ident)
                        last.then_inc(s.ptr_done, 1)
                        n_pt += 1
                elif what == "PO":
                    h, = a
                    pe.wait_ge(s.ptr_read, 4 * (h + 1))
                    if h % 2 == 0 and h:
                        pe.wait_ge(s.pv_read, h // 2)
                    at_ = 0
                    for j in range(S // P):
                        w = S - P * j
                        last = pe.matmul(ps[64 * (h % 2):64 * (h % 2) + 64, 5, P * j:S], v_tok[:, j, DH * h:DH * h + DH],
                                         wgtT_p[:, at_:at_ + w], start=(j == 0), stop=(j == S // P - 1),
                                         skip_group_check=True)
                        at_ += w
                    last.then_inc(s.pv_done, 1)

            pe.wait_ge(s.conv_done, 2)
            pe.wait_ge(s.dconv_done, 2)
            pe.wait_ge(s.sconv_done, KC)
            pe.wait_ge(s.z_read, n_z)
            pe.wait_ge(s.pv_read, H // 2)
            for k in range(KC):
                last = sum_squares(yc[:, k], k, n=KC)
            last.then_inc(s.ln_sum, 1)
            for k in range(KC):
                pe.wait_ge(s.ln_sq, k + 1)
                last = sum_squares(sq1[:, k % 2], k, bank=6, n=KC)
                last.then_inc(s.ln_sqsum, 1)

            def merge_units(i):
                for q in range(2):
                    for j in range(3):
                        u = 3 * q + j
                        slot = u % 2
                        pe.wait_ge(s.split_done, i * 6 + (U_MERGE + u + 1))
                        if j < 2:
                            tiles = [(2 * j + m, m, hH, hL, all_k) for m in range(MT)]
                        else:
                            tiles = [(4 + m, m, acH, acL, [(k, KC + k) for k in range(KC)]) for m in range(MT)]
                            tiles += [(6 + m, m, acH, acL, [(KC + k, k) for k in range(KC)]) for m in range(MT)]
                        for t, m, rh, rl, ks in tiles:
                            acc_tile(i * 8 + (A_MERGE // 2 + 4 * q + t // 2), t, slot, m, rh, rl, ks)

            pe.wait_ge(s.ln_lo, KC)
            with pe.Fori(0, 2) as i:
                merge_units(i)
            pe.wait_ge(s.merged_lo, KD)
            with pe.Fori(0, 2) as i:
                for j in range(2):
                    pe.wait_ge(s.split_done, i * 2 + (U_WO + j + 1))
                    for m in range(MT):
                        t = 2 * j + m
                        acc_tile(i * 2 + (A_WO // 2 + t // 2), t, j, m, mH, mL)

            def total(need):
                pe.wait_ge(s.wo_sum, need)
                for half in range(2):
                    last = pe.matmul(ps[:, 4 + half, 0:HT], ones, ssum[:, HT * half:HT * half + HT], start=True, stop=True)
                last.then_inc(s.ssq_done, 1)

            total(KD)
            for k in range(KD):
                pe.wait_ge(s.sq_ready2, k + 1)
                last = sum_squares(sq2[:, k % 2], k, bank=6)
                last.then_inc(s.ssq_done, 1)
            pe.wait_ge(s.norm_l, 2 * KD)
            with pe.Fori(0, FF // UC) as i:
                for j in range(2):
                    pe.wait_ge(s.split_done, i * 2 + (U_FFI + j + 1))
                    for m in range(MT):
                        t = 2 * j + m
                        acc_tile(i * 2 + (A_FFI // 2 + t // 2), t, j, m, hH, hL)
            pe.wait_ge(s.act_lo, KF)
            pe.wait_ge(acc_read[0], (A_FFI + 4 * (FF // UC)) // 2)
            pe.wait_ge(acc_read[1], (A_FFI + 4 * (FF // UC)) // 2)
            for mp in range(D // UC):
                for j in range(3):
                    n = U_FFO + 3 * mp + j
                    pe.wait_ge(s.split_done, n + 1)
                    ks = [(k, 8 * j + k) for k in range(min(8, KF - 8 * j))]
                    for m in range(MT):
                        if j == 0 and mp >= 2:
                            pe.wait_ge(s.out_acc_read, 2 * (mp - 2) + m + 1)
                        bank = 4 * (mp % 2) + 2 * m
                        last = gemm_tile(n % 2, m, ps[:, bank:bank + 2, 0:HT], actH, actL, ks, start=(j == 0), stop=(j == 2))
                        if j == 2:
                            last.then_inc(s.out_acc_done, 1)
                        elif m == MT - 1:
                            last.then_inc(s.unit_used, 1)
            pe.wait_ge(s.wo_sum, 2 * KD)
            pe.wait_ge(s.out_acc_read, KD)
            total(2 * KD)
            for k in range(KD):
                pe.wait_ge(s.y_ready, k + 1)
                if k >= 2:
                    pe.wait_ge(s.yt_read, k - 1)
                for j in range(S // P):
                    pe.transpose(ps[:, 2 * (k % 2), P * j:P * j + P], pout[:, k, P * j:P * j + P], ident)
                pe.transpose(ps[0:NS, 2 * (k % 2) + 1, 0:P], pout[:, k, S:T], ident).then_inc(s.yt_done, 1)

        @block.scalar
        def _(act):
            def used(n):
                if n < U_MERGE:
                    act.wait_ge(acc_done[1], n + 1)
                elif n < U_WO:
                    u = n - U_MERGE
                    act.wait_ge(acc_done[1], (A_MERGE + 8 * (u // 3) + (2, 4, 8)[u % 3]) // 2)
                elif n < U_FFO:
                    act.wait_ge(acc_done[1], A_WO // 2 + n - U_WO + 1)
                elif (n - U_FFO) % 3 < 2:
                    act.wait_ge(s.unit_used, 2 * ((n - U_FFO) // 3) + (n - U_FFO) % 3 + 1)
                else:
                    act.wait_ge(s.out_acc_done, 2 * ((n - U_FFO) // 3) + 2)

            def split_hi(n):
                act.wait_ge(raw_loaded[n % 2], 32 * (n // 2 + 1))
                if n >= 2:
                    used(n - 2)
                act.copy(w_hi[:, n % 2], w_raw[:, n % 2]).then_inc(s.hi_done, 1)

            for k in range(KD):
                act.wait_ge(s.x_copied, k + 1)
                if k >= 2:
                    act.wait_ge(s.ssq_done, k - 1)
                act.activation(sq0[:, k % 2], xT[:, k], ACT.Square).then_inc(s.sq_ready, 1)
            split_hi(0)

            def std(out, bank, width, need, sem=s.ssq_done):
                act.wait_ge(sem, need)
                act.activation(halves(out[:]), ps[:, bank:bank + 2, 0:HT], ACT.Sqrt, bias=eps, scale=1.0 / width)\
                    .then_inc(s.std_ready, 1)

            def norm_hi(tmp, g, first):
                for k in range(KD):
                    act.wait_ge(s.norm_t, first + k + 1)
                    act.activation(hH[:, k], tmp[:, k % 2], ACT.Identity, scale=gain(g, k)).then_inc(s.norm_h, 1)

            std(std0, 4, D, KD)
            norm_hi(tmp0, 0, 0)
            act.wait_ge(s.zeroed, 5)
            for n in range(U_MERGE):
                if n + 1 < U_MERGE:
                    split_hi(n + 1)
                for m in range(MT):
                    a = acc(m)
                    if n in (0, 2):
                        act.wait_ge(acc_done[m], n + 1)
                        if n:
                            act.wait_ge(acc_read[m], n)
                        act.activation(halves(sig_u[:, m]), a, ACT.Sigmoid).then_inc(acc_read[m], 1)
                    elif n in (4, 5):
                        p = 2 * (n - 4) + m
                        act.wait_ge(acc_done[m], n + 1)
                        for r, (q, lo) in enumerate(((q_even, 0), (q_odd, 64))):
                            act.copy(q[lo:lo + 64, p, 0:HT], a[lo:lo + 64, 0, :])
                            act.copy(q[lo:lo + 64, p, HT:S], a[lo:lo + 64, 1, 0:S1])
                            last = act.copy(q_s[lo:lo + 64, :, p, 2 * p + r, :],
                                            a[lo:lo + 64, 1, S1:HT].rearrange("p (b t) -> p b t", t=NT))
                        last.then_inc(acc_read[m], 1)
                    elif n in (6, 7):
                        act.wait_ge(acc_done[m], n + 1)
                        act.copy(halves(kT[:, 2 * (n - 6) + m]), a).then_inc(acc_read[m], 1)
            act.wait_ge(s.sconv_done, KC)
            for k in range(KC):
                act.wait_ge(s.ktok_done, k + 1)
                act.copy(k_tok[:, :, P * k:P * k + P], ps[:, 5, :].rearrange("p (j c) -> p j c", c=P)).then_inc(s.ktok_read, 1)
            act.wait_ge(s.ktok_done, KC + 1)
            act.copy(ks_tok[:, :], ps[0:NS, 7, :]).then_inc(s.ktok_read, 1)

            act.wait_ge(s.bias_ready, 1)
            n_kt = 0
            for st in STEPS:
                what, a = st[0], st[1:]
                if what == "KT":
                    g, j = a
                    ks = PAGES * g + j
                    for b in range(GB):
                        if n_kt % 2 == 0:
                            if ks >= 2 and b < 2:
                                act.wait_ge(s.score_done, ks - 1 + (ks - 2) // PAGES)
                            act.wait_ge(s.kt_done, n_kt + 1)
                            act.copy(keysT[:, ks % 2, b], ps[:, 2, :].rearrange("p (k c) -> p k c", c=P)).then_inc(kt_read[0], 1)
                        n_kt += 1
                elif what == "SC" and a[1] % 4 == 3:
                    g, j = a
                    act.wait_ge(s.score_done, PAGES * g + j + 1 + g)
                    act.activation(beta_s[:, P * (j - 3):P * (j + 1)], ps[:, 4, :], ACT.Sigmoid, bias=bias_r[:, :], scale=SCALE)\
                        .then_inc(s.z_read, 1)
                elif what == "ZN":
                    g, = a
                    act.wait_ge(s.score_done, (PAGES + 1) * (g + 1))
                    act.activation(beta_s[:, PAST:LS], ps[:, 4, 0:NS], ACT.Sigmoid, bias=bias_r[:, :], scale=SCALE)\
                        .then_inc(s.z_read, 1)
                elif what == "AT":
                    for part_ in range(3):
                        if n_kt % 2 == 0:
                            act.wait_ge(s.kt_done, n_kt + 1)
                            if part_ < 2:
                                act.copy(wgtT_s[:, 4 * part_:4 * part_ + 4], ps[:, 2, :].rearrange("p (k c) -> p k c", c=P))\
                                    .then_inc(kt_read[0], 1)
                            else:
                                act.copy(wgtT_s[0:NS, PAGES], ps[0:NS, 2, 0:P]).then_inc(kt_read[0], 1)
                        n_kt += 1
                elif what == "SO":
                    g, = a
                    act.wait_ge(s.attT_done, g + 1)
                    act.copy(acH[:, 0:KC, S + GB * NT * g:S + GB * NT * (g + 1)],
                             ps[:, 4, 0:KC * GB * NT].rearrange("p (k c) -> p k c", k=KC)).then_inc(s.attT_hi, 1)
                elif what == "PS":
                    h, = a
                    if h == 0:
                        act.wait_ge(s.kv_stored, 16 * (5 + NB))
                    for i in range(S // P):
                        n = 4 * h + i
                        act.wait_ge(s.pscore_done, n + 1)
                        act.activation(beta_p[:, POS[i]:POS[i] + WID[i]], ps[:, n % 2, 0:WID[i]], ACT.Sigmoid,
                                       bias=bias_h[:, h:h + 1], scale=SCALE).then_inc(s.pscore_read, 1)
                elif what == "PT":
                    h, = a
                    at_ = 0
                    for j in range(S // P):
                        n, w = 4 * h + j, S - P * j
                        act.wait_ge(s.ptr_done, n + 1)
                        act.copy(wgtT_p[:, at_:at_ + w], ps[:, 6 + n % 2, 0:w]).then_inc(s.ptr_read, 1)
                        at_ += w
                elif what == "PO" and a[0] % 2:
                    h, = a
                    act.wait_ge(s.pv_done, h + 1)
                    act.copy(acH[:, h // 2, 0:S], ps[:, 5, :]).then_inc(s.pv_hi, 1)

            split_hi(U_MERGE)
            for k in range(KC):
                act.wait_ge(s.ln_cent, k + 1)
                if k >= 2:
                    act.wait_ge(s.ln_sqsum, k - 1)
                act.activation(sq1[:, k % 2], yc[:, k], ACT.Square).then_inc(s.ln_sq, 1)
            std(std1, 6, C, KC, s.ln_sqsum)
            for k in range(KC + 1):
                if k < KC:
                    act.wait_ge(s.ln_t, k + 1)
                    if k >= 2:
                        act.wait_ge(s.ln_y, k - 1)
                    act.activation(sig1[:, k % 2], tmp1[:, k % 2], ACT.Sigmoid, bias=cvec(2, k)).then_inc(s.ln_sig, 1)
                if k >= 1:
                    act.wait_ge(s.ln_y, k)
                    act.copy(acH[:, KC + k - 1], tmp1[:, (k - 1) % 2]).then_inc(s.ln_hi, 1)
            for mp in range(D // UC):
                for j in range(3):
                    split_hi(U_MERGE + 3 * mp + j + 1)
                    for m in range(MT):
                        if j < 2:
                            c = A_MERGE + 8 * mp + 2 * j + m
                            act.wait_ge(acc_done[m], c // 2 + 1)
                            act.activation(halves((sig_c, sig_a)[j][:, m]), acc(c), ACT.Sigmoid).then_inc(acc_read[m], 1)
                        else:
                            act.wait_ge(s.merged_t, 2 * mp + m + 1)
                            act.copy(mH[:, 2 * mp + m], both[:, m]).then_inc(s.merged_hi, 1)

            def copy_and_square(t, a, read, sums):
                act.copy(halves(pout[:, t]), a)
                if sums is not None:
                    act.wait_ge(s.wo_sum, sums)
                act.activation(halves(sq2[:, t % 2]), a, ACT.Square).then_inc(read, 1)

            for j in range(D // UC):
                split_hi(U_WO + j + 1)
                for m in range(MT):
                    t = 2 * j + m
                    act.wait_ge(acc_done[m], (A_WO + t) // 2 + 1)
                    copy_and_square(t, acc(m), acc_read[m], t - 1 if t >= 2 else None)
            std(std2, 4, D, KD + 1)
            for k in range(KD):
                act.wait_ge(s.x1_ready, k + 1)
                if k >= 2:
                    act.wait_ge(s.ssq_done, KD + 1 + k - 1)
                act.activation(sq2[:, k % 2], xT[:, k], ACT.Square).then_inc(s.sq_ready2, 1)
            std(std2, 6, D, 2 * KD + 1)
            norm_hi(tmp2, 2, KD)
            with act.Fori(0, FF // UC) as i:
                for j in range(2):
                    n1 = U_FFI + j + 1
                    act.wait_ge(raw_loaded[n1 % 2], i * 32 + 32 * (n1 // 2 + 1))
                    act.wait_ge(acc_done[1], i * 2 + (A_WO // 2 + n1 - 2 - U_WO + 1))
                    act.copy(w_hi[:, n1 % 2], w_raw[:, n1 % 2]).then_inc(s.hi_done, 1)
                    for m in range(MT):
                        if j == 0:
                            act.wait_ge(acc_done[m], i * 2 + (A_FFI // 2 + 1))
                            act.activation(halves(sig_f[:, m]), acc(m), ACT.Sigmoid).then_inc(s.silu_ready, 1)
                        else:
                            act.wait_ge(acc_read[m], i * 2 + (A_FFI // 2 + 2))
                            act.copy(actH[:, bass.ds(i * 2 + m, 1), :], up_f[:, m:m + 1]).then_inc(s.act_hi, 1)
            for mp in range(D // UC):
                for j in range(3):
                    n = U_FFO + 3 * mp + j
                    if n + 1 < U_FFO + 12:
                        split_hi(n + 1)
                for m in range(MT):
                    t = 2 * mp + m
                    act.wait_ge(s.out_acc_done, t + 1)
                    bank = 4 * (mp % 2) + 2 * m
                    copy_and_square(t, ps[:, bank:bank + 2, 0:HT], s.out_acc_read, KD + t - 1 if t >= 2 else None)
            std(std2, 4, D, 2 * KD + 2)
            for k in range(KD):
                act.wait_ge(s.yt_done, k + 1)
                act.copy(y_tok[:, 0:4, P * k:P * k + P], ps[:, 2 * (k % 2), :].rearrange("p (j c) -> p j c", c=P))
                act.copy(y_tok[0:NS, 4, P * k:P * k + P], ps[0:NS, 2 * (k % 2) + 1, 0:P]).then_inc(s.yt_read, 1)

        @block.vector
        def _(dve):
            step = Count()

            def split_lo(n):
                dve.wait_ge(s.hi_done, n + 1)
                dve.tensor_tensor(w_lo[:, n % 2], w_raw[:, n % 2], w_hi[:, n % 2], ALU.subtract).then_inc(s.split_done, 1)

            dve.wait_ge(s.par_done, 1)
            dve.tensor_copy(vec[:, :], ps[:, 6, 0:44])
            dve.tensor_copy(dw[:], ps[:, 6, 64:64 + KC * CW].rearrange("p (k w) -> p k w", w=CW))
            dve.tensor_copy(bias_h[:, :], ps[:, 6, 192:200]).then_inc(s.dve_step, step.up())
            dve.wait_ge(s.dve_step, step.n)
            dve.tensor_tensor(tmp0[:, 0, 0:H], bias_h[:, :],
                                        headmask.rearrange("p (h d) -> p h d", d=DH)[:, :, 0], ALU.mult).then_inc(s.dve_step, step.up())
            dve.wait_ge(s.dve_step, step.n)
            dve.tensor_reduce(bias_r[:, :], tmp0[:, 0, 0:H], AX.X, ALU.add).then_inc(s.bias_ready, 1)
            dve.wait_ge(s.bias_ready, 1)
            dve.tensor_copy(tmp0[:, 0, 0:1], bias_r[:, :]).then_inc(s.par_read, 1)
            for k in range(KD):
                dve.wait_ge(s.xt_done, k + 1)
                dve.tensor_copy(xT[:, k, 0:S], ps[:, 2 * (k % 2), :])
                dve.tensor_copy(xT[:, k, S:T], ps[:, 2 * (k % 2) + 1, 0:NS]).then_inc(s.x_copied, 1)
            split_lo(0)

            def reciprocal(a, need):
                dve.wait_ge(s.std_ready, need)
                dve.reciprocal(a[:, :], a[:, :]).then_inc(s.dve_step, step.up())
                dve.wait_ge(s.dve_step, step.n)

            def norm(tmp, rstd, g, first):
                for k in range(KD + 1):
                    if k < KD:
                        if k >= 2:
                            dve.wait_ge(s.norm_l, first + k - 1)
                        dve.tensor_tensor(tmp[:, k % 2], xT[:, k], rstd[:, :], ALU.mult).then_inc(s.norm_t, 1)
                    if k >= 1:
                        dve.wait_ge(s.norm_h, first + k)
                        dve.scalar_tensor_tensor(out=hL[:, k - 1], in0=tmp[:, (k - 1) % 2], scalar=gain(g, k - 1),
                                                 in1=hH[:, k - 1], op0=ALU.mult, op1=ALU.subtract).then_inc(s.norm_l, 1)

            reciprocal(std0, 1)
            norm(tmp0, std0, 0, 0)
            dve.wait_ge(s.st_done, GROUPS)
            for g in range(GROUPS):
                for k in range(KC):
                    last = dve.tensor_copy(uS[:, k, GB * g:GB * g + GB, 0:HIST],
                                           ps[:, 6 + g, GB * HIST * k:GB * HIST * (k + 1)].rearrange("p (b r) -> p b r", r=HIST))
                last.then_inc(s.st_read, 1)

            def sample_conv(ct):
                if ct:
                    dve.wait_ge(s.sconv_done, ct)
                for t in range(NT):
                    last = dve.tensor_tensor(prod[:, t], uS[:, ct, :, t:t + CW],
                                             dw[:, ct].unsqueeze(1).to_broadcast([P, NB, CW]), ALU.mult)
                last.then_inc(s.dve_step, step.up())
                dve.wait_ge(s.dve_step, step.n)
                y = yc[:, ct, S:T].rearrange("p (b t) -> p t b", t=NT)
                dve.tensor_reduce(y, prod[:], AX.X, ALU.add).then_inc(s.dve_step, step.up())
                dve.wait_ge(s.dve_step, step.n)
                dve.tensor_scalar(yc[:, ct, S:T], yc[:, ct, S:T], cvec(0, ct), None, ALU.add).then_inc(s.sconv_done, 1)

            conv_at = 0

            def prompt_conv(upto):
                nonlocal conv_at
                while conv_at < min(upto, 2 * CW):
                    w, ct = conv_at // 2, conv_at % 2
                    y, u = yc[:, ct, 0:S], uP[:, ct, w:w + S]
                    if w == 0:
                        dve.tensor_scalar(y, u, dw[:, ct, 0:1], cvec(0, ct), ALU.mult, ALU.add).then_inc(s.dve_step, step.up())
                    else:
                        dve.wait_ge(s.dve_step, step.n - 1 if conv_at < 2 * CW - 1 else step.n)
                        ins = dve.scalar_tensor_tensor(out=y, in0=u, scalar=dw[:, ct, w:w + 1], in1=y, op0=ALU.mult, op1=ALU.add)
                        if w < CW - 1:
                            ins.then_inc(s.dve_step, step.up())
                        else:
                            ins.then_inc(s.dconv_done, 1)
                    conv_at += 1

            for n in range(U_MERGE):
                if n + 1 < U_MERGE:
                    split_lo(n + 1)
                for m in range(MT):
                    a = acc(m)
                    if n in (1, 3):
                        ct = 2 * (n // 2) + m
                        if n == 1 and m == 0:
                            dve.wait_ge(s.zeroed, 5)
                            dve.wait_ge(s.st_read, GROUPS)
                        dve.wait_ge(acc_read[m], n)
                        dve.wait_ge(acc_done[m], n + 1)
                        dve.tensor_tensor(uP[:, ct, HIST:HIST + HT], a[:, 0, :], sig_u[:, m, 0:HT], ALU.mult)
                        dve.tensor_tensor(uP[:, ct, HIST + HT:HIST + S], a[:, 1, 0:S1], sig_u[:, m, HT:S], ALU.mult)
                        dve.tensor_tensor(uS[:, ct, :, HIST:HIST + NT], a[:, 1, S1:HT].rearrange("p (b t) -> p b t", t=NT),
                                          sig_u[:, m, S:T].rearrange("p (b t) -> p b t", t=NT), ALU.mult)
                        dve.tensor_tensor(u_new[:, ct], a[:, 1, S1:HT], sig_u[:, m, S:T], ALU.mult).then_inc(acc_read[m], 1)
                    elif n in (8, 9):
                        dve.wait_ge(acc_done[m], n + 1)
                        dve.tensor_copy(halves(vT[:, 2 * (n - 8) + m]), a).then_inc(acc_read[m], 1)
                if n >= 2:
                    if n == 2:
                        for m in range(MT):
                            dve.wait_ge(acc_read[m], 2)
                    if n == 4:
                        for m in range(MT):
                            dve.wait_ge(acc_read[m], 4)
                    if 4 <= n < 8:
                        sample_conv(n - 4)
                    prompt_conv(2 * CW if n == U_MERGE - 1 else 8 * (n - 1))
            dve.wait_ge(s.zeroed, 5)
            for k in range(KC):
                dve.wait_ge(s.vt_done, k + 1)
                dve.tensor_copy(v_tok[:, :, P * k:P * k + P], ps[:, 4, :].rearrange("p (j c) -> p j c", c=P)).then_inc(s.vt_read, 1)
            dve.wait_ge(s.vt_done, KC + 1)
            dve.tensor_copy(vs_tok[0:NS, :], ps[0:NS, 6, :]).then_inc(s.vt_read, 1)
            dve.wait_ge(s.cout_done, 1)
            dve.tensor_copy(conv_tail[:, :], ps[0:HIST, 0, :]).then_inc(s.cout_read, 1)
            dve.tensor_copy(conv_new[:, :], ps[0:NS, 1, :]).then_inc(s.cout_read, 1)

            def stick(beta, left, width, out_sem):
                dve.tensor_scalar(left[:, 0:width], beta, -1.0, 1.0, ALU.mult, ALU.add).then_inc(s.dve_step, step.up())
                dve.wait_ge(s.dve_step, step.n)
                back = left[:, 0:width][:, ::-1]
                dve.tensor_tensor_scan(back, back, back, 1.0, ALU.mult, ALU.min).then_inc(s.dve_step, step.up())
                dve.wait_ge(s.dve_step, step.n)
                dve.tensor_tensor(beta, beta, left[:, 1:width + 1], ALU.mult).then_inc(out_sem, 1)

            n_kt = 0
            for st in STEPS:
                what, a = st[0], st[1:]
                if what == "KT":
                    g, j = a
                    ks = PAGES * g + j
                    for b in range(GB):
                        if n_kt % 2:
                            if ks >= 2 and b < 2:
                                dve.wait_ge(s.score_done, ks - 1 + (ks - 2) // PAGES)
                            dve.wait_ge(s.kt_done, n_kt + 1)
                            dve.tensor_copy(keysT[:, ks % 2, b], ps[:, 3, :].rearrange("p (k c) -> p k c", c=P)).then_inc(kt_read[1], 1)
                        n_kt += 1
                elif what == "ZN":
                    g, = a
                    dve.wait_ge(s.z_read, 4 * g + 3)
                    if g == 0:
                        dve.memset(stick_s[:, LS:LS + 1], 1.0)
                        dve.memset(wgtT_s[:, PAGES], 0.0)
                    dve.tensor_tensor(beta_s[:, PAST:LS], beta_s[:, PAST:LS], newmask(g), ALU.mult).then_inc(s.dve_step, step.up())
                    dve.wait_ge(s.dve_step, step.n)
                    stick(beta_s[:, :], stick_s, LS, s.weight_s)
                elif what == "AT":
                    for part_ in range(3):
                        if n_kt % 2:
                            dve.wait_ge(s.kt_done, n_kt + 1)
                            if part_ < 2:
                                dve.tensor_copy(wgtT_s[:, 4 * part_:4 * part_ + 4], ps[:, 3, :].rearrange("p (k c) -> p k c", c=P))\
                                    .then_inc(kt_read[1], 1)
                            else:
                                dve.tensor_copy(wgtT_s[0:NS, PAGES], ps[0:NS, 3, 0:P]).then_inc(kt_read[1], 1)
                        n_kt += 1
                elif what == "PN":
                    g, = a
                    dve.wait_ge(s.own_done, g + 1)
                    dve.tensor_tensor(own_s[:, :], ps[:, 4, :], headmask, ALU.mult).then_inc(s.own_ready, 1)
                elif what == "SO":
                    g, = a
                    cols = slice(S + GB * NT * g, S + GB * NT * (g + 1))
                    dve.wait_ge(s.attT_hi, g + 1)
                    dve.tensor_tensor(acL[:, 0:KC, cols], ps[:, 4, 0:KC * GB * NT].rearrange("p (k c) -> p k c", k=KC),
                                      acH[:, 0:KC, cols], ALU.subtract).then_inc(s.z_read, 1)
                elif what == "PS":
                    h, = a
                    for i in range(S // P):
                        dve.wait_ge(s.pscore_read, 4 * h + i + 1)
                        if h == 0 and i == 0:
                            dve.memset(stick_p[:, :, S:S + 1], 1.0).then_inc(s.dve_step, step.up())
                        diag = beta_p[:, POS[i] + P * i:POS[i] + P * i + P]
                        dve.tensor_tensor(diag, diag, tri, ALU.mult).then_inc(s.dve_step, step.up())
                        dve.wait_ge(s.dve_step, step.n)
                        if 4 * h + i >= 2:
                            dve.wait_ge(s.pweight, 4 * h + i - 1)
                        stick(beta_p[:, POS[i]:POS[i] + WID[i]], stick_p[:, i % 2, S - WID[i]:S + 1], WID[i], s.pweight)
                elif what == "PO" and a[0] % 2:
                    h, = a
                    dve.wait_ge(s.pv_hi, h // 2 + 1)
                    dve.tensor_tensor(acL[:, h // 2, 0:S], ps[:, 5, :], acH[:, h // 2, 0:S], ALU.subtract).then_inc(s.pv_read, 1)

            split_lo(U_MERGE)
            dve.wait_ge(s.ln_sum, 1)
            for k in range(KC):
                dve.scalar_tensor_tensor(out=halves(yc[:, k]), in0=ps[:, 4:6, 0:HT], scalar=-1.0 / C, in1=halves(yc[:, k]),
                                         op0=ALU.mult, op1=ALU.add).then_inc(s.ln_cent, 1)
            reciprocal(std1, 2)
            for k in range(KC + 1):
                if k < KC:
                    if k >= 2:
                        dve.wait_ge(s.ln_lo, k - 1)
                    dve.scalar_tensor_tensor(out=tmp1[:, k % 2], in0=yc[:, k], scalar=cvec(1, k), in1=std1[:, :],
                                             op0=ALU.mult, op1=ALU.mult).then_inc(s.ln_t, 1)
                if k >= 1:
                    t = tmp1[:, (k - 1) % 2]
                    dve.wait_ge(s.ln_sig, k)
                    dve.scalar_tensor_tensor(out=t, in0=t, scalar=cvec(2, k - 1), in1=sig1[:, (k - 1) % 2],
                                             op0=ALU.add, op1=ALU.mult).then_inc(s.ln_y, 1)
                    dve.wait_ge(s.ln_hi, k)
                    dve.tensor_tensor(acL[:, KC + k - 1], t, acH[:, KC + k - 1], ALU.subtract).then_inc(s.ln_lo, 1)
            for mp in range(D // UC):
                for j in range(3):
                    split_lo(U_MERGE + 3 * mp + j + 1)
                c0 = A_MERGE + 8 * mp + 4
                if mp:
                    dve.wait_ge(s.merged_lo, 2 * mp)
                for m in range(MT):
                    dve.wait_ge(acc_done[m], c0 // 2 + 1)
                    dve.tensor_tensor(halves(part[:, m]), acc(m), halves(sig_c[:, m]), ALU.mult).then_inc(acc_read[m], 1)
                for m in range(MT):
                    dve.wait_ge(acc_done[m], c0 // 2 + 2)
                    dve.tensor_tensor(halves(both[:, m]), acc(m), halves(sig_a[:, m]), ALU.mult).then_inc(acc_read[m], 1)
                for m in range(MT):
                    dve.wait_ge(acc_read[m], c0 // 2 + 2)
                    dve.tensor_tensor(both[:, m], both[:, m], part[:, m], ALU.add).then_inc(s.merged_t, 1)
                for m in range(MT):
                    dve.wait_ge(s.merged_hi, 2 * mp + m + 1)
                    dve.tensor_tensor(mL[:, 2 * mp + m], both[:, m], mH[:, 2 * mp + m], ALU.subtract).then_inc(s.merged_lo, 1)

            def add_squares(t, first):
                if t == 0:
                    dve.tensor_copy(ssum[:, :], sq2[:, 0]).then_inc(s.wo_sum, 1)
                else:
                    dve.wait_ge(s.wo_sum, first + t)
                    dve.tensor_tensor(ssum[:, :], ssum[:, :], sq2[:, t % 2], ALU.add).then_inc(s.wo_sum, 1)

            for j in range(D // UC):
                split_lo(U_WO + j + 1)
                for m in range(MT):
                    dve.wait_ge(acc_read[m], (A_WO + 2 * j + m) // 2 + 1)
                    add_squares(2 * j + m, 0)
            reciprocal(std2, 3)

            def residual(g):
                for k in range(KD + 1):
                    if k < KD:
                        dve.scalar_tensor_tensor(out=tmp2[:, k % 2], in0=pout[:, k], scalar=gain(g, k), in1=std2[:, :],
                                                           op0=ALU.mult, op1=ALU.mult).then_inc(s.dve_step, step.up())
                    if k >= 1:
                        dve.wait_ge(s.dve_step, step.n - (1 if k < KD else 0))
                        dve.tensor_tensor(xT[:, k - 1], xT[:, k - 1], tmp2[:, (k - 1) % 2], ALU.add).then_inc(s.x1_ready, 1)
                        if k < KD:
                            dve.wait_ge(s.x1_ready, k)

            residual(1)
            reciprocal(std2, 4)
            norm(tmp2, std2, 2, KD)
            with dve.Fori(0, FF // UC) as i:
                for j in range(2):
                    n1 = U_FFI + j + 1
                    dve.wait_ge(s.hi_done, i * 2 + (n1 + 1))
                    dve.tensor_tensor(w_lo[:, n1 % 2], w_raw[:, n1 % 2], w_hi[:, n1 % 2], ALU.subtract).then_inc(s.split_done, 1)
                    for m in range(MT):
                        if j == 0:
                            dve.wait_ge(s.silu_ready, i * 2 + (m + 1))
                            dve.tensor_tensor(halves(sig_f[:, m]), acc(m), halves(sig_f[:, m]), ALU.mult).then_inc(acc_read[m], 1)
                        else:
                            dve.wait_ge(acc_done[m], i * 2 + (A_FFI // 2 + 2))
                            dve.tensor_tensor(halves(up_f[:, m]), acc(m), halves(sig_f[:, m]), ALU.mult).then_inc(acc_read[m], 1)
                for m in range(MT):
                    dve.wait_ge(s.act_hi, i * 2 + (m + 1))
                    dve.tensor_tensor(actL[:, bass.ds(i * 2 + m, 1), :], up_f[:, m:m + 1], actH[:, bass.ds(i * 2 + m, 1), :],
                                      ALU.subtract).then_inc(s.act_lo, 1)
            for mp in range(D // UC):
                for j in range(3):
                    n = U_FFO + 3 * mp + j
                    if n + 1 < U_FFO + 12:
                        split_lo(n + 1)
                for m in range(MT):
                    t = 2 * mp + m
                    dve.wait_ge(s.out_acc_read, t + 1)
                    add_squares(t, KD)
            reciprocal(std2, 5)
            for k in range(KD + 1):
                if k < KD:
                    dve.scalar_tensor_tensor(out=pout[:, k], in0=pout[:, k], scalar=gain(3, k), in1=std2[:, :],
                                                       op0=ALU.mult, op1=ALU.mult).then_inc(s.dve_step, step.up())
                if k >= 1:
                    dve.wait_ge(s.dve_step, step.n - (1 if k < KD else 0))
                    dve.tensor_tensor(pout[:, k - 1], pout[:, k - 1], xT[:, k - 1], ALU.add).then_inc(s.y_ready, 1)

        @block.gpsimd
        def _(pool):
            for n, zero in enumerate((q_even[64:128], q_odd[0:64], q_s[:], vs_tok[:], uP[:, :, 0:HIST])):
                if n:
                    pool.wait_ge(s.zeroed, n)
                pool.memset(zero, 0.0).then_inc(s.zeroed, 1)
            tap = Count()
            for ct in range(2, KC):
                pool.wait_ge(acc_read[ct % 2], 2 * (ct // 2) + 2)
                y = yc[:, ct, 0:S]
                pool.tensor_scalar(y, uP[:, ct, 0:S], dw[:, ct, 0:1], cvec(0, ct), ALU.mult, ALU.add).then_inc(s.conv_tap, tap.up())
                for w in range(1, CW):
                    product = tap_prod[:, w % 2]
                    pool.tensor_scalar(product, uP[:, ct, w:w + S], dw[:, ct, w:w + 1], None, ALU.mult).then_inc(s.conv_tap, tap.up())
                    pool.wait_ge(s.conv_tap, tap.n)
                    if w < CW - 1:
                        pool.tensor_tensor(y, y, product, ALU.add).then_inc(s.conv_tap, tap.up())
                    else:
                        pool.tensor_tensor(y, y, product, ALU.add).then_inc(s.conv_done, 1)


_INS = ["x_prompt", "x_sample", "cache_k", "cache_v", "state_conv", "page_table", "norm_pre_mix", "norm_post_mix",
        "norm_pre_ffn", "norm_post_ffn", "w_in", "conv_dw", "conv_b", "conv_ln_g", "conv_ln_b", "w_conv_out",
        "att_bias", "w_att_out", "w_o", "w_ffn_in", "w_ffn_out"]
_OUTS = [(1, S, D), (NB, NT, D), (1, 1, S, H, DH), (1, 1, S, H, DH), (1, 1, HIST, C), (1, NB, NT, H, DH),
         (1, NB, NT, H, DH), (1, NB, HIST, C)]


def kernel(**inputs):
    import concourse.bacc as bacc
    from concourse.bass_utils import run_bass_kernel_spmd

    nc = bacc.Bacc("TRN2", target_bir_lowering=False, num_devices=1)
    arrays, args = {}, []
    for name in _INS + ["consts"]:
        a = constants() if name == "consts" else np.ascontiguousarray(inputs[name])
        arrays[f"in_{name}"] = a
        args.append(nc.dram_tensor(f"in_{name}", a.shape, mybir.dt.from_np(a.dtype), kind="ExternalInput").ap())
    for i, shape in enumerate(_OUTS):
        args.append(nc.dram_tensor(f"out_{i}", shape, F32, kind="ExternalOutput").ap())
    layer_kernel(nc, *args)
    r = run_bass_kernel_spmd(nc, [arrays], core_ids=[0])
    return tuple(r.results[0][f"out_{i}"] for i in range(len(_OUTS)))
```

```python
from contextlib import ExitStack

import numpy as np

import concourse.bass as bass
from concourse import mybir

F32 = mybir.dt.float32
F32R = mybir.dt.float32r
I32 = mybir.dt.int32
ALU = mybir.AluOpType
ACT = mybir.ActivationFunctionType
AX = mybir.AxisListType

P = 128
D = 1024
S = 512
NB, NT = 8, 4
NS = NB * NT
T = S + NS
HT = T // 2
S1 = S - HT
H, DH = 8, 64
C = 512
CW = 31
HIST = CW - 1
PAGES, PAGE = 8, 128
PAST = PAGES * PAGE
FF = 2816
KD, KC, KF = D // P, C // P, FF // P
EPS = 1e-6
SCALE = DH ** -0.5
UC = 256
UK = 8
MT = UC // P
RING = 2
GB = 4
GROUPS = NB // GB

COL_GLU_A, COL_GLU_B, COL_Q, COL_K, COL_V, COL_GC, COL_GA = 0, 512, 1024, 1536, 2048, 2560, 3584
FIRST_UNITS = [COL_GLU_B, COL_GLU_A, COL_GLU_B + UC, COL_GLU_A + UC, COL_Q, COL_Q + UC,
               COL_K, COL_K + UC, COL_V, COL_V + UC]
U_IN, U_MERGE, U_WO, U_FFI, U_FFO = 0, 10, 22, 26, 48
A_IN, A_MERGE, A_WO, A_FFI = 0, 20, 52, 60

K_ID, K_TRI, K_ONE, K_NEW, K_SEL, K_HEAD, K_EPS = 0, 128, 256, 384, 448, 464, 472
K_COLS = 473


def constants():
    c = np.zeros((P, K_COLS), np.float32)
    r = np.arange(P)
    b, h, q = r // 32, r // NT % H, r % NT
    c[:, K_ID:K_ID + P] = np.eye(P)
    c[:, K_TRI:K_TRI + P] = r[None, :] < r[:, None]
    c[:, K_ONE:K_ONE + P] = 1.0
    n = np.arange(NS)
    for g in range(GROUPS):
        c[:, K_NEW + NS * g:K_NEW + NS * (g + 1)] = (n[None] // NT == GB * g + b[:, None]) & (n[None] % NT < q[:, None])
    m = np.arange(GB * NT)
    c[:, K_SEL:K_SEL + GB * NT] = (m[None] // NT == b[:, None]) & (m[None] % NT == q[:, None])
    c[:, K_HEAD:K_HEAD + H] = np.arange(H)[None] == h[:, None]
    c[:, K_EPS] = EPS
    return c


def attention_steps():
    prompt = [("PS", 0, 0), ("PS", 0, 1)]
    for h in range(H):
        if h + 1 < H:
            prompt += [("PS", h + 1, 0), ("PS", h + 1, 1)]
        prompt += [("PT", h), ("PO", h)]
    prompt = iter(prompt)
    steps = []

    def pieces(n):
        for _ in range(n):
            steps.extend([next(prompt)])

    for g in range(GROUPS):
        for j in range(PAGES):
            steps.append(("KT", g, j))
            if g and j == 0:
                steps.append(("SO", g - 1))
            if j:
                steps.append(("SC", g, j - 1))
            pieces((0, 1, 0, 1, 1, 0, 1, 1)[j])
        steps += [("SC", g, PAGES - 1), ("ZN", g)]
        pieces(3)
        steps.append(("AT", g))
        for j in range(PAGES):
            steps.append(("PV", g, j))
            pieces((1, 1, 1, 1, 1, 1, 1, 1)[j])
        if g == GROUPS - 1:
            steps += [("MW", 0), ("LS",)]
        steps += [("PN", g)]
    assert next(prompt, None) is None
    return steps + [("LQ",), ("SO", GROUPS - 1), ("MW", 1), ("LY",)]


class Semaphores:

    def __init__(self, new):
        self.ld_const = new("ld_const")
        self.ld_par = new("ld_par")
        self.ld_x0 = new("ld_x0")
        self.ld_x1 = new("ld_x1")
        self.ld_state = new("ld_state")
        self.ld_table = new("ld_table")
        self.stored = new("stored")
        self.kv_stored = new("kv_stored")
        self.k_stored = new("k_stored")
        self.hi_done = new("hi_done")
        self.split_done = new("split_done")
        self.unit_used = new("unit_used")
        self.par_done = new("par_done")
        self.par_read = new("par_read")
        self.bias_ready = new("bias_ready")
        self.st_done = new("st_done")
        self.st_read = new("st_read")
        self.xt_done = new("xt_done")
        self.x_copied = new("x_copied")
        self.sq_ready = new("sq_ready")
        self.ssq_done = new("ssq_done")
        self.std_ready = new("std_ready")
        self.sig_ready = new("sig_ready")
        self.q_copied = new("q_copied")
        self.gates_ready = new("gates_ready")
        self.mix_ready = new("mix_ready")
        self.silu_times = new("silu_times")
        self.silu_scaled = new("silu_scaled")
        self.norm_h = new("norm_h")
        self.norm_l = new("norm_l")
        self.zeroed = new("zeroed")
        self.sconv_done = new("sconv_done")
        self.conv_done = new("conv_done")
        self.dconv_done = new("dconv_done")
        self.conv_tap = new("conv_tap")
        self.vt_done = new("vt_done")
        self.vt_read = new("vt_read")
        self.ktok_done = new("ktok_done")
        self.ktok_read = new("ktok_read")
        self.cout_done = new("cout_done")
        self.cout_read = new("cout_read")
        self.page_used = new("page_used")
        self.kt_done = new("kt_done")
        self.score_done = new("score_done")
        self.z_read = new("z_read")
        self.weight_s = new("weight_s")
        self.own_done = new("own_done")
        self.own_ready = new("own_ready")
        self.attT_done = new("attT_done")
        self.attT_hi = new("attT_hi")
        self.pscore_done = new("pscore_done")
        self.pscore_read = new("pscore_read")
        self.pweight = new("pweight")
        self.ptr_done = new("ptr_done")
        self.ptr_read = new("ptr_read")
        self.pv_done = new("pv_done")
        self.pv_hi = new("pv_hi")
        self.pv_read = new("pv_read")
        self.ln_sum = new("ln_sum")
        self.ln_cent = new("ln_cent")
        self.ln_sq = new("ln_sq")
        self.ln_sqsum = new("ln_sqsum")
        self.ln_t = new("ln_t")
        self.ln_sig = new("ln_sig")
        self.ln_y = new("ln_y")
        self.ln_hi = new("ln_hi")
        self.ln_lo = new("ln_lo")
        self.dve_step = new("dve_step")
        self.merged_t = new("merged_t")
        self.merged_hi = new("merged_hi")
        self.merged_lo = new("merged_lo")
        self.out_sq = new("out_sq")
        self.wo_sum = new("wo_sum")
        self.silu_ready = new("silu_ready")
        self.act_hi = new("act_hi")
        self.act_lo = new("act_lo")
        self.x1_ready = new("x1_ready")
        self.sq_ready2 = new("sq_ready2")
        self.out_acc_done = new("out_acc_done")
        self.out_acc_read = new("out_acc_read")
        self.y_ready = new("y_ready")
        self.yt_done = new("yt_done")
        self.yt_read = new("yt_read")
        self.raw_loaded = [new("raw_loaded0"), new("raw_loaded1")]
        self.pages_loaded = [new("pages_loaded0"), new("pages_loaded1")]
        self.acc_done = [new("acc_done0"), new("acc_done1")]
        self.acc_read = [new("acc_read0"), new("acc_read1")]
        self.kt_read = [new("kt_read0"), new("kt_read1")]


class Count:

    def __init__(self):
        self.n = 0

    def up(self):
        self.n = self.n + 1
        return 1


def layer_kernel(nc, x_prompt, x_sample, cache_k, cache_v, state_conv, page_table, g_pre_mix, g_post_mix,
                 g_pre_ffn, g_post_ffn, w_in, conv_dw, conv_b, conv_ln_g, conv_ln_b, w_conv_out, att_bias,
                 w_att_out, w_o, w_ffn_in, w_ffn_out, consts,
                 y_prompt, y_sample, k_prompt, v_prompt, conv_prompt, k_sample, v_sample, conv_sample):
    n_phys = cache_k.shape[1]
    rows = lambda w: w[0].rearrange("(k p) c -> p k c", p=P)
    win_v, wconv_v, watt_v, wo_v, wfi_v, wfo_v = map(rows, (w_in, w_conv_out, w_att_out, w_o, w_ffn_in, w_ffn_out))
    STEPS = attention_steps()

    with ExitStack() as ctx:
        arena_bytes = 212768
        arena = ctx.enter_context(nc.sbuf_tensor("arena", [P, arena_bytes // 4], F32))
        base = nc.sbuf_base - arena_bytes

        def at(name, shape, dt, offset):
            size = 4 * int(np.prod(shape[1:]))
            assert offset % 32 == 0 and offset + size <= arena_bytes, (name, offset, size)
            return nc.alloc_sbuf_tensor_at(name, shape, dt, offset=base + offset)

        kc = at("consts", [P, K_COLS], F32, 0)
        vec = at("vec", [P, 44], F32, 1920)
        dw = at("dw", [P, KC, CW], F32, 2112)
        bias_h = at("bias_h", [P, H], F32, 2624)
        bias_r = at("bias_r", [P, 1], F32, 2656)
        ptab = at("ptab", [1, NB * PAGES], I32, 2688)
        O = 2944
        ident, tri, ones = kc[:, K_ID:K_ID + P], kc[:, K_TRI:K_TRI + P], kc[:, K_ONE:K_ONE + P]
        newmask = lambda g: kc[:, K_NEW + NS * g:K_NEW + NS * (g + 1)]
        selq, headmask, eps = kc[:, K_SEL:K_SEL + GB * NT], kc[:, K_HEAD:K_HEAD + H], kc[:, K_EPS:K_EPS + 1]
        gain = lambda n, k: vec[:, 8 * n + k:8 * n + k + 1]
        cvec = lambda n, k: vec[:, 32 + KC * n + k:33 + KC * n + k]

        TB = 4 * T
        xT = at("xT", [P, KD, T], F32, O)
        hH = at("hH", [P, KD, T], F32R, O + KD * TB)
        hL = at("hL", [P, KD, T], F32R, O + 2 * KD * TB)
        pout = at("pout", [P, KD, T], F32, O + KD * TB)
        W0 = O + 3 * KD * TB
        w_raw = at("w_raw", [P, RING, UK, UC], F32, W0)
        w_hi = at("w_hi", [P, RING, UK, UC], F32R, W0 + 16384)
        w_lo = at("w_lo", [P, RING, UK, UC], F32R, W0 + 32768)
        pages = at("pages", [P, RING, GB, C], F32, W0)
        keysT = at("keysT", [P, RING, GB, KC, P], F32, W0 + 16384)
        LS = PAST + NS
        beta_s = at("beta_s", [P, LS], F32, W0 + 32768)
        stick_s = at("stick_s", [P, LS + 1], F32, W0 + 36992)
        wgtT_s = at("wgtT_s", [P, PAGES + 1, P], F32, W0 + 41248)
        own_s = at("own_s", [P, C], F32, W0 + 45856)
        B = W0 + 49152
        acH = at("acH", [P, 2 * KC, T], F32R, B)
        acL = at("acL", [P, 2 * KC, T], F32R, B + 17408)
        yc = at("yc", [P, KC, T], F32, B + 17408 + KC * TB)
        q_even = at("q_even", [P, KC, S], F32, B + 34816)
        q_odd = at("q_odd", [P, KC, S], F32, B + 43008)
        q_s = at("q_s", [P, NB, KC, H, NT], F32, B + 51200)
        kT = at("kT", [P, KC, T], F32, B + 55296)
        vT = at("vT", [P, KC, T], F32, B + 64000)
        k_tok = at("k_tok", [P, S // P, C], F32, B + 72704)
        ks_tok = at("ks_tok", [NS, C], F32, B + 80896)
        v_tok = at("v_tok", [P, S // P, C], F32, B + 82944)
        vs_tok = at("vs_tok", [P, C], F32, B + 91136)
        uP = at("uP", [P, KC, HIST + S], F32, B + 93184)
        uS = at("uS", [P, KC, NB, HIST + NT], F32, B + 101856)
        rstd = at("rstd", [P, T], F32, B + 106208)
        x_tok = at("x_tok", [P, S // P, D], F32, B)
        xs_tok = at("xs_tok", [NS, D], F32, B + 16384)
        st_tok = at("st_tok", [GB * HIST, GROUPS, C], F32, B + 20480)
        par = at("par", [44, P], F32, B + 24576)
        dw_tok = at("dw_tok", [CW, C], F32, B + 25088)
        ab_tok = at("ab_tok", [1, H], F32, B + 27136)
        sq0 = at("sq0", [P, RING, T], F32, B + 55296)
        bias_own = at("bias_own", [P, H], F32, B + 59648)
        sig_u = at("sig_u", [P, MT, T], F32, B + 72704)
        prod = at("prod", [P, NT, NB, CW], F32, B + 72704 + 4352)
        u_new = at("u_new", [P, KC, NS], F32, B + 72704 + 8320)
        conv_tail = at("conv_tail", [HIST, C], F32, B + 8704)
        conv_new = at("conv_new", [NS, C], F32, B + 10752)
        tap_prod = at("tap_prod", [P, 2, S], F32, B + 12800)
        WID = [P * (i + 1) for i in range(S // P)]
        POS = [sum(WID[:i]) for i in range(S // P)]
        FILLS = ((0,), (1, 3), (2,))
        beta_p = at("beta_p", [P, 2, sum(WID)], F32, B + 64000)
        wgtT_p = at("wgtT_p", [P, sum(WID)], F32, B + 74240)
        stick_p = [at("stick_p0", [P, S + 4], F32, B + 79360), at("stick_p1", [P, S + 4], F32, B + 104064)]
        sq1 = at("sq1", [P, RING, T], F32, B + 93184)
        sig1 = at("sig1", [P, RING, T], F32, B + 93184)
        std1 = at("std1", [P, T], F32, B + 97536)
        tmp1 = at("tmp1", [P, RING, T], F32, B + 99712)
        mH = at("mH", [P, KD, T], F32R, B + 34816)
        mL = at("mL", [P, KD, T], F32R, B + 52224)
        sig_c = at("sig_c", [P, MT, T], F32, B + 69632)
        sig_a = at("sig_a", [P, MT, T], F32, B + 73984)
        part = at("part", [P, MT, T], F32, B + 78336)
        both = at("both", [P, MT, T], F32, B + 82688)
        actH = at("actH", [P, KF, T], F32R, B)
        actL = at("actL", [P, KF, T], F32R, B + KF * TB)
        tmp2 = at("tmp2", [P, RING, T], F32, B + 87040)
        sig_f = at("sig_f", [P, MT, T], F32, B + 95744)
        gate_f = at("gate_f", [P, MT, T], F32, B + 100096)
        sq2 = at("sq2", [P, RING, T], F32, B + 95744)
        ssum = at("ssum", [P, T], F32, B + 100096)
        std2 = at("std2", [P, T], F32, B + 102272)
        y_tok = at("y_tok", [P, S // P + 1, D], F32, B)

        ps = ctx.enter_context(nc.psum_tensor("ps", [P, 8, 512], F32))

        s = Semaphores(lambda name: ctx.enter_context(nc.semaphore(name)))
        raw_loaded, acc_done, acc_read, pages_loaded, kt_read = s.raw_loaded, s.acc_done, s.acc_read, s.pages_loaded, s.kt_read



        cache = (cache_k[0].rearrange("n r h d -> n r (h d)"), cache_v[0].rearrange("n r h d -> n r (h d)"))

        def keys_used(g, j, b):
            return GB * (PAGES * g + j) + b + 1 + 3 * g

        halves = lambda a: a.rearrange("p (h t) -> p h t", h=2)
        acc = lambda c: ps[:, 2 * (c % 2):2 * (c % 2) + 2, 0:HT]
        block = ctx.enter_context(nc.Block())

        @block.sync
        def _(sp):
            xp_v, xs_v = x_prompt[0].rearrange("(j p) d -> p j d", p=P), x_sample.rearrange("b t d -> (b t) d")

            def load_x(half):
                cols = slice(512 * half, 512 * half + 512)
                sp.dma_start(x_tok[:, :, cols], xp_v[:, :, cols]).then_inc((s.ld_x0, s.ld_x1)[half], 16)

            sp.dma_start(kc[:], consts).then_inc(s.ld_const, 16)
            sp.dma_start(xs_tok[:], xs_v).then_inc(s.ld_x0, 16)
            load_x(0)
            for n, g in enumerate((g_pre_mix, g_post_mix, g_pre_ffn, g_post_ffn)):
                sp.dma_start(par[8 * n:8 * n + 8, :], g[0].rearrange("(k p) -> k p", p=P)).then_inc(s.ld_par, 16)
            for n, g in enumerate((conv_b, conv_ln_g, conv_ln_b)):
                sp.dma_start(par[32 + KC * n:36 + KC * n, :], g[0].rearrange("(k p) -> k p", p=P)).then_inc(s.ld_par, 16)
            sp.dma_start(dw_tok[:], conv_dw[0]).then_inc(s.ld_par, 16)
            sp.dma_start(ab_tok[:], att_bias).then_inc(s.ld_par, 16)

            def load_unit(par_, lo, hi, need=None):
                if need is not None:
                    sp.wait_ge(s.split_done, need)
                sp.dma_start(w_raw[:, par_, 0:4], lo).then_inc(raw_loaded[par_], 16)
                sp.dma_start(w_raw[:, par_, 4:4 + hi.shape[1]], hi).then_inc(raw_loaded[par_], 16)

            def columns(v, c, k0=0, k1=UK):
                return v[:, k0:k0 + 4, bass.ds(c, UC)], v[:, k0 + 4:k1, bass.ds(c, UC)]

            load_unit(0, *columns(win_v, FIRST_UNITS[0]))
            load_x(1)
            sp.dma_start(st_tok[:], state_conv[0].rearrange("(g b) r c -> (b r) g c", g=GROUPS)).then_inc(s.ld_state, 16)
            sp.dma_start(ptab[:], page_table.rearrange("(o b) n -> o (b n)", o=1)).then_inc(s.ld_table, 16)
            load_unit(1, *columns(win_v, FIRST_UNITS[1]))
            sp.dma_start(conv_sample[0, :, 0:HIST - NT, :], state_conv[0, :, NT:HIST, :]).then_inc(s.stored, 16)
            for n in range(2, U_MERGE):
                load_unit(n % 2, *columns(win_v, FIRST_UNITS[n]), need=n - 1)

            sp.wait_ge(s.ld_table, 16)

            def load_pages(g, kv, j, slot, used=None, seqs=range(GB - 1)):
                for b in seqs:
                    if used is not None and (b == 0 or kv == 0):
                        used(b)
                    page = sp.value_load(ptab[0:1, bass.ds((GB * g + b) * PAGES + j, 1)], min_val=0, max_val=n_phys - 1)
                    sp.dma_start(pages[:, slot, b, :], cache[kv][bass.ds(page, 1)].rearrange("n r c -> r (n c)"))\
                        .then_inc(pages_loaded[slot], 16)

            sp.wait_ge(s.split_done, U_MERGE)
            for slot in range(RING):
                load_pages(0, 0, slot, slot, seqs=range(GB))
            sp.wait_ge(s.ktok_read, KC + 1)
            sp.dma_start(k_prompt[0, 0].rearrange("(j p) h d -> p j (h d)", p=P), k_tok[:]).then_inc(s.k_stored, 16)
            sp.dma_start(k_sample[0].rearrange("b t h d -> (b t) (h d)"), ks_tok[:]).then_inc(s.k_stored, 16)

            def small_stores():
                sp.wait_ge(s.vt_read, KC + 1)
                sp.dma_start(v_prompt[0, 0].rearrange("(j p) h d -> p j (h d)", p=P), v_tok[:]).then_inc(s.kv_stored, 16)
                sp.dma_start(v_sample[0].rearrange("b t h d -> (b t) (h d)"), vs_tok[0:NS, :]).then_inc(s.kv_stored, 16)
                sp.wait_ge(s.cout_read, 2)
                sp.dma_start(conv_prompt[0, 0], conv_tail[:]).then_inc(s.kv_stored, 16)
                for b in range(NB):
                    sp.dma_start(conv_sample[0, b, HIST - NT:HIST, :], conv_new[NT * b:NT * b + NT, :]).then_inc(s.kv_stored, 16)

            for g in range(GROUPS):
                for kv in range(2):
                    for slot in range(RING):
                        if kv or g:
                            if kv:
                                sp.wait_ge(s.kt_done, keys_used(g, PAGES - RING + slot, GB - 1))
                            else:
                                sp.wait_ge(s.page_used, PAGES * g - RING + slot + 1)
                            load_pages(g, kv, slot, slot)
                    if g == 0 and kv == 1:
                        small_stores()
                    with sp.Fori(1, PAGES // RING) as i:
                        for slot in range(RING):
                            if kv:
                                used = lambda b: sp.wait_ge(s.page_used, i * RING + (PAGES * g + slot - RING + 1))
                            else:
                                used = lambda b: sp.wait_ge(s.kt_done, i * (RING * GB) + keys_used(g, slot - RING, b))
                            load_pages(g, kv, i * RING + slot, slot, used)

            pages_left = {U_MERGE: GROUPS * PAGES - 1, U_MERGE + 1: GROUPS * PAGES}
            for mp in range(D // UC):
                for j in range(3):
                    n = U_MERGE + 3 * mp + j
                    if j < 2:
                        src = columns(win_v, (COL_GC, COL_GA)[j] + UC * mp)
                    else:
                        src = wconv_v[:, :, UC * mp:UC * mp + UC], watt_v[:, :, UC * mp:UC * mp + UC]
                    if n in pages_left:
                        sp.wait_ge(s.page_used, pages_left[n])
                    load_unit(n % 2, *src, need=n - 1)
            for m in range(D // UC):
                n = U_WO + m
                load_unit(n % 2, *columns(wo_v, UC * m), need=n - 1)
            with sp.Fori(0, FF // UC) as i:
                for j in range(2):
                    load_unit(j, *columns(wfi_v, i * UC + j * FF), need=i * 2 + (U_FFI + j - 1))
            for mp in range(D // UC):
                for j in range(3):
                    n = U_FFO + 3 * mp + j
                    load_unit(n % 2, *columns(wfo_v, UC * mp, 8 * j, min(8 * j + 8, KF)), need=n - 1)

            yp_v = y_prompt[0].rearrange("(j p) d -> p j d", p=P)
            for half in range(2):
                sp.wait_ge(s.yt_read, (KD // 2) * (half + 1))
                cols = slice(512 * half, 512 * half + 512)
                sp.dma_start(yp_v[:, :, cols], y_tok[:, 0:4, cols]).then_inc(s.stored, 16)
                sp.dma_start(y_sample.rearrange("b t d -> (b t) d")[:, cols], y_tok[0:NS, 4, cols]).then_inc(s.stored, 16)
            sp.wait_ge(s.k_stored, 32)
            sp.wait_ge(s.kv_stored, 16 * (3 + NB))
            sp.wait_ge(s.stored, 16 * 5)

        @block.tensor
        def _(pe):
            def gemm_tile(slot, m, out, rh, rl, ks, start=True, stop=True):
                for n, (k, kk) in enumerate(ks):
                    cols = slice(P * m, P * m + P)
                    for q, (w, r) in enumerate(((w_hi, rh), (w_hi, rl), (w_lo, rh))):
                        for half in range(2):
                            last = pe.matmul(out[:, half], w[:, slot, k, cols], r[:, kk, HT * half:HT * half + HT],
                                             start=start and n == 0 and q == 0, stop=stop and n == len(ks) - 1 and q == 2)
                return last

            all_k = [(k, k) for k in range(UK)]

            def acc_tile(c_half, c, slot, m, rh, rl, ks=all_k, wait=True):
                if wait:
                    pe.wait_ge(acc_read[c % 2], c_half)
                gemm_tile(slot, m, acc(c), rh, rl, ks).then_inc(acc_done[c % 2], 1)

            def sum_squares(sq, k, bank=4, n=KD):
                for half in range(2):
                    last = pe.matmul(ps[:, bank + half, 0:HT], ones, sq[:, HT * half:HT * half + HT],
                                     start=(k == 0), stop=(k == n - 1))
                return last

            pe.wait_ge(s.ld_const, 16)
            pe.wait_ge(s.ld_x0, 32)
            for k in range(KD):
                last = pe.transpose(ps[:, 3, NS * k:NS * k + NS], xs_tok[:, P * k:P * k + P], ident[0:NS, 0:NS])
            last.then_inc(s.xt_done, 1)
            for k in range(KD + 1):
                if k < KD:
                    if k == KD // 2:
                        pe.wait_ge(s.ld_x1, 16)
                    if k >= 2:
                        pe.wait_ge(s.x_copied, k)
                    for j in range(S // P):
                        last = pe.transpose(ps[:, 6 + k % 2, P * j:P * j + P], x_tok[:, j, P * k:P * k + P], ident)
                    last.then_inc(s.xt_done, 1)
                if k == 0:
                    pe.wait_ge(s.ld_par, 16 * 9)
                    pe.transpose(ps[:, 2, 0:44], par[:, :], ident[0:44, 0:44])
                    for n in range(KC):
                        pe.transpose(ps[:, 2, 64 + CW * n:64 + CW * n + CW], dw_tok[:, P * n:P * n + P], ident[0:CW, 0:CW])
                    pe.matmul(ps[:, 2, 192:200], ones[0:1, :], ab_tok[0:1, :], start=True, stop=True).then_inc(s.par_done, 1)
                else:
                    pe.wait_ge(s.sq_ready, k)
                    sum_squares(sq0[:, (k - 1) % 2], k - 1).then_inc(s.ssq_done, 1)
                if k > KD // 2:
                    if k == KD // 2 + 1:
                        pe.wait_ge(s.split_done, 1)
                    for kk in range(2 * (k - KD // 2 - 1), 2 * (k - KD // 2)):
                        pe.wait_ge(s.norm_l, kk + 1)
                        last = gemm_tile(0, 0, acc(0), hH, hL, [(kk, kk)], start=(kk == 0), stop=(kk == KD - 1))
            last.then_inc(acc_done[0], 1)
            pe.wait_ge(s.ld_state, 16)
            pe.wait_ge(s.x_copied, KD + 1)
            pe.wait_ge(s.par_read, 1)
            for g in range(GROUPS):
                for k in range(KC):
                    last = pe.transpose(ps[:, 6 + g, GB * HIST * k:GB * HIST * (k + 1)], st_tok[:, g, P * k:P * k + P],
                                        ident[0:GB * HIST, 0:GB * HIST])
                last.then_inc(s.st_done, 1)

            def in_pair(i, peeled):
                for j in range(2):
                    pe.wait_ge(s.split_done, i * 2 + (j + 1))
                    for m in range(MT):
                        t = 2 * j + m
                        if not peeled or t:
                            acc_tile(i * 2 + t // 2, t, j, m, hH, hL, wait=not peeled or t >= 2)

            in_pair(0, True)
            with pe.Fori(1, U_MERGE // 2) as i:
                in_pair(i, False)

            n_in = U_MERGE
            pe.wait_ge(acc_read[0], n_in)
            pe.wait_ge(acc_read[1], n_in)
            pe.wait_ge(s.st_read, GROUPS)
            for k in range(KC):
                pe.transpose(ps[0:HIST, 0, P * k:P * k + P], uP[:, k, S:S + HIST], ident)
                last = pe.transpose(ps[0:NS, 1, P * k:P * k + P], u_new[:, k], ident)
            last.then_inc(s.cout_done, 1)
            kinds = ((vT, 4, 6, s.vt_done, s.vt_read), (kT, 5, 7, s.ktok_done, s.ktok_read))
            for k in range(KC):
                for src, big, small, done, read in kinds:
                    if k:
                        pe.wait_ge(read, k)
                    for j in range(S // P):
                        last = pe.transpose(ps[:, big, P * j:P * j + P], src[:, k, P * j:P * j + P], ident)
                    last.then_inc(done, 1)
            for src, big, small, done, read in kinds:
                for k in range(KC):
                    last = pe.transpose(ps[0:NS, small, P * k:P * k + P], src[:, k, S:T], ident)
                last.then_inc(done, 1)

            pe.wait_ge(s.q_copied, H // 2)
            pe.wait_ge(s.cout_read, 2)
            pe.wait_ge(s.vt_read, KC + 1)
            pe.wait_ge(s.ktok_read, KC + 1)
            n_kt = n_z = n_ps = n_pt = n_pw = 0

            def next_kt():
                nonlocal n_kt
                if n_kt >= 2:
                    pe.wait_ge(kt_read[n_kt % 2], n_kt // 2)
                n_kt += 1
                return 2 + (n_kt - 1) % 2

            for st in STEPS:
                what, a = st[0], st[1:]
                if what == "KT":
                    g, j = a
                    r = 2 * PAGES * g + j
                    pe.wait_ge(pages_loaded[r % 2], 16 * GB * (r // 2 + 1))
                    for b in range(GB):
                        bank = next_kt()
                        for k in range(KC):
                            last = pe.transpose(ps[:, bank, P * k:P * k + P], pages[:, r % 2, b, P * k:P * k + P], ident)
                        last.then_inc(s.kt_done, 1)
                elif what == "SC":
                    g, j = a
                    ks = PAGES * g + j
                    upto = 4 * (ks + 1) + 3 * g
                    pe.wait_ge(kt_read[0], (upto + 1) // 2)
                    pe.wait_ge(kt_read[1], upto // 2)
                    if j % 4 == 0 and n_z:
                        pe.wait_ge(s.z_read, n_z)
                    for k in range(KC):
                        for b in range(GB):
                            last = pe.matmul(ps[32 * b:32 * b + 32, 4, P * (j % 4):P * (j % 4) + P],
                                             q_s[:, GB * g + b, k], keysT[:, ks % 2, b, k], start=(k == 0),
                                             stop=(k == KC - 1), skip_group_check=True)
                    last.then_inc(s.score_done, 1)
                    if j % 4 == 3:
                        n_z += 1
                elif what == "ZN":
                    g, = a
                    pe.wait_ge(s.z_read, n_z)
                    for k in range(KC):
                        for b in range(GB):
                            last = pe.matmul(ps[32 * b:32 * b + 32, 4, 0:NS], q_s[:, GB * g + b, k], kT[:, k, S:T],
                                             start=(k == 0), stop=(k == KC - 1), skip_group_check=True)
                    last.then_inc(s.score_done, 1)
                    n_z += 1
                elif what == "AT":
                    g, = a
                    pe.wait_ge(s.weight_s, g + 1)
                    for blocks in (range(0, 4), range(4, 8), range(8, 9)):
                        bank = next_kt()
                        for n, j in enumerate(blocks):
                            w = P if j < PAGES else NS
                            last = pe.transpose(ps[0:w, bank, P * n:P * n + P], beta_s[:, P * j:P * j + w], ident)
                        last.then_inc(s.kt_done, 1)
                    pe.wait_ge(kt_read[0], (n_kt + 1) // 2)
                    pe.wait_ge(kt_read[1], n_kt // 2)
                    pe.wait_ge(s.z_read, n_z)
                elif what in ("PV", "PN"):
                    g = a[0]
                    j = a[1] if what == "PV" else PAGES
                    r = 2 * PAGES * g + PAGES + j
                    if what == "PV":
                        pe.wait_ge(pages_loaded[r % 2], 16 * GB * (r // 2 + 1))
                    for b in range(GB):
                        v = pages[:, r % 2, b, :] if what == "PV" else vs_tok[:, :]
                        last = pe.matmul(ps[32 * b:32 * b + 32, 4, :], wgtT_s[:, j, 32 * b:32 * b + 32], v,
                                         start=(j == 0), stop=(j == PAGES), skip_group_check=True)
                    last.then_inc(s.page_used if what == "PV" else s.own_done, 1)
                elif what == "SO":
                    g, = a
                    pe.wait_ge(s.own_ready, g + 1)
                    for k in range(KC):
                        last = pe.matmul(ps[:, 4, GB * NT * k:GB * NT * (k + 1)], own_s[:, P * k:P * k + P], selq,
                                         start=True, stop=True, skip_group_check=True)
                    last.then_inc(s.attT_done, 1)
                    n_z += 1
                elif what == "PS":
                    h, part_ = a
                    q = (q_even, q_odd)[h % 2]
                    for i in (2 * part_, 2 * part_ + 1):
                        if n_ps >= 2:
                            pe.wait_ge(s.pscore_read, n_ps - 1)
                        pe.matmul(ps[:, n_ps % 2, 0:WID[i]], q[:, h // 2, P * i:P * i + P], kT[:, h // 2, 0:WID[i]],
                                  start=True, stop=True).then_inc(s.pscore_done, 1)
                        n_ps += 1
                elif what == "PT":
                    h, = a
                    pe.wait_ge(s.pweight, 4 * (h + 1))
                    for fill in FILLS:
                        if n_pt >= 2:
                            pe.wait_ge(s.ptr_read, n_pt - 1)
                        at_ = 0
                        for j in fill:
                            for i in range(j, S // P):
                                last = pe.transpose(ps[:, 6 + n_pt % 2, at_:at_ + P],
                                                    beta_p[:, h % 2, POS[i] + P * j:POS[i] + P * j + P], ident)
                                at_ += P
                        last.then_inc(s.ptr_done, 1)
                        n_pt += 1
                elif what == "PO":
                    h, = a
                    pe.wait_ge(s.ptr_read, len(FILLS) * (h + 1))
                    if h % 2 == 0 and h:
                        pe.wait_ge(s.pv_read, h // 2)
                    at_ = 0
                    for j in sum(FILLS, ()):
                        w = S - P * j
                        last = pe.matmul(ps[64 * (h % 2):64 * (h % 2) + 64, 5, P * j:S], v_tok[:, j, DH * h:DH * h + DH],
                                         wgtT_p[:, at_:at_ + w], start=(j == 0), stop=(at_ + w == sum(WID)),
                                         skip_group_check=True)
                        at_ += w
                    last.then_inc(s.pv_done, 1)
                elif what == "LS":
                    pe.wait_ge(s.conv_done, 2)
                    pe.wait_ge(s.dconv_done, 2)
                    pe.wait_ge(s.sconv_done, KC)
                    pe.wait_ge(s.ptr_read, n_pt)
                    for k in range(KC):
                        last = sum_squares(yc[:, k], k, bank=6, n=KC)
                    last.then_inc(s.ln_sum, 1)
                elif what == "LQ":
                    pe.wait_ge(s.ln_cent, KC)
                    for k in range(KC):
                        pe.wait_ge(s.ln_sq, k + 1)
                        sum_squares(sq1[:, k % 2], k, bank=6, n=KC).then_inc(s.ln_sqsum, 1)

            def merge_units(i):
                for q in range(2):
                    for j in range(3):
                        u = 3 * q + j
                        slot = u % 2
                        pe.wait_ge(s.split_done, i * 6 + (U_MERGE + u + 1))
                        if j < 2:
                            tiles = [(2 * j + m, m, hH, hL, all_k) for m in range(MT)]
                        else:
                            pe.wait_ge(s.ln_lo, KC)
                            pe.wait_ge(s.z_read, n_z)
                            pe.wait_ge(s.pv_read, H // 2)
                            tiles = [(4 + m, m, acH, acL, [(k, KC + k) for k in range(KC)]) for m in range(MT)]
                            tiles += [(6 + m, m, acH, acL, [(KC + k, k) for k in range(KC)]) for m in range(MT)]
                        for t, m, rh, rl, ks in tiles:
                            acc_tile(i * 8 + (A_MERGE // 2 + 4 * q + t // 2), t, slot, m, rh, rl, ks)

            pe.wait_ge(s.pscore_read, n_ps)
            pe.wait_ge(kt_read[0], (n_kt + 1) // 2)
            pe.wait_ge(kt_read[1], n_kt // 2)
            with pe.Fori(0, 2) as i:
                merge_units(i)
            def wo_units(i, peeled):
                for j in range(2):
                    if not peeled or j:
                        pe.wait_ge(s.split_done, i * 2 + (U_WO + j + 1))
                    for m in range(MT):
                        t = 2 * j + m
                        if not peeled or t:
                            acc_tile(i * 2 + (A_WO // 2 + t // 2), t, j, m, mH, mL)

            pe.wait_ge(s.split_done, U_WO + 1)
            pe.wait_ge(acc_read[0], A_WO // 2)
            for k in range(KD):
                pe.wait_ge(s.merged_lo, k + 1)
                last = gemm_tile(0, 0, acc(0), mH, mL, [(k, k)], start=(k == 0), stop=(k == KD - 1))
            last.then_inc(acc_done[0], 1)
            wo_units(0, True)
            with pe.Fori(1, 2) as i:
                wo_units(i, False)

            def total(need):
                pe.wait_ge(s.wo_sum, need)
                for half in range(2):
                    last = pe.matmul(ps[:, 4 + half, 0:HT], ones, ssum[:, HT * half:HT * half + HT], start=True, stop=True)
                last.then_inc(s.ssq_done, 1)

            total(KD)
            def ffn_pair(i, peeled):
                for j in range(2):
                    if not peeled or j:
                        pe.wait_ge(s.split_done, i * 2 + (U_FFI + j + 1))
                    for m in range(MT):
                        t = 2 * j + m
                        if not peeled or t:
                            acc_tile(i * 2 + (A_FFI // 2 + t // 2), t, j, m, hH, hL)

            pe.wait_ge(s.split_done, U_FFI + 1)
            pe.wait_ge(acc_read[0], A_FFI // 2)
            for k in range(KD):
                pe.wait_ge(s.norm_l, KD + k + 1)
                last = gemm_tile(0, 0, acc(0), hH, hL, [(k, k)], start=(k == 0), stop=(k == KD - 1))
                if k == KD - 1:
                    last.then_inc(acc_done[0], 1)
                pe.wait_ge(s.sq_ready2, k + 1)
                sum_squares(sq2[:, k % 2], k, bank=6).then_inc(s.ssq_done, 1)
            ffn_pair(0, True)
            with pe.Fori(1, FF // UC) as i:
                ffn_pair(i, False)
            pe.wait_ge(s.act_lo, KF)
            pe.wait_ge(acc_read[0], (A_FFI + 4 * (FF // UC)) // 2)
            pe.wait_ge(acc_read[1], (A_FFI + 4 * (FF // UC)) // 2)
            for mp in range(D // UC):
                for j in range(3):
                    n = U_FFO + 3 * mp + j
                    pe.wait_ge(s.split_done, n + 1)
                    ks = [(k, 8 * j + k) for k in range(min(8, KF - 8 * j))]
                    for m in range(MT):
                        if j == 0 and mp >= 2:
                            pe.wait_ge(s.out_acc_read, 2 * (mp - 2) + m + 1)
                        bank = 4 * (mp % 2) + 2 * m
                        last = gemm_tile(n % 2, m, ps[:, bank:bank + 2, 0:HT], actH, actL, ks, start=(j == 0), stop=(j == 2))
                        if j == 2:
                            last.then_inc(s.out_acc_done, 1)
                        elif m == MT - 1:
                            last.then_inc(s.unit_used, 1)
            pe.wait_ge(s.wo_sum, 2 * KD)
            pe.wait_ge(s.out_acc_read, KD)
            total(2 * KD)
            for k in range(KD):
                pe.wait_ge(s.y_ready, k + 1)
                if k >= 2:
                    pe.wait_ge(s.yt_read, k - 1)
                for j in range(S // P):
                    pe.transpose(ps[:, 2 * (k % 2), P * j:P * j + P], pout[:, k, P * j:P * j + P], ident)
                pe.transpose(ps[0:NS, 2 * (k % 2) + 1, 0:P], pout[:, k, S:T], ident).then_inc(s.yt_done, 1)

        @block.scalar
        def _(act):
            def used(n):
                if n < U_MERGE:
                    act.wait_ge(acc_done[1], n + 1)
                elif n < U_WO:
                    u = n - U_MERGE
                    act.wait_ge(acc_done[1], (A_MERGE + 8 * (u // 3) + (2, 4, 8)[u % 3]) // 2)
                elif n < U_FFO:
                    act.wait_ge(acc_done[1], A_WO // 2 + n - U_WO + 1)
                elif (n - U_FFO) % 3 < 2:
                    act.wait_ge(s.unit_used, 2 * ((n - U_FFO) // 3) + (n - U_FFO) % 3 + 1)
                else:
                    act.wait_ge(s.out_acc_done, 2 * ((n - U_FFO) // 3) + 2)

            def split_hi(n):
                act.wait_ge(raw_loaded[n % 2], 32 * (n // 2 + 1))
                if n >= 2:
                    used(n - 2)
                act.copy(w_hi[:, n % 2], w_raw[:, n % 2]).then_inc(s.hi_done, 1)

            act.wait_ge(s.par_read, 1)
            act.wait_ge(s.x_copied, 1)
            for k in range(KD):
                act.wait_ge(s.x_copied, k + 2)
                act.activation(hH[:, k], xT[:, k], ACT.Identity, scale=gain(0, k)).then_inc(s.norm_h, 1)
                if k >= 2:
                    act.wait_ge(s.ssq_done, k - 1)
                act.activation(sq0[:, k % 2], xT[:, k], ACT.Square).then_inc(s.sq_ready, 1)
                if k == KD // 2 - 1:
                    split_hi(0)

            def std(out, bank, width, need, sem=s.ssq_done):
                act.wait_ge(sem, need)
                act.activation(halves(out[:]), ps[:, bank:bank + 2, 0:HT], ACT.Sqrt, bias=eps, scale=1.0 / width)\
                    .then_inc(s.std_ready, 1)

            std(rstd, 4, D, KD)
            act.wait_ge(s.zeroed, 5)
            for n in range(U_MERGE):
                if n + 1 < U_MERGE:
                    split_hi(n + 1)
                for m in range(MT):
                    if n in (0, 2):
                        act.wait_ge(acc_read[m], n + 1)
                        act.activation(sig_u[:, m], sig_u[:, m], ACT.Sigmoid).then_inc(s.sig_ready, 1)
                    elif n in (4, 5):
                        p = 2 * (n - 4) + m
                        act.wait_ge(acc_read[m], n + 1)
                        for r, (q, lo) in enumerate(((q_even, 0), (q_odd, 64))):
                            act.copy(q[lo:lo + 64, p], sig_u[lo:lo + 64, m, 0:S])
                            last = act.copy(q_s[lo:lo + 64, :, p, 2 * p + r, :],
                                            sig_u[lo:lo + 64, m, S:T].rearrange("p (b t) -> p b t", t=NT))
                        last.then_inc(s.q_copied, 1)
            act.wait_ge(s.sconv_done, KC)
            for k in range(KC):
                act.wait_ge(s.ktok_done, k + 1)
                act.copy(k_tok[:, :, P * k:P * k + P], ps[:, 5, :].rearrange("p (j c) -> p j c", c=P)).then_inc(s.ktok_read, 1)
            act.wait_ge(s.ktok_done, KC + 1)
            act.copy(ks_tok[:, :], ps[0:NS, 7, :]).then_inc(s.ktok_read, 1)

            def load_last(r):
                if r < 2 * GROUPS * PAGES:
                    g, kv, j = r // (2 * PAGES), r // PAGES % 2, r % PAGES
                    seq = (GB * g + GB - 1) * PAGES + j
                    page = act.value_load(ptab[0:1, seq:seq + 1], min_val=0, max_val=n_phys - 1)
                    act.dma_start(pages[:, r % 2, GB - 1, :], cache[kv][bass.ds(page, 1)].rearrange("n r c -> r (n c)"))\
                        .then_inc(pages_loaded[r % 2], 16)

            act.wait_ge(s.bias_ready, 1)
            act.wait_ge(s.ld_table, 16)
            n_kt = 0
            for st in STEPS:
                what, a = st[0], st[1:]
                if what == "KT":
                    g, j = a
                    ks = PAGES * g + j
                    if ks >= 2:
                        act.wait_ge(s.score_done, ks - 1 + (ks - 2) // PAGES)
                    for b in range(GB):
                        act.wait_ge(s.kt_done, n_kt + 1)
                        act.copy(keysT[:, ks % 2, b], ps[:, 2 + n_kt % 2, :].rearrange("p (k c) -> p k c", c=P))\
                            .then_inc(kt_read[n_kt % 2], 1)
                        n_kt += 1
                    load_last(2 * PAGES * g + j + RING)
                elif what == "PV":
                    g, j = a
                    act.wait_ge(s.page_used, PAGES * g + j + 1)
                    load_last(2 * PAGES * g + PAGES + j + RING)
                elif what == "SC" and a[1] % 4 == 3:
                    g, j = a
                    act.wait_ge(s.score_done, PAGES * g + j + 1 + g)
                    act.activation(beta_s[:, P * (j - 3):P * (j + 1)], ps[:, 4, :], ACT.Sigmoid, bias=bias_r[:, :], scale=SCALE)\
                        .then_inc(s.z_read, 1)
                elif what == "ZN":
                    g, = a
                    act.wait_ge(s.score_done, (PAGES + 1) * (g + 1))
                    act.activation(beta_s[:, PAST:LS], ps[:, 4, 0:NS], ACT.Sigmoid, bias=bias_r[:, :], scale=SCALE)\
                        .then_inc(s.z_read, 1)
                elif what == "AT":
                    for part_ in range(3):
                        bank = 2 + n_kt % 2
                        act.wait_ge(s.kt_done, n_kt + 1)
                        if part_ < 2:
                            act.copy(wgtT_s[:, 4 * part_:4 * part_ + 4], ps[:, bank, :].rearrange("p (k c) -> p k c", c=P))\
                                .then_inc(kt_read[n_kt % 2], 1)
                        else:
                            act.copy(wgtT_s[0:NS, PAGES], ps[0:NS, bank, 0:P]).then_inc(kt_read[n_kt % 2], 1)
                        n_kt += 1
                elif what == "SO":
                    g, = a
                    act.wait_ge(s.attT_done, g + 1)
                    act.copy(acH[:, 0:KC, S + GB * NT * g:S + GB * NT * (g + 1)],
                             ps[:, 4, 0:KC * GB * NT].rearrange("p (k c) -> p k c", k=KC)).then_inc(s.attT_hi, 1)
                elif what == "PS":
                    h, part_ = a
                    if h == part_ == 0:
                        act.wait_ge(s.k_stored, 32)
                    for i in (2 * part_, 2 * part_ + 1):
                        n = 4 * h + i
                        act.wait_ge(s.pscore_done, n + 1)
                        act.activation(beta_p[:, h % 2, POS[i]:POS[i] + WID[i]], ps[:, n % 2, 0:WID[i]], ACT.Sigmoid,
                                       bias=bias_h[:, h:h + 1], scale=SCALE).then_inc(s.pscore_read, 1)
                elif what == "PT":
                    h, = a
                    at_ = 0
                    for n, fill in enumerate(FILLS, len(FILLS) * h):
                        w = sum(S - P * j for j in fill)
                        act.wait_ge(s.ptr_done, n + 1)
                        act.copy(wgtT_p[:, at_:at_ + w], ps[:, 6 + n % 2, 0:w]).then_inc(s.ptr_read, 1)
                        at_ += w
                elif what == "PO" and a[0] % 2:
                    h, = a
                    act.wait_ge(s.pv_done, h + 1)
                    act.copy(acH[:, h // 2, 0:S], ps[:, 5, :]).then_inc(s.pv_hi, 1)
                elif what == "MW":
                    split_hi(U_MERGE + a[0])
                elif what == "LS":
                    for k in range(KC):
                        act.wait_ge(s.ln_cent, k + 1)
                        if k >= 2:
                            act.wait_ge(s.ln_sqsum, k - 1)
                        act.activation(sq1[:, k % 2], yc[:, k], ACT.Square).then_inc(s.ln_sq, 1)
                elif what == "LQ":
                    std(std1, 6, C, KC, s.ln_sqsum)
                elif what == "LY":
                    act.wait_ge(s.kv_stored, 16 * (3 + NB))
                    for k in range(KC + 1):
                        if k < KC:
                            act.wait_ge(s.ln_t, k + 1)
                            if k >= 2:
                                act.wait_ge(s.ln_y, k - 1)
                            act.activation(sig1[:, k % 2], tmp1[:, k % 2], ACT.Sigmoid, bias=cvec(2, k)).then_inc(s.ln_sig, 1)
                        if k >= 1:
                            act.wait_ge(s.ln_y, k)
                            act.copy(acH[:, KC + k - 1], tmp1[:, (k - 1) % 2]).then_inc(s.ln_hi, 1)
            for mp in range(D // UC):
                for j in range(3):
                    if mp or j:
                        split_hi(U_MERGE + 3 * mp + j + 1)
                    for m in range(MT):
                        if j < 2:
                            c = A_MERGE + 8 * mp + 2 * j + m
                            act.wait_ge(acc_read[m], c // 2 + 1)
                            gate = (sig_c, sig_a)[j][:, m]
                            act.activation(gate, gate, ACT.Sigmoid).then_inc(s.gates_ready, 1)
                        else:
                            act.wait_ge(s.merged_t, 2 * mp + m + 1)
                            act.copy(mH[:, 2 * mp + m], both[:, m]).then_inc(s.merged_hi, 1)

            def copy_and_square(t, a, read, sums):
                if sums is not None:
                    act.wait_ge(s.wo_sum, sums)
                act.activation(halves(sq2[:, t % 2]), a, ACT.Square).then_inc(s.out_sq, 1)
                act.copy(halves(pout[:, t]), a).then_inc(read, 1)

            for j in range(D // UC):
                split_hi(U_WO + j + 1)
                for m in range(MT):
                    t = 2 * j + m
                    act.wait_ge(acc_done[m], (A_WO + t) // 2 + 1)
                    copy_and_square(t, acc(m), acc_read[m], t - 1 if t >= 2 else None)
            std(std2, 4, D, KD + 1)
            for k in range(KD):
                act.wait_ge(s.x1_ready, k + 1)
                if k >= 2:
                    act.wait_ge(s.ssq_done, KD + 1 + k - 1)
                act.activation(hH[:, k], xT[:, k], ACT.Identity, scale=gain(2, k)).then_inc(s.norm_h, 1)
                act.activation(sq2[:, k % 2], xT[:, k], ACT.Square).then_inc(s.sq_ready2, 1)
            std(rstd, 6, D, 2 * KD + 1)
            with act.Fori(0, FF // UC) as i:
                for j in range(2):
                    n1 = U_FFI + j + 1
                    act.wait_ge(raw_loaded[n1 % 2], i * 32 + 32 * (n1 // 2 + 1))
                    act.wait_ge(acc_done[1], i * 2 + (A_WO // 2 + n1 - 2 - U_WO + 1))
                    act.copy(w_hi[:, n1 % 2], w_raw[:, n1 % 2]).then_inc(s.hi_done, 1)
                    for m in range(MT):
                        if j == 0:
                            act.wait_ge(acc_read[m], i * 2 + (A_FFI // 2 + 1))
                            act.activation(sig_f[:, m], gate_f[:, m], ACT.Sigmoid).then_inc(s.silu_ready, 1)
                        else:
                            act.wait_ge(acc_read[m], i * 2 + (A_FFI // 2 + 2))
                            act.copy(actH[:, bass.ds(i * 2 + m, 1), :], sig_f[:, m:m + 1]).then_inc(s.act_hi, 1)
            for mp in range(D // UC):
                for j in range(3):
                    n = U_FFO + 3 * mp + j
                    if n + 1 < U_FFO + 12:
                        split_hi(n + 1)
                for m in range(MT):
                    t = 2 * mp + m
                    act.wait_ge(s.out_acc_done, t + 1)
                    bank = 4 * (mp % 2) + 2 * m
                    copy_and_square(t, ps[:, bank:bank + 2, 0:HT], s.out_acc_read, KD + t - 1 if t >= 2 else None)
            std(std2, 4, D, 2 * KD + 2)
            for k in range(KD):
                act.wait_ge(s.yt_done, k + 1)
                act.copy(y_tok[:, 0:4, P * k:P * k + P], ps[:, 2 * (k % 2), :].rearrange("p (j c) -> p j c", c=P))
                act.copy(y_tok[0:NS, 4, P * k:P * k + P], ps[0:NS, 2 * (k % 2) + 1, 0:P]).then_inc(s.yt_read, 1)

        @block.vector
        def _(dve):
            step = Count()

            def split_lo(n):
                dve.wait_ge(s.hi_done, n + 1)
                dve.tensor_tensor(w_lo[:, n % 2], w_raw[:, n % 2], w_hi[:, n % 2], ALU.subtract).then_inc(s.split_done, 1)

            dve.wait_ge(s.par_done, 1)
            dve.tensor_copy(vec[:, :], ps[:, 2, 0:44])
            dve.tensor_copy(dw[:], ps[:, 2, 64:64 + KC * CW].rearrange("p (k w) -> p k w", w=CW))
            dve.tensor_copy(bias_h[:, :], ps[:, 2, 192:200]).then_inc(s.par_read, 1)

            def rest_of_h(k, g, first):
                dve.wait_ge(s.norm_h, first + k + 1)
                dve.scalar_tensor_tensor(out=hL[:, k], in0=xT[:, k], scalar=gain(g, k), in1=hH[:, k],
                                         op0=ALU.mult, op1=ALU.subtract).then_inc(s.norm_l, 1)

            dve.wait_ge(s.xt_done, 1)
            dve.tensor_copy(xT[:, :, S:T], ps[:, 3, 0:KD * NS].rearrange("p (k t) -> p k t", t=NS)).then_inc(s.x_copied, 1)
            dve.wait_ge(s.par_read, 1)
            for k in range(KD + 1):
                if k < KD:
                    dve.wait_ge(s.xt_done, k + 2)
                    dve.tensor_copy(xT[:, k, 0:S], ps[:, 6 + k % 2, :]).then_inc(s.x_copied, 1)
                if k >= 1:
                    rest_of_h(k - 1, 0, 0)
                if k == KD // 2:
                    split_lo(0)

            def reciprocal(a, need):
                dve.wait_ge(s.std_ready, need)
                dve.reciprocal(a[:, :], a[:, :]).then_inc(s.dve_step, step.up())
                dve.wait_ge(s.dve_step, step.n)

            reciprocal(rstd, 1)
            dve.tensor_tensor(bias_own[:, :], bias_h[:, :], headmask, ALU.mult).then_inc(s.dve_step, step.up())
            dve.wait_ge(s.dve_step, step.n)
            dve.tensor_reduce(bias_r[:, :], bias_own[:, :], AX.X, ALU.add).then_inc(s.bias_ready, 1)
            dve.wait_ge(s.st_done, GROUPS)
            for g in range(GROUPS):
                for k in range(KC):
                    last = dve.tensor_copy(uS[:, k, GB * g:GB * g + GB, 0:HIST],
                                           ps[:, 6 + g, GB * HIST * k:GB * HIST * (k + 1)].rearrange("p (b r) -> p b r", r=HIST))
                last.then_inc(s.st_read, 1)

            def sample_conv(ct):
                if ct:
                    dve.wait_ge(s.sconv_done, ct)
                for t in range(NT):
                    last = dve.tensor_tensor(prod[:, t], uS[:, ct, :, t:t + CW],
                                             dw[:, ct].unsqueeze(1).to_broadcast([P, NB, CW]), ALU.mult)
                last.then_inc(s.dve_step, step.up())
                dve.wait_ge(s.dve_step, step.n)
                y = yc[:, ct, S:T].rearrange("p (b t) -> p t b", t=NT)
                dve.tensor_reduce(y, prod[:], AX.X, ALU.add).then_inc(s.dve_step, step.up())
                dve.wait_ge(s.dve_step, step.n)
                dve.tensor_scalar(yc[:, ct, S:T], yc[:, ct, S:T], cvec(0, ct), None, ALU.add).then_inc(s.sconv_done, 1)

            conv_at = 0

            def prompt_conv(upto):
                nonlocal conv_at
                while conv_at < min(upto, 2 * CW):
                    w, ct = conv_at // 2, conv_at % 2
                    y, u = yc[:, ct, 0:S], uP[:, ct, w:w + S]
                    if w == 0:
                        dve.tensor_scalar(y, u, dw[:, ct, 0:1], cvec(0, ct), ALU.mult, ALU.add).then_inc(s.dve_step, step.up())
                    else:
                        dve.wait_ge(s.dve_step, step.n - 1 if conv_at < 2 * CW - 1 else step.n)
                        ins = dve.scalar_tensor_tensor(out=y, in0=u, scalar=dw[:, ct, w:w + 1], in1=y, op0=ALU.mult, op1=ALU.add)
                        if w < CW - 1:
                            ins.then_inc(s.dve_step, step.up())
                        else:
                            ins.then_inc(s.dconv_done, 1)
                    conv_at += 1

            for n in range(U_MERGE):
                if n + 1 < U_MERGE:
                    split_lo(n + 1)
                for m in range(MT):
                    a = acc(m)
                    if n not in (1, 3):
                        if n in (2, 4):
                            dve.wait_ge(acc_read[m], n)
                        if n == 5:
                            dve.wait_ge(s.q_copied, m + 1)
                        out = (sig_u[:, m] if n < 6 else kT[:, 2 * (n - 6) + m] if n < 8 else vT[:, 2 * (n - 8) + m])
                        dve.wait_ge(acc_done[m], n + 1)
                        dve.tensor_tensor(halves(out), a, halves(rstd[:]), ALU.mult).then_inc(acc_read[m], 1)
                    else:
                        ct = 2 * (n // 2) + m
                        if n == 1 and m == 0:
                            dve.wait_ge(s.zeroed, 5)
                            dve.wait_ge(s.st_read, GROUPS)
                        dve.wait_ge(s.sig_ready, n + m)
                        dve.tensor_tensor(sig_u[:, m], sig_u[:, m], rstd[:, :], ALU.mult).then_inc(s.dve_step, step.up())
                        dve.wait_ge(acc_done[m], n + 1)
                        dve.wait_ge(s.dve_step, step.n)
                        dve.tensor_tensor(uP[:, ct, HIST:HIST + HT], a[:, 0, :], sig_u[:, m, 0:HT], ALU.mult)
                        dve.tensor_tensor(uP[:, ct, HIST + HT:HIST + S], a[:, 1, 0:S1], sig_u[:, m, HT:S], ALU.mult)
                        dve.tensor_tensor(uS[:, ct, :, HIST:HIST + NT], a[:, 1, S1:HT].rearrange("p (b t) -> p b t", t=NT),
                                          sig_u[:, m, S:T].rearrange("p (b t) -> p b t", t=NT), ALU.mult)
                        dve.tensor_tensor(u_new[:, ct], a[:, 1, S1:HT], sig_u[:, m, S:T], ALU.mult).then_inc(acc_read[m], 1)
                if n >= 2:
                    if n == 2:
                        for m in range(MT):
                            dve.wait_ge(acc_read[m], 2)
                    if n == 4:
                        for m in range(MT):
                            dve.wait_ge(acc_read[m], 4)
                    if 4 <= n < 8:
                        sample_conv(n - 4)
                    prompt_conv(9 * (n - 1))
            dve.wait_ge(s.zeroed, 5)
            for k in range(KC):
                dve.wait_ge(s.vt_done, k + 1)
                dve.tensor_copy(v_tok[:, :, P * k:P * k + P], ps[:, 4, :].rearrange("p (j c) -> p j c", c=P)).then_inc(s.vt_read, 1)
            dve.wait_ge(s.vt_done, KC + 1)
            dve.tensor_copy(vs_tok[0:NS, :], ps[0:NS, 6, :]).then_inc(s.vt_read, 1)
            dve.wait_ge(s.cout_done, 1)
            dve.tensor_copy(conv_tail[:, :], ps[0:HIST, 0, :]).then_inc(s.cout_read, 1)
            dve.tensor_copy(conv_new[:, :], ps[0:NS, 1, :]).then_inc(s.cout_read, 1)

            def stick(beta, left, width, out_sem):
                dve.tensor_scalar(left[:, 0:width], beta, -1.0, 1.0, ALU.mult, ALU.add).then_inc(s.dve_step, step.up())
                dve.wait_ge(s.dve_step, step.n)
                back = left[:, 0:width][:, ::-1]
                dve.tensor_tensor_scan(back, back, back, 1.0, ALU.mult, ALU.min).then_inc(s.dve_step, step.up())
                dve.wait_ge(s.dve_step, step.n)
                dve.tensor_tensor(beta, beta, left[:, 1:width + 1], ALU.mult).then_inc(out_sem, 1)

            for st in STEPS:
                what, a = st[0], st[1:]
                if what == "ZN":
                    g, = a
                    dve.wait_ge(s.z_read, 4 * g + 3)
                    if g == 0:
                        dve.memset(stick_s[:, LS:LS + 1], 1.0)
                        dve.memset(wgtT_s[:, PAGES], 0.0)
                    dve.tensor_tensor(beta_s[:, PAST:LS], beta_s[:, PAST:LS], newmask(g), ALU.mult).then_inc(s.dve_step, step.up())
                    dve.wait_ge(s.dve_step, step.n)
                    stick(beta_s[:, :], stick_s, LS, s.weight_s)
                elif what == "PN":
                    g, = a
                    dve.wait_ge(s.own_done, g + 1)
                    dve.tensor_tensor(own_s[:, :].rearrange("p (h d) -> p h d", d=DH), ps[:, 4, :].rearrange("p (h d) -> p h d", d=DH),
                                      headmask.unsqueeze(2).to_broadcast([P, H, DH]), ALU.mult).then_inc(s.own_ready, 1)
                elif what == "SO":
                    g, = a
                    cols = slice(S + GB * NT * g, S + GB * NT * (g + 1))
                    dve.wait_ge(s.attT_hi, g + 1)
                    dve.tensor_tensor(acL[:, 0:KC, cols], ps[:, 4, 0:KC * GB * NT].rearrange("p (k c) -> p k c", k=KC),
                                      acH[:, 0:KC, cols], ALU.subtract).then_inc(s.z_read, 1)
                elif what == "PS":
                    h, part_ = a
                    for i in (2 * part_, 2 * part_ + 1):
                        dve.wait_ge(s.pscore_read, 4 * h + i + 1)
                        left = stick_p[i % 2][:, S - WID[i]:S + 1]
                        if h == 0 and i < 2:
                            dve.memset(left[:, WID[i]:], 1.0)
                        beta = beta_p[:, h % 2, POS[i]:POS[i] + WID[i]]
                        diag = beta[:, P * i:P * i + P]
                        dve.tensor_tensor(diag, diag, tri, ALU.mult).then_inc(s.dve_step, step.up())
                        dve.wait_ge(s.dve_step, step.n)
                        if 4 * h + i >= 2:
                            dve.wait_ge(s.pweight, 4 * h + i - 1)
                        stick(beta, left, WID[i], s.pweight)
                elif what == "PO" and a[0] % 2:
                    h, = a
                    dve.wait_ge(s.pv_hi, h // 2 + 1)
                    dve.tensor_tensor(acL[:, h // 2, 0:S], ps[:, 5, :], acH[:, h // 2, 0:S], ALU.subtract).then_inc(s.pv_read, 1)
                elif what == "MW":
                    split_lo(U_MERGE + a[0])
                elif what == "LS":
                    dve.wait_ge(s.ln_sum, 1)
                    for k in range(KC):
                        dve.scalar_tensor_tensor(out=halves(yc[:, k]), in0=ps[:, 6:8, 0:HT], scalar=-1.0 / C, in1=halves(yc[:, k]),
                                                 op0=ALU.mult, op1=ALU.add).then_inc(s.ln_cent, 1)
                elif what == "LQ":
                    reciprocal(std1, 2)
                elif what == "LY":
                    for k in range(KC + 1):
                        if k < KC:
                            if k >= 2:
                                dve.wait_ge(s.ln_lo, k - 1)
                            dve.scalar_tensor_tensor(out=tmp1[:, k % 2], in0=yc[:, k], scalar=cvec(1, k), in1=std1[:, :],
                                                     op0=ALU.mult, op1=ALU.mult).then_inc(s.ln_t, 1)
                        if k >= 1:
                            t = tmp1[:, (k - 1) % 2]
                            dve.wait_ge(s.ln_sig, k)
                            dve.scalar_tensor_tensor(out=t, in0=t, scalar=cvec(2, k - 1), in1=sig1[:, (k - 1) % 2],
                                                     op0=ALU.add, op1=ALU.mult).then_inc(s.ln_y, 1)
                            dve.wait_ge(s.ln_hi, k)
                            dve.tensor_tensor(acL[:, KC + k - 1], t, acH[:, KC + k - 1], ALU.subtract).then_inc(s.ln_lo, 1)
            for mp in range(D // UC):
                for j in range(3):
                    if mp or j:
                        split_lo(U_MERGE + 3 * mp + j + 1)
                    for m in range(MT if j < 2 else 0):
                        c = A_MERGE + 8 * mp + 2 * j + m
                        dve.wait_ge(acc_done[m], c // 2 + 1)
                        dve.tensor_tensor(halves((sig_c, sig_a)[j][:, m]), acc(m), halves(rstd[:]), ALU.mult).then_inc(acc_read[m], 1)
                c0 = A_MERGE + 8 * mp + 4
                if mp:
                    dve.wait_ge(s.merged_lo, 2 * mp)
                dve.wait_ge(s.gates_ready, 4 * (mp + 1))
                for m in range(MT):
                    dve.wait_ge(acc_done[m], c0 // 2 + 1)
                    dve.tensor_tensor(halves(part[:, m]), acc(m), halves(sig_c[:, m]), ALU.mult).then_inc(acc_read[m], 1)
                for m in range(MT):
                    dve.wait_ge(acc_done[m], c0 // 2 + 2)
                    dve.tensor_tensor(halves(both[:, m]), acc(m), halves(sig_a[:, m]), ALU.mult).then_inc(acc_read[m], 1)
                for m in range(MT):
                    dve.wait_ge(acc_read[m], c0 // 2 + 2)
                    dve.tensor_tensor(both[:, m], both[:, m], part[:, m], ALU.add).then_inc(s.merged_t, 1)
                for m in range(MT):
                    dve.wait_ge(s.merged_hi, 2 * mp + m + 1)
                    dve.tensor_tensor(mL[:, 2 * mp + m], both[:, m], mH[:, 2 * mp + m], ALU.subtract).then_inc(s.merged_lo, 1)

            def add_squares(t, first):
                if t == 0:
                    dve.tensor_copy(ssum[:, :], sq2[:, 0]).then_inc(s.wo_sum, 1)
                else:
                    dve.wait_ge(s.wo_sum, first + t)
                    dve.tensor_tensor(ssum[:, :], ssum[:, :], sq2[:, t % 2], ALU.add).then_inc(s.wo_sum, 1)

            for j in range(D // UC):
                split_lo(U_WO + j + 1)
                for m in range(MT):
                    dve.wait_ge(s.out_sq, 2 * j + m + 1)
                    add_squares(2 * j + m, 0)
            reciprocal(std2, 3)

            for k in range(KD + 1):
                if k < KD:
                    if k >= 2:
                        dve.wait_ge(s.x1_ready, k - 1)
                    dve.scalar_tensor_tensor(out=tmp2[:, k % 2], in0=pout[:, k], scalar=gain(1, k), in1=std2[:, :],
                                             op0=ALU.mult, op1=ALU.mult).then_inc(s.mix_ready, 1)
                if k >= 1:
                    rest_of_h(k - 1, 2, KD)
            reciprocal(rstd, 4)
            with dve.Fori(0, FF // UC) as i:
                for j in range(2):
                    n1 = U_FFI + j + 1
                    dve.wait_ge(s.hi_done, i * 2 + (n1 + 1))
                    dve.tensor_tensor(w_lo[:, n1 % 2], w_raw[:, n1 % 2], w_hi[:, n1 % 2], ALU.subtract).then_inc(s.split_done, 1)
                    for m in range(MT):
                        if j == 0:
                            dve.wait_ge(acc_done[m], i * 2 + (A_FFI // 2 + 1))
                            dve.tensor_tensor(halves(gate_f[:, m]), acc(m), halves(rstd[:]), ALU.mult).then_inc(acc_read[m], 1)
                        else:
                            dve.wait_ge(s.silu_scaled, i * 2 + (m + 1))
                            dve.wait_ge(acc_done[m], i * 2 + (A_FFI // 2 + 2))
                            dve.tensor_tensor(halves(sig_f[:, m]), acc(m), halves(sig_f[:, m]), ALU.mult).then_inc(acc_read[m], 1)
                for m in range(MT):
                    dve.wait_ge(s.act_hi, i * 2 + (m + 1))
                    dve.tensor_tensor(actL[:, bass.ds(i * 2 + m, 1), :], sig_f[:, m:m + 1], actH[:, bass.ds(i * 2 + m, 1), :],
                                      ALU.subtract).then_inc(s.act_lo, 1)
            for mp in range(D // UC):
                for j in range(3):
                    n = U_FFO + 3 * mp + j
                    if n + 1 < U_FFO + 12:
                        split_lo(n + 1)
                for m in range(MT):
                    t = 2 * mp + m
                    dve.wait_ge(s.out_sq, KD + t + 1)
                    add_squares(t, KD)
            reciprocal(std2, 5)
            for k in range(KD + 1):
                if k < KD:
                    dve.scalar_tensor_tensor(out=pout[:, k], in0=pout[:, k], scalar=gain(3, k), in1=std2[:, :],
                                                       op0=ALU.mult, op1=ALU.mult).then_inc(s.dve_step, step.up())
                if k >= 1:
                    dve.wait_ge(s.dve_step, step.n - (1 if k < KD else 0))
                    dve.tensor_tensor(pout[:, k - 1], pout[:, k - 1], xT[:, k - 1], ALU.add).then_inc(s.y_ready, 1)

        @block.gpsimd
        def _(pool):
            for n, zero in enumerate((q_even[64:128], q_odd[0:64], q_s[:], vs_tok[:], uP[:, :, 0:HIST])):
                if n:
                    pool.wait_ge(s.zeroed, n)
                pool.memset(zero, 0.0).then_inc(s.zeroed, 1)
            tap = Count()
            for ct in range(2, KC):
                pool.wait_ge(acc_read[ct % 2], 2 * (ct // 2) + 2)
                y = yc[:, ct, 0:S]
                pool.tensor_scalar(y, uP[:, ct, 0:S], dw[:, ct, 0:1], cvec(0, ct), ALU.mult, ALU.add).then_inc(s.conv_tap, tap.up())
                for w in range(1, CW):
                    product = tap_prod[:, w % 2]
                    pool.tensor_scalar(product, uP[:, ct, w:w + S], dw[:, ct, w:w + 1], None, ALU.mult).then_inc(s.conv_tap, tap.up())
                    pool.wait_ge(s.conv_tap, tap.n)
                    if w < CW - 1:
                        pool.tensor_tensor(y, y, product, ALU.add).then_inc(s.conv_tap, tap.up())
                    else:
                        pool.tensor_tensor(y, y, product, ALU.add).then_inc(s.conv_done, 1)
            for k in range(KD):
                pool.wait_ge(s.mix_ready, k + 1)
                pool.tensor_tensor(xT[:, k], xT[:, k], tmp2[:, k % 2], ALU.add).then_inc(s.x1_ready, 1)
            with pool.Fori(0, FF // UC) as i:
                for m in range(MT):
                    pool.wait_ge(s.silu_ready, i * 2 + (m + 1))
                    pool.tensor_tensor(sig_f[:, m], sig_f[:, m], gate_f[:, m], ALU.mult).then_inc(s.silu_times, 1)
                for m in range(MT):
                    pool.wait_ge(s.silu_times, i * 2 + (m + 1))
                    pool.tensor_tensor(sig_f[:, m], sig_f[:, m], rstd[:, :], ALU.mult).then_inc(s.silu_scaled, 1)


_INS = ["x_prompt", "x_sample", "cache_k", "cache_v", "state_conv", "page_table", "norm_pre_mix", "norm_post_mix",
        "norm_pre_ffn", "norm_post_ffn", "w_in", "conv_dw", "conv_b", "conv_ln_g", "conv_ln_b", "w_conv_out",
        "att_bias", "w_att_out", "w_o", "w_ffn_in", "w_ffn_out"]
_OUTS = [(1, S, D), (NB, NT, D), (1, 1, S, H, DH), (1, 1, S, H, DH), (1, 1, HIST, C), (1, NB, NT, H, DH),
         (1, NB, NT, H, DH), (1, NB, HIST, C)]


def kernel(**inputs):
    import concourse.bacc as bacc
    from concourse.bass_utils import run_bass_kernel_spmd

    nc = bacc.Bacc("TRN2", target_bir_lowering=False, num_devices=1)
    arrays, args = {}, []
    for name in _INS + ["consts"]:
        a = constants() if name == "consts" else np.ascontiguousarray(inputs[name])
        arrays[f"in_{name}"] = a
        args.append(nc.dram_tensor(f"in_{name}", a.shape, mybir.dt.from_np(a.dtype), kind="ExternalInput").ap())
    for i, shape in enumerate(_OUTS):
        args.append(nc.dram_tensor(f"out_{i}", shape, F32, kind="ExternalOutput").ap())
    layer_kernel(nc, *args)
    r = run_bass_kernel_spmd(nc, [arrays], core_ids=[0])
    return tuple(r.results[0][f"out_{i}"] for i in range(len(_OUTS)))
```

```python
from contextlib import ExitStack

import numpy as np

import concourse.bass as bass
from concourse import mybir

F32 = mybir.dt.float32
F32R = mybir.dt.float32r
I32 = mybir.dt.int32
ALU = mybir.AluOpType
ACT = mybir.ActivationFunctionType
AX = mybir.AxisListType

P = 128
D = 1024
S = 512
NB, NT = 8, 4
NS = NB * NT
T = S + NS
HT = T // 2
S1 = S - HT
H, DH = 8, 64
C = 512
CW = 31
HIST = CW - 1
PAGES, PAGE = 8, 128
PAST = PAGES * PAGE
FF = 2816
KD, KC, KF = D // P, C // P, FF // P
EPS = 1e-6
SCALE = DH ** -0.5
UC = 256
UK = 8
MT = UC // P
RING = 2
GB = 4
GROUPS = NB // GB

COL_GLU_A, COL_GLU_B, COL_Q, COL_K, COL_V, COL_GC, COL_GA = 0, 512, 1024, 1536, 2048, 2560, 3584
FIRST_UNITS = [COL_GLU_B, COL_GLU_A, COL_GLU_B + UC, COL_GLU_A + UC, COL_Q, COL_Q + UC,
               COL_K, COL_K + UC, COL_V, COL_V + UC]
U_MERGE, U_WO, U_FFI, U_FFO = 10, 22, 26, 48
A_MERGE, A_WO, A_FFI = 20, 52, 60

K_ID, K_TRI, K_ONE, K_NEW, K_SEL, K_HEAD, K_EPS = 0, 128, 256, 384, 448, 464, 472
K_COLS = 473


def constants():
    c = np.zeros((P, K_COLS), np.float32)
    r = np.arange(P)
    b, h, q = r // 32, r // NT % H, r % NT
    c[:, K_ID:K_ID + P] = np.eye(P)
    c[:, K_TRI:K_TRI + P] = r[None, :] < r[:, None]
    c[:, K_ONE:K_ONE + P] = 1.0
    n = np.arange(NS)
    for g in range(GROUPS):
        c[:, K_NEW + NS * g:K_NEW + NS * (g + 1)] = (n[None] // NT == GB * g + b[:, None]) & (n[None] % NT < q[:, None])
    m = np.arange(GB * NT)
    c[:, K_SEL:K_SEL + GB * NT] = (m[None] // NT == b[:, None]) & (m[None] % NT == q[:, None])
    c[:, K_HEAD:K_HEAD + H] = np.arange(H)[None] == h[:, None]
    c[:, K_EPS] = EPS
    return c


def attention_steps():
    prompt = [("PS", 0, 0), ("PS", 0, 1)]
    for h in range(H):
        if h + 1 < H:
            prompt += [("PS", h + 1, 0), ("PS", h + 1, 1)]
        prompt += [("PT", h, 0), ("PT", h, 1), ("PO", h)]
    prompt = iter(prompt)
    steps = []

    def pieces(n):
        for _ in range(n):
            steps.extend([next(prompt)])

    for g in range(GROUPS):
        for j in range(PAGES):
            steps.append(("KT", g, j))
            if g and j == 0:
                steps.append(("SO", g - 1))
            if j:
                steps.append(("SC", g, j - 1))
            pieces((0, 1, 0, 1, 0, 1, 0, 1)[j])
        steps += [("SC", g, PAGES - 1), ("ZN", g)]
        pieces(4)
        steps.append(("AT", g))
        for j in range(PAGES):
            steps.append(("PV", g, j))
            if g < GROUPS - 1 or j < PAGES - 1:
                pieces((3, 2, 1, 2, 1, 1, 1, 1)[j])
        if g == GROUPS - 1:
            steps += [("LS",), ("MW", 0)]
            pieces(1)
        steps += [("PN", g)]
    assert next(prompt, None) is None
    steps += [("LQ",), ("SO", GROUPS - 1), ("MW", 1)]
    for k in range(KC + 1):
        steps.append(("LY", k))
        if k in (0, 2):
            steps.append(("MG", k // 2))
    return steps


def tail_steps():
    slots = [[("x", n)] if n < KD else [] for n in range(3 * D // P)]
    for t in range(KD):
        slots[min(6 * (t // 2) + 5 + t % 2, len(slots) - 1)].append(("o", t))
    return slots


class Semaphores:

    def __init__(self, new):
        self.ld_const = new("ld_const")
        self.ld_par = new("ld_par")
        self.ld_x0 = new("ld_x0")
        self.ld_x1 = new("ld_x1")
        self.ld_state = new("ld_state")
        self.ld_table = new("ld_table")
        self.stored = new("stored")
        self.kv_stored = new("kv_stored")
        self.k_stored = new("k_stored")
        self.hi_done = new("hi_done")
        self.split_done = new("split_done")
        self.unit_used = new("unit_used")
        self.par_done = new("par_done")
        self.par_read = new("par_read")
        self.bias_ready = new("bias_ready")
        self.st_done = new("st_done")
        self.st_read = new("st_read")
        self.xt_done = new("xt_done")
        self.x_copied = new("x_copied")
        self.sq_ready = new("sq_ready")
        self.sq_added = new("sq_added")
        self.y_added = new("y_added")
        self.ssq_done = new("ssq_done")
        self.std_ready = new("std_ready")
        self.sig_ready = new("sig_ready")
        self.q_copied = new("q_copied")
        self.gates_ready = new("gates_ready")
        self.mix_ready = new("mix_ready")
        self.silu_times = new("silu_times")
        self.silu_scaled = new("silu_scaled")
        self.norm_h = new("norm_h")
        self.norm_l = new("norm_l")
        self.zeroed = new("zeroed")
        self.sconv_done = new("sconv_done")
        self.conv_done = new("conv_done")
        self.dconv_done = new("dconv_done")
        self.conv_tap = new("conv_tap")
        self.vt_done = new("vt_done")
        self.vt_read = new("vt_read")
        self.ktok_done = new("ktok_done")
        self.ktok_read = new("ktok_read")
        self.cout_done = new("cout_done")
        self.cout_read = new("cout_read")
        self.page_used = new("page_used")
        self.kt_done = new("kt_done")
        self.score_done = new("score_done")
        self.z_read = new("z_read")
        self.weight_s = new("weight_s")
        self.own_done = new("own_done")
        self.own_ready = new("own_ready")
        self.attT_done = new("attT_done")
        self.attT_hi = new("attT_hi")
        self.pscore_done = new("pscore_done")
        self.pscore_read = new("pscore_read")
        self.pweight = new("pweight")
        self.ptr_done = new("ptr_done")
        self.ptr_read = new("ptr_read")
        self.pv_done = new("pv_done")
        self.pv_hi = new("pv_hi")
        self.pv_read = new("pv_read")
        self.ln_sum = new("ln_sum")
        self.ln_cent = new("ln_cent")
        self.ln_sq = new("ln_sq")
        self.ln_sqsum = new("ln_sqsum")
        self.ln_t = new("ln_t")
        self.ln_sig = new("ln_sig")
        self.ln_y = new("ln_y")
        self.ln_hi = new("ln_hi")
        self.ln_lo = new("ln_lo")
        self.dve_step = new("dve_step")
        self.merged_t = new("merged_t")
        self.merged_hi = new("merged_hi")
        self.merged_lo = new("merged_lo")
        self.out_sq = new("out_sq")
        self.wo_sum = new("wo_sum")
        self.silu_ready = new("silu_ready")
        self.act_hi = new("act_hi")
        self.act_lo = new("act_lo")
        self.x1_ready = new("x1_ready")
        self.sq_ready2 = new("sq_ready2")
        self.out_acc_done = new("out_acc_done")
        self.out_acc_read = new("out_acc_read")
        self.y_ready = new("y_ready")
        self.yt_done = new("yt_done")
        self.yt_read = new("yt_read")
        self.raw_loaded = [new("raw_loaded0"), new("raw_loaded1")]
        self.pages_loaded = [new("pages_loaded0"), new("pages_loaded1")]
        self.acc_done = [new("acc_done0"), new("acc_done1")]
        self.acc_read = [new("acc_read0"), new("acc_read1")]
        self.kt_read = [new("kt_read0"), new("kt_read1")]


class Count:

    def __init__(self):
        self.n = 0

    def up(self):
        self.n = self.n + 1
        return 1


def layer_kernel(nc, x_prompt, x_sample, cache_k, cache_v, state_conv, page_table, g_pre_mix, g_post_mix,
                 g_pre_ffn, g_post_ffn, w_in, conv_dw, conv_b, conv_ln_g, conv_ln_b, w_conv_out, att_bias,
                 w_att_out, w_o, w_ffn_in, w_ffn_out, consts,
                 y_prompt, y_sample, k_prompt, v_prompt, conv_prompt, k_sample, v_sample, conv_sample):
    n_phys = cache_k.shape[1]
    rows = lambda w: w[0].rearrange("(k p) c -> p k c", p=P)
    win_v, wconv_v, watt_v, wo_v, wfi_v, wfo_v = map(rows, (w_in, w_conv_out, w_att_out, w_o, w_ffn_in, w_ffn_out))
    STEPS, TAIL = attention_steps(), tail_steps()
    tail_order = sum(TAIL, [])

    with ExitStack() as ctx:
        arena_bytes = 212768
        arena = ctx.enter_context(nc.sbuf_tensor("arena", [P, arena_bytes // 4], F32))
        base = nc.sbuf_base - arena_bytes

        def at(name, shape, dt, offset):
            size = 4 * int(np.prod(shape[1:]))
            assert offset % 32 == 0 and offset + size <= arena_bytes, (name, offset, size)
            return nc.alloc_sbuf_tensor_at(name, shape, dt, offset=base + offset)

        kc = at("consts", [P, K_COLS], F32, 0)
        vec = at("vec", [P, 44], F32, 1920)
        dw = at("dw", [P, KC, CW], F32, 2112)
        bias_h = at("bias_h", [P, H], F32, 2624)
        bias_r = at("bias_r", [P, 1], F32, 2656)
        ptab = at("ptab", [1, NB * PAGES], I32, 2688)
        O = 2944
        ident, tri, ones = kc[:, K_ID:K_ID + P], kc[:, K_TRI:K_TRI + P], kc[:, K_ONE:K_ONE + P]
        newmask = lambda g: kc[:, K_NEW + NS * g:K_NEW + NS * (g + 1)]
        selq, headmask, eps = kc[:, K_SEL:K_SEL + GB * NT], kc[:, K_HEAD:K_HEAD + H], kc[:, K_EPS:K_EPS + 1]
        gain = lambda n, k: vec[:, 8 * n + k:8 * n + k + 1]
        cvec = lambda n, k: vec[:, 32 + KC * n + k:33 + KC * n + k]

        TB = 4 * T
        xT = at("xT", [P, KD, T], F32, O)
        hH = at("hH", [P, KD, T], F32R, O + KD * TB)
        hL = at("hL", [P, KD, T], F32R, O + 2 * KD * TB)
        pout = at("pout", [P, KD, T], F32, O + KD * TB)
        W0 = O + 3 * KD * TB
        w_raw = at("w_raw", [P, RING, UK, UC], F32, W0)
        w_hi = at("w_hi", [P, RING, UK, UC], F32R, W0 + 16384)
        w_lo = at("w_lo", [P, RING, UK, UC], F32R, W0 + 32768)
        pages = at("pages", [P, RING, GB, C], F32, W0)
        keysT = at("keysT", [P, RING, GB, KC, P], F32, W0 + 16384)
        LS = PAST + NS
        beta_s = at("beta_s", [P, LS], F32, W0 + 32768)
        stick_s = at("stick_s", [P, LS + 1], F32, W0 + 36992)
        wgtT_s = at("wgtT_s", [P, PAGES + 1, P], F32, W0 + 41248)
        own_s = at("own_s", [P, C], F32, W0 + 45856)
        B = W0 + 49152
        acH = at("acH", [P, 2 * KC, T], F32R, B)
        acL = at("acL", [P, 2 * KC, T], F32R, B + 17408)
        yc = at("yc", [P, KC, T], F32, B + 17408 + KC * TB)
        q_even = at("q_even", [P, KC, S], F32, B + 34816)
        q_odd = at("q_odd", [P, KC, S], F32, B + 43008)
        q_s = at("q_s", [P, NB, KC, H, NT], F32, B + 51200)
        kT = at("kT", [P, KC, T], F32, B + 55296)
        vT = at("vT", [P, KC, T], F32, B + 64000)
        k_tok = at("k_tok", [P, S // P, C], F32, B + 72704)
        ks_tok = at("ks_tok", [NS, C], F32, B + 80896)
        v_tok = at("v_tok", [P, S // P, C], F32, B + 82944)
        vs_tok = at("vs_tok", [P, C], F32, B + 91136)
        uP = at("uP", [P, KC, HIST + S], F32, B + 93184)
        uS = at("uS", [P, KC, NB, HIST + NT], F32, B + 101856)
        rstd = at("rstd", [P, T], F32, B + 106208)
        early = at("early", [P, 9], F32, B + 108384)
        x_tok = at("x_tok", [P, S // P, D], F32, B)
        xs_tok = at("xs_tok", [NS, D], F32, B + 16384)
        st_tok = at("st_tok", [GB * HIST, GROUPS, C], F32, B + 20480)
        par = at("par", [36, P], F32, B + 24576)
        par0 = at("par0", [8, P], F32, B + 27168)
        dw_tok = at("dw_tok", [CW, C], F32, B + 25088)
        ab_tok = at("ab_tok", [1, H], F32, B + 27136)
        sq0 = at("sq0", [P, RING, T], F32, B + 55296)
        bias_own = at("bias_own", [P, H], F32, B + 59648)
        ssum0 = at("ssum0", [P, T], F32, B + 59680)
        sig_u = at("sig_u", [P, MT, T], F32, B + 72704)
        prod = at("prod", [P, NT, NB, CW], F32, B + 72704 + 4352)
        u_new = at("u_new", [P, KC, NS], F32, B + 72704 + 8320)
        conv_tail = at("conv_tail", [HIST, C], F32, B + 8704)
        conv_new = at("conv_new", [NS, C], F32, B + 10752)
        tap_prod = at("tap_prod", [P, 2, S], F32, B + 12800)
        WID = [P * (i + 1) for i in range(S // P)]
        POS = [sum(WID[:i]) for i in range(S // P)]
        FILLS = ((0,), (1, 3), (2,))
        fills = lambda part_: (0, 1) if part_ == 0 else (2,)
        beta_p = at("beta_p", [P, 2, sum(WID)], F32, B + 64000)
        wgtT_p = at("wgtT_p", [P, sum(WID)], F32, B + 74240)
        stick_p = [at("stick_p0", [P, S + 4], F32, B + 79360), at("stick_p1", [P, S + 4], F32, B + 104064)]
        sq1 = at("sq1", [P, KC, T], F32, B + 93184)
        sig1 = at("sig1", [P, RING, T], F32, B + 93184)
        tmp1 = at("tmp1", [P, RING, T], F32, B + 97536)
        ysum = at("ysum", [P, T], F32, B + 101888)
        std1 = at("std1", [P, T], F32, B + 101888)
        mH = at("mH", [P, KD, T], F32R, B + 34816)
        mL = at("mL", [P, KD, T], F32R, B + 52224)
        sig_c = at("sig_c", [P, MT, T], F32, B + 69632)
        sig_a = at("sig_a", [P, MT, T], F32, B + 73984)
        part = at("part", [P, MT, T], F32, B + 78336)
        both = at("both", [P, MT, T], F32, B + 82688)
        actH = at("actH", [P, KF, T], F32R, B)
        actL = at("actL", [P, KF, T], F32R, B + KF * TB)
        tmp2 = at("tmp2", [P, RING, T], F32, B + 87040)
        sig_f = at("sig_f", [P, MT, T], F32, B + 95744)
        gate_f = at("gate_f", [P, MT, T], F32, B + 100096)
        sq2 = at("sq2", [P, RING, T], F32, B + 95744)
        ssum = at("ssum", [P, T], F32, B + 100096)
        std2 = at("std2", [P, T], F32, B + 102272)
        NC = S // P
        o_tok = at("o_tok", [P, NC, D], F32, O + KD * TB)
        x1_tok = at("x1_tok", [P, NC, D], F32, O + 2 * KD * TB)
        o_fm = at("o_fm", [P, RING, T], F32, O)
        os_tok = at("os_tok", [NS, D], F32, O + 2 * TB)
        x1s_tok = at("x1s_tok", [NS, D], F32, B + 102272)
        r_tok = at("r_tok", [P, NC + 1], F32, B + 106368)

        ps = ctx.enter_context(nc.psum_tensor("ps", [P, 8, 512], F32))

        s = Semaphores(lambda name: ctx.enter_context(nc.semaphore(name)))
        raw_loaded, acc_done, acc_read, pages_loaded, kt_read = s.raw_loaded, s.acc_done, s.acc_read, s.pages_loaded, s.kt_read

        cache = (cache_k[0].rearrange("n r h d -> n r (h d)"), cache_v[0].rearrange("n r h d -> n r (h d)"))

        def keys_used(g, j, b):
            return GB * (PAGES * g + j) + b + 1 + 3 * g

        halves = lambda a: a.rearrange("p (h t) -> p h t", h=2)
        acc = lambda c: ps[:, 2 * (c % 2):2 * (c % 2) + 2, 0:HT]
        block = ctx.enter_context(nc.Block())

        @block.sync
        def _(sp):
            xp_v, xs_v = x_prompt[0].rearrange("(j p) d -> p j d", p=P), x_sample.rearrange("b t d -> (b t) d")

            def load_x(half):
                cols = slice(512 * half, 512 * half + 512)
                sp.dma_start(x_tok[:, :, cols], xp_v[:, :, cols]).then_inc((s.ld_x0, s.ld_x1)[half], 16)

            sp.dma_start(kc[:], consts).then_inc(s.ld_const, 16)
            sp.dma_start(par0[:], g_pre_mix[0].rearrange("(k p) -> k p", p=P)).then_inc(s.ld_x0, 16)
            sp.dma_start(xs_tok[:], xs_v).then_inc(s.ld_x0, 16)
            load_x(0)
            for n, g in enumerate((g_post_mix, g_pre_ffn, g_post_ffn)):
                sp.dma_start(par[8 * n:8 * n + 8, :], g[0].rearrange("(k p) -> k p", p=P)).then_inc(s.ld_par, 16)
            for n, g in enumerate((conv_b, conv_ln_g, conv_ln_b)):
                sp.dma_start(par[24 + KC * n:28 + KC * n, :], g[0].rearrange("(k p) -> k p", p=P)).then_inc(s.ld_par, 16)
            sp.dma_start(dw_tok[:], conv_dw[0]).then_inc(s.ld_par, 16)
            sp.dma_start(ab_tok[:], att_bias).then_inc(s.ld_par, 16)

            def load_unit(par_, lo, hi, need=None):
                if need is not None:
                    sp.wait_ge(s.split_done, need)
                sp.dma_start(w_raw[:, par_, 0:4], lo).then_inc(raw_loaded[par_], 16)
                sp.dma_start(w_raw[:, par_, 4:4 + hi.shape[1]], hi).then_inc(raw_loaded[par_], 16)

            def columns(v, c, k0=0, k1=UK):
                return v[:, k0:k0 + 4, bass.ds(c, UC)], v[:, k0 + 4:k1, bass.ds(c, UC)]

            load_unit(0, *columns(win_v, FIRST_UNITS[0]))
            load_x(1)
            sp.dma_start(st_tok[:], state_conv[0].rearrange("(g b) r c -> (b r) g c", g=GROUPS)).then_inc(s.ld_state, 16)
            sp.dma_start(ptab[:], page_table.rearrange("(o b) n -> o (b n)", o=1)).then_inc(s.ld_table, 16)
            load_unit(1, *columns(win_v, FIRST_UNITS[1]))
            sp.dma_start(conv_sample[0, :, 0:HIST - NT, :], state_conv[0, :, NT:HIST, :]).then_inc(s.stored, 16)
            for n in range(2, U_MERGE):
                load_unit(n % 2, *columns(win_v, FIRST_UNITS[n]), need=n - 1)

            sp.wait_ge(s.ld_table, 16)

            def load_pages(g, kv, j, slot, used=None, seqs=None):
                for b in seqs or range(GB - 1):
                    if used is not None and (b == 0 or kv == 0):
                        used(b)
                    page = sp.value_load(ptab[0:1, bass.ds((GB * g + b) * PAGES + j, 1)])
                    sp.dma_start(pages[:, slot, b, :], cache[kv][bass.ds(page, 1)].rearrange("n r c -> r (n c)"))\
                        .then_inc(pages_loaded[slot], 16)

            sp.wait_ge(s.split_done, U_MERGE)
            for slot in range(RING):
                load_pages(0, 0, slot, slot, seqs=range(GB))

            def small_stores():
                sp.wait_ge(s.vt_read, KC + 1)
                sp.dma_start(v_prompt[0, 0].rearrange("(j p) h d -> p j (h d)", p=P), v_tok[:]).then_inc(s.kv_stored, 16)
                sp.dma_start(v_sample[0].rearrange("b t h d -> (b t) (h d)"), vs_tok[0:NS, :]).then_inc(s.kv_stored, 16)
                sp.wait_ge(s.cout_read, 2)
                sp.dma_start(conv_prompt[0, 0], conv_tail[:]).then_inc(s.kv_stored, 16)
                for b in range(NB):
                    sp.dma_start(conv_sample[0, b, HIST - NT:HIST, :], conv_new[NT * b:NT * b + NT, :]).then_inc(s.kv_stored, 16)

            for g in range(GROUPS):
                for kv in range(2):
                    for slot in range(RING):
                        if kv or g:
                            if kv:
                                sp.wait_ge(s.kt_done, keys_used(g, PAGES - RING + slot, GB - 1))
                            else:
                                sp.wait_ge(s.page_used, PAGES * g - RING + slot + 1)
                            load_pages(g, kv, slot, slot)
                    if g == 0 and kv == 1:
                        small_stores()
                    with sp.Fori(1, PAGES // RING) as i:
                        for slot in range(RING):
                            if kv:
                                used = lambda b: sp.wait_ge(s.page_used, i * RING + (PAGES * g + slot - RING + 1))
                            else:
                                used = lambda b: sp.wait_ge(s.kt_done, i * (RING * GB) + keys_used(g, slot - RING, b))
                            load_pages(g, kv, i * RING + slot, slot, used)

            pages_left = {U_MERGE: GROUPS * PAGES - 1, U_MERGE + 1: GROUPS * PAGES}
            for mp in range(D // UC):
                for j in range(3):
                    n = U_MERGE + 3 * mp + j
                    if j < 2:
                        src = columns(win_v, (COL_GC, COL_GA)[j] + UC * mp)
                    else:
                        src = wconv_v[:, :, UC * mp:UC * mp + UC], watt_v[:, :, UC * mp:UC * mp + UC]
                    if n in pages_left:
                        sp.wait_ge(s.page_used, pages_left[n])
                    load_unit(n % 2, *src, need=n - 1)
            for m in range(D // UC):
                n = U_WO + m
                load_unit(n % 2, *columns(wo_v, UC * m), need=n - 1)
            with sp.Fori(0, FF // UC) as i:
                for j in range(2):
                    load_unit(j, *columns(wfi_v, i * UC + j * FF), need=i * 2 + (U_FFI + j - 1))
            for mp in range(D // UC):
                for j in range(3):
                    n = U_FFO + 3 * mp + j
                    load_unit(n % 2, *columns(wfo_v, UC * mp, 8 * j, min(8 * j + 8, KF)), need=n - 1)

            for c in range(NC):
                sp.wait_ge(s.y_ready, c + 1)
                sp.dma_start(y_prompt[0, P * c:P * c + P, :], o_tok[:, c]).then_inc(s.stored, 16)
            sp.wait_ge(s.y_ready, NC + 1)
            sp.dma_start(y_sample.rearrange("b t d -> (b t) d"), os_tok[:]).then_inc(s.stored, 16)
            sp.wait_ge(s.k_stored, 32)
            sp.wait_ge(s.kv_stored, 16 * (3 + NB))
            sp.wait_ge(s.stored, 16 * (NC + 2))

        @block.tensor
        def _(pe):
            def gemm_tile(slot, m, out, rh, rl, ks, start=True, stop=True):
                for n, (k, kk) in enumerate(ks):
                    cols = slice(P * m, P * m + P)
                    for q, (w, r) in enumerate(((w_hi, rh), (w_hi, rl), (w_lo, rh))):
                        for half in range(2):
                            last = pe.matmul(out[:, half], w[:, slot, k, cols], r[:, kk, HT * half:HT * half + HT],
                                             start=start and n == 0 and q == 0, stop=stop and n == len(ks) - 1 and q == 2)
                return last

            all_k = [(k, k) for k in range(UK)]

            def acc_tile(c_half, c, slot, m, rh, rl, ks=all_k, wait=True):
                if wait:
                    pe.wait_ge(acc_read[c % 2], c_half)
                gemm_tile(slot, m, acc(c), rh, rl, ks).then_inc(acc_done[c % 2], 1)

            def sum_squares(sq, k, bank=4, n=KD):
                for half in range(2):
                    last = pe.matmul(ps[:, bank + half, 0:HT], ones, sq[:, HT * half:HT * half + HT],
                                     start=(k == 0), stop=(k == n - 1))
                return last

            pe.wait_ge(s.ld_const, 16)
            pe.wait_ge(s.ld_x0, 48)
            for k in range(KD):
                pe.transpose(ps[:, 3, NS * k:NS * k + NS], xs_tok[:, P * k:P * k + P], ident[0:NS, 0:NS])
            last = pe.transpose(ps[:, 3, KD * NS:KD * NS + 8], par0[:, :], ident[0:8, 0:8])
            last.then_inc(s.xt_done, 1)
            for k in range(KD + 1):
                if k < KD:
                    if k == KD // 2:
                        pe.wait_ge(s.ld_x1, 16)
                    if k >= 2:
                        pe.wait_ge(s.x_copied, k)
                    for j in range(S // P):
                        last = pe.transpose(ps[:, 6 + k % 2, P * j:P * j + P], x_tok[:, j, P * k:P * k + P], ident)
                    last.then_inc(s.xt_done, 1)
                if k == 2:
                    pe.wait_ge(s.ld_par, 16 * 8)
                    pe.transpose(ps[:, 2, 8:44], par[:, :], ident[0:36, 0:36])
                    for n in range(KC):
                        pe.transpose(ps[:, 2, 64 + CW * n:64 + CW * n + CW], dw_tok[:, P * n:P * n + P], ident[0:CW, 0:CW])
                    pe.matmul(ps[:, 2, 192:200], ones[0:1, :], ab_tok[0:1, :], start=True, stop=True).then_inc(s.par_done, 1)
                if k > KD - 3:
                    if k == KD - 2:
                        pe.wait_ge(s.split_done, 1)
                    for kk in ((0, 1), (2, 3, 4), (5, 6, 7))[k - (KD - 2)]:
                        pe.wait_ge(s.norm_l, kk + 1)
                        last = gemm_tile(0, 0, acc(0), hH, hL, [(kk, kk)], start=(kk == 0), stop=(kk == KD - 1))
            last.then_inc(acc_done[0], 1)
            pe.wait_ge(s.sq_added, KD)
            sum_squares(ssum0[:, :], 0, n=1).then_inc(s.ssq_done, 1)
            pe.wait_ge(s.ld_state, 16)
            pe.wait_ge(s.x_copied, KD + 1)
            pe.wait_ge(s.par_read, 1)
            for g in range(GROUPS):
                for k in range(KC):
                    last = pe.transpose(ps[:, 6 + g, GB * HIST * k:GB * HIST * (k + 1)], st_tok[:, g, P * k:P * k + P],
                                        ident[0:GB * HIST, 0:GB * HIST])
                last.then_inc(s.st_done, 1)

            def in_pair(i, peeled):
                for j in range(2):
                    pe.wait_ge(s.split_done, i * 2 + (j + 1))
                    for m in range(MT):
                        t = 2 * j + m
                        if not peeled or t:
                            acc_tile(i * 2 + t // 2, t, j, m, hH, hL, wait=not peeled or t >= 2)

            in_pair(0, True)
            with pe.Fori(1, U_MERGE // 2) as i:
                in_pair(i, False)

            n_in = U_MERGE
            pe.wait_ge(acc_read[0], n_in)
            pe.wait_ge(acc_read[1], n_in)
            pe.wait_ge(s.st_read, GROUPS)
            for k in range(KC):
                pe.transpose(ps[0:HIST, 0, P * k:P * k + P], uP[:, k, S:S + HIST], ident)
                last = pe.transpose(ps[0:NS, 1, P * k:P * k + P], u_new[:, k], ident)
            last.then_inc(s.cout_done, 1)
            kinds = ((vT, 4, 6, s.vt_done, s.vt_read), (kT, 5, 7, s.ktok_done, s.ktok_read))
            for k in range(KC):
                for src, big, small, done, read in kinds:
                    if k:
                        pe.wait_ge(read, k)
                    for j in range(S // P):
                        last = pe.transpose(ps[:, big, P * j:P * j + P], src[:, k, P * j:P * j + P], ident)
                    last.then_inc(done, 1)
            for src, big, small, done, read in kinds:
                for k in range(KC):
                    last = pe.transpose(ps[0:NS, small, P * k:P * k + P], src[:, k, S:T], ident)
                last.then_inc(done, 1)

            pe.wait_ge(s.q_copied, H // 2)
            n_kt = n_z = n_ps = n_pt = 0

            def next_kt():
                nonlocal n_kt
                if n_kt >= 2:
                    pe.wait_ge(kt_read[n_kt % 2], n_kt // 2)
                n_kt += 1
                return 2 + (n_kt - 1) % 2

            for st in STEPS:
                what, a = st[0], st[1:]
                if what == "KT":
                    g, j = a
                    r = 2 * PAGES * g + j
                    pe.wait_ge(pages_loaded[r % 2], 16 * GB * (r // 2 + 1))
                    for b in range(GB):
                        bank = next_kt()
                        for k in range(KC):
                            last = pe.transpose(ps[:, bank, P * k:P * k + P], pages[:, r % 2, b, P * k:P * k + P], ident)
                        last.then_inc(s.kt_done, 1)
                elif what == "SC":
                    g, j = a
                    ks = PAGES * g + j
                    upto = 4 * (ks + 1) + 3 * g
                    if ks == 0:
                        pe.wait_ge(s.vt_read, KC)
                    pe.wait_ge(kt_read[0], (upto + 1) // 2)
                    pe.wait_ge(kt_read[1], upto // 2)
                    if j % 4 == 0 and n_z:
                        pe.wait_ge(s.z_read, n_z)
                    for k in range(KC):
                        for b in range(GB):
                            last = pe.matmul(ps[32 * b:32 * b + 32, 4, P * (j % 4):P * (j % 4) + P],
                                             q_s[:, GB * g + b, k], keysT[:, ks % 2, b, k], start=(k == 0),
                                             stop=(k == KC - 1), skip_group_check=True)
                    last.then_inc(s.score_done, 1)
                    if j % 4 == 3:
                        n_z += 1
                elif what == "ZN":
                    g, = a
                    pe.wait_ge(s.z_read, n_z)
                    for k in range(KC):
                        for b in range(GB):
                            last = pe.matmul(ps[32 * b:32 * b + 32, 4, 0:NS], q_s[:, GB * g + b, k], kT[:, k, S:T],
                                             start=(k == 0), stop=(k == KC - 1), skip_group_check=True)
                    last.then_inc(s.score_done, 1)
                    n_z += 1
                elif what == "AT":
                    g, = a
                    pe.wait_ge(s.weight_s, g + 1)
                    for blocks in (range(0, 4), range(4, 8), range(8, 9)):
                        bank = next_kt()
                        for n, j in enumerate(blocks):
                            w = P if j < PAGES else NS
                            last = pe.transpose(ps[0:w, bank, P * n:P * n + P], beta_s[:, P * j:P * j + w], ident)
                        last.then_inc(s.kt_done, 1)
                    pe.wait_ge(kt_read[0], (n_kt + 1) // 2)
                    pe.wait_ge(kt_read[1], n_kt // 2)
                    pe.wait_ge(s.z_read, n_z)
                elif what in ("PV", "PN"):
                    g = a[0]
                    j = a[1] if what == "PV" else PAGES
                    r = 2 * PAGES * g + PAGES + j
                    if what == "PV":
                        pe.wait_ge(pages_loaded[r % 2], 16 * GB * (r // 2 + 1))
                    for b in range(GB):
                        v = pages[:, r % 2, b, :] if what == "PV" else vs_tok[:, :]
                        last = pe.matmul(ps[32 * b:32 * b + 32, 4, :], wgtT_s[:, j, 32 * b:32 * b + 32], v,
                                         start=(j == 0), stop=(j == PAGES), skip_group_check=True)
                    last.then_inc(s.page_used if what == "PV" else s.own_done, 1)
                elif what == "SO":
                    g, = a
                    pe.wait_ge(s.own_ready, g + 1)
                    for k in range(KC):
                        last = pe.matmul(ps[:, 4, GB * NT * k:GB * NT * (k + 1)], own_s[:, P * k:P * k + P], selq,
                                         start=True, stop=True, skip_group_check=True)
                    last.then_inc(s.attT_done, 1)
                    n_z += 1
                elif what == "PS":
                    h, part_ = a
                    q = (q_even, q_odd)[h % 2]
                    if h == part_ == 0:
                        pe.wait_ge(s.cout_read, 2)
                    for i in (2 * part_, 2 * part_ + 1):
                        if n_ps >= 2:
                            pe.wait_ge(s.pscore_read, n_ps - 1)
                        pe.matmul(ps[:, n_ps % 2, 0:WID[i]], q[:, h // 2, P * i:P * i + P], kT[:, h // 2, 0:WID[i]],
                                  start=True, stop=True).then_inc(s.pscore_done, 1)
                        n_ps += 1
                elif what == "PT":
                    h, part_ = a
                    if h == part_ == 0:
                        pe.wait_ge(s.vt_read, KC + 1)
                        pe.wait_ge(s.ktok_read, KC + 1)
                    pe.wait_ge(s.pweight, 4 * (h + 1))
                    for fill in (FILLS[n] for n in fills(part_)):
                        if n_pt >= 2:
                            pe.wait_ge(s.ptr_read, n_pt - 1)
                        at_ = 0
                        for j in fill:
                            for i in range(j, S // P):
                                last = pe.transpose(ps[:, 6 + n_pt % 2, at_:at_ + P],
                                                    beta_p[:, h % 2, POS[i] + P * j:POS[i] + P * j + P], ident)
                                at_ += P
                        last.then_inc(s.ptr_done, 1)
                        n_pt += 1
                elif what == "PO":
                    h, = a
                    pe.wait_ge(s.ptr_read, len(FILLS) * (h + 1))
                    if h % 2 == 0 and h:
                        pe.wait_ge(s.pv_read, h // 2)
                    at_ = 0
                    for j in sum(FILLS, ()):
                        w = S - P * j
                        last = pe.matmul(ps[64 * (h % 2):64 * (h % 2) + 64, 5, P * j:S], v_tok[:, j, DH * h:DH * h + DH],
                                         wgtT_p[:, at_:at_ + w], start=(j == 0), stop=(at_ + w == sum(WID)),
                                         skip_group_check=True)
                        at_ += w
                    last.then_inc(s.pv_done, 1)
                elif what == "LS":
                    pe.wait_ge(s.y_added, KC - 1)
                    pe.wait_ge(s.ptr_read, n_pt)
                    sum_squares(ysum[:, :], 0, bank=6, n=1).then_inc(s.ln_sum, 1)
                elif what == "LQ":
                    pe.wait_ge(s.ln_cent, KC)
                    for k in range(KC):
                        pe.wait_ge(s.ln_sq, k + 1)
                        sum_squares(sq1[:, k], k, bank=6, n=KC).then_inc(s.ln_sqsum, 1)

            def merge_units(i):
                for q in range(2):
                    for j in range(3):
                        u = 3 * q + j
                        slot = u % 2
                        pe.wait_ge(s.split_done, i * 6 + (U_MERGE + u + 1))
                        if j < 2:
                            tiles = [(2 * j + m, m, hH, hL, all_k) for m in range(MT)]
                        else:
                            pe.wait_ge(s.ln_lo, KC)
                            pe.wait_ge(s.z_read, n_z)
                            pe.wait_ge(s.pv_read, H // 2)
                            tiles = [(4 + m, m, acH, acL, [(k, KC + k) for k in range(KC)]) for m in range(MT)]
                            tiles += [(6 + m, m, acH, acL, [(KC + k, k) for k in range(KC)]) for m in range(MT)]
                        for t, m, rh, rl, ks in tiles:
                            acc_tile(i * 8 + (A_MERGE // 2 + 4 * q + t // 2), t, slot, m, rh, rl, ks)

            pe.wait_ge(s.pscore_read, n_ps)
            pe.wait_ge(kt_read[0], (n_kt + 1) // 2)
            pe.wait_ge(kt_read[1], n_kt // 2)
            with pe.Fori(0, 2) as i:
                merge_units(i)
            def wo_units(i, peeled):
                for j in range(2):
                    if not peeled or j:
                        pe.wait_ge(s.split_done, i * 2 + (U_WO + j + 1))
                    for m in range(MT):
                        t = 2 * j + m
                        if not peeled or t:
                            acc_tile(i * 2 + (A_WO // 2 + t // 2), t, j, m, mH, mL)

            pe.wait_ge(s.split_done, U_WO + 1)
            pe.wait_ge(acc_read[0], A_WO // 2)
            for k in range(KD):
                pe.wait_ge(s.merged_lo, k + 1)
                last = gemm_tile(0, 0, acc(0), mH, mL, [(k, k)], start=(k == 0), stop=(k == KD - 1))
            last.then_inc(acc_done[0], 1)
            wo_units(0, True)
            with pe.Fori(1, 2) as i:
                wo_units(i, False)

            def total(need):
                pe.wait_ge(s.wo_sum, need)
                for half in range(2):
                    last = pe.matmul(ps[:, 4 + half, 0:HT], ones, ssum[:, HT * half:HT * half + HT], start=True, stop=True)
                last.then_inc(s.ssq_done, 1)

            total(KD)
            def ffn_pair(i, peeled):
                for j in range(2):
                    if not peeled or j:
                        pe.wait_ge(s.split_done, i * 2 + (U_FFI + j + 1))
                    for m in range(MT):
                        t = 2 * j + m
                        if not peeled or t:
                            acc_tile(i * 2 + (A_FFI // 2 + t // 2), t, j, m, hH, hL)

            pe.wait_ge(s.split_done, U_FFI + 1)
            pe.wait_ge(acc_read[0], A_FFI // 2)
            for k in range(KD):
                pe.wait_ge(s.norm_l, KD + k + 1)
                last = gemm_tile(0, 0, acc(0), hH, hL, [(k, k)], start=(k == 0), stop=(k == KD - 1))
                if k == KD - 1:
                    last.then_inc(acc_done[0], 1)
                pe.wait_ge(s.sq_ready2, k + 1)
                sum_squares(sq2[:, k % 2], k, bank=6).then_inc(s.ssq_done, 1)
            ffn_pair(0, True)
            with pe.Fori(1, FF // UC) as i:
                ffn_pair(i, False)
            pe.wait_ge(acc_read[0], (A_FFI + 4 * (FF // UC)) // 2)
            pe.wait_ge(acc_read[1], (A_FFI + 4 * (FF // UC)) // 2)
            n_y = 0
            for mp in range(D // UC):
                for j in range(3):
                    n = U_FFO + 3 * mp + j
                    pe.wait_ge(s.split_done, n + 1)
                    ks = [(k, UK * j + k) for k in range(min(UK, KF - UK * j))]
                    if mp == 0:
                        pe.wait_ge(s.act_lo, ks[-1][1] + 1)
                    for m in range(MT):
                        if j == 0 and mp:
                            pe.wait_ge(s.out_acc_read, 2 * (mp - 1) + m + 1)
                        last = gemm_tile(n % 2, m, acc(m), actH, actL, ks, start=(j == 0), stop=(j == 2))
                        if j == 2:
                            last.then_inc(s.out_acc_done, 1)
                        elif m == MT - 1:
                            last.then_inc(s.unit_used, 1)
                        for kind, t in TAIL[6 * mp + 2 * j + m]:
                            if kind == "o":
                                pe.wait_ge(s.out_acc_read, t + 1)
                            if n_y >= 2:
                                pe.wait_ge(s.yt_read, n_y - 1)
                            src = xT[:, t] if kind == "x" else o_fm[:, t % 2]
                            for c in range(NC):
                                pe.transpose(ps[:, 6 + n_y % 2, P * c:P * c + P], src[:, P * c:P * c + P], ident)
                            pe.transpose(ps[0:NS, 4 + n_y % 2, 0:P], src[:, S:T], ident).then_inc(s.yt_done, 1)
                            n_y += 1
            pe.wait_ge(s.wo_sum, 2 * KD)
            pe.wait_ge(s.yt_read, n_y - 1)
            for c in range(NC + 1):
                w = min(P, T - P * c)
                last = pe.matmul(ps[0:w, 4, c:c + 1], ssum[:, P * c:P * c + w], ones[:, 0:1], start=True, stop=True)
            last.then_inc(s.ssq_done, 1)

        @block.scalar
        def _(act):
            def used(n):
                if n < U_MERGE:
                    act.wait_ge(acc_done[1], n + 1)
                elif n < U_WO:
                    u = n - U_MERGE
                    act.wait_ge(acc_done[1], (A_MERGE + 8 * (u // 3) + (2, 4, 8)[u % 3]) // 2)
                elif n < U_FFO:
                    act.wait_ge(acc_done[1], A_WO // 2 + n - U_WO + 1)
                elif (n - U_FFO) % 3 < 2:
                    act.wait_ge(s.unit_used, 2 * ((n - U_FFO) // 3) + (n - U_FFO) % 3 + 1)
                else:
                    act.wait_ge(s.out_acc_done, 2 * ((n - U_FFO) // 3) + 2)

            def split_hi(n):
                act.wait_ge(raw_loaded[n % 2], 32 * (n // 2 + 1))
                if n >= 2:
                    used(n - 2)
                act.copy(w_hi[:, n % 2], w_raw[:, n % 2]).then_inc(s.hi_done, 1)

            tables = Count()

            def load_table(function):
                column = early[:, tables.n:tables.n + tables.up()]
                act.activation(column, eps, function)

            act.wait_ge(s.ld_const, 16)
            load_table(ACT.Sqrt)
            act.wait_ge(s.x_copied, 1)
            for k in range(KD):
                act.wait_ge(s.x_copied, k + 2)
                act.activation(hH[:, k], xT[:, k], ACT.Identity, scale=gain(0, k)).then_inc(s.norm_h, 1)
                if k >= 2:
                    act.wait_ge(s.sq_added, k - 1)
                act.activation(sq0[:, k % 2], xT[:, k], ACT.Square).then_inc(s.sq_ready, 1)
                if k == 2:
                    split_hi(0)

            split_hi(1)
            act.wait_ge(s.par_read, 1)

            def std(out, bank, width, need, sem=s.ssq_done):
                if need > 1:
                    load_table(ACT.Sqrt)
                act.wait_ge(sem, need)
                act.activation(halves(out[:]), ps[:, bank:bank + 2, 0:HT], ACT.Sqrt, bias=eps, scale=1.0 / width)\
                    .then_inc(s.std_ready, 1)
                load_table(ACT.Sigmoid)

            std(rstd, 4, D, 1)
            act.wait_ge(s.zeroed, 5)
            for n in range(U_MERGE):
                if 0 < n < U_MERGE - 1:
                    split_hi(n + 1)
                for m in range(MT):
                    if n in (0, 2):
                        act.wait_ge(acc_read[m], n + 1)
                        act.activation(sig_u[:, m], sig_u[:, m], ACT.Sigmoid).then_inc(s.sig_ready, 1)
                    elif n in (4, 5):
                        p = 2 * (n - 4) + m
                        act.wait_ge(acc_read[m], n + 1)
                        for r, (q, lo) in enumerate(((q_even, 0), (q_odd, 64))):
                            act.copy(q[lo:lo + 64, p], sig_u[lo:lo + 64, m, 0:S])
                            last = act.copy(q_s[lo:lo + 64, :, p, 2 * p + r, :],
                                            sig_u[lo:lo + 64, m, S:T].rearrange("p (b t) -> p b t", t=NT))
                        last.then_inc(s.q_copied, 1)
            act.wait_ge(s.sconv_done, KC)
            for k in range(KC):
                act.wait_ge(s.ktok_done, k + 1)
                act.copy(k_tok[:, :, P * k:P * k + P], ps[:, 5, :].rearrange("p (j c) -> p j c", c=P)).then_inc(s.ktok_read, 1)
            act.wait_ge(s.ktok_done, KC + 1)
            act.copy(ks_tok[:, :], ps[0:NS, 7, :]).then_inc(s.ktok_read, 1)
            act.wait_ge(s.ktok_read, KC + 1)
            act.dma_start(k_prompt[0, 0].rearrange("(j p) h d -> p j (h d)", p=P), k_tok[:]).then_inc(s.k_stored, 16)
            act.dma_start(k_sample[0].rearrange("b t h d -> (b t) (h d)"), ks_tok[:]).then_inc(s.k_stored, 16)

            def load_last(r):
                if r < 2 * GROUPS * PAGES:
                    g, kv, j = r // (2 * PAGES), r // PAGES % 2, r % PAGES
                    for b in range(GB - 1, GB):
                        seq = (GB * g + b) * PAGES + j
                        page = act.value_load(ptab[0:1, seq:seq + 1])
                        act.dma_start(pages[:, r % 2, b, :], cache[kv][bass.ds(page, 1)].rearrange("n r c -> r (n c)"))\
                            .then_inc(pages_loaded[r % 2], 16)

            def gate_sigmoid(mp, j, m):
                act.wait_ge(acc_read[m], (A_MERGE + 8 * mp + 2 * j + m) // 2 + 1)
                gate = (sig_c, sig_a)[j][:, m]
                act.activation(gate, gate, ACT.Sigmoid).then_inc(s.gates_ready, 1)

            act.wait_ge(s.bias_ready, 1)
            act.wait_ge(s.ld_table, 16)
            n_kt = 0
            for st in STEPS:
                what, a = st[0], st[1:]
                if what == "KT":
                    g, j = a
                    ks = PAGES * g + j
                    if ks >= 2:
                        act.wait_ge(s.score_done, ks - 1 + (ks - 2) // PAGES)
                    for b in range(GB):
                        act.wait_ge(s.kt_done, n_kt + 1)
                        act.copy(keysT[:, ks % 2, b], ps[:, 2 + n_kt % 2, :].rearrange("p (k c) -> p k c", c=P))\
                            .then_inc(kt_read[n_kt % 2], 1)
                        n_kt += 1
                    load_last(2 * PAGES * g + j + RING)
                elif what == "PV":
                    g, j = a
                    act.wait_ge(s.page_used, PAGES * g + j + 1)
                    load_last(2 * PAGES * g + PAGES + j + RING)
                elif what == "SC" and a[1] % 4 == 3:
                    g, j = a
                    act.wait_ge(s.score_done, PAGES * g + j + 1 + g)
                    act.activation(beta_s[:, P * (j - 3):P * (j + 1)], ps[:, 4, :], ACT.Sigmoid, bias=bias_r[:, :], scale=SCALE)\
                        .then_inc(s.z_read, 1)
                elif what == "ZN":
                    g, = a
                    act.wait_ge(s.score_done, (PAGES + 1) * (g + 1))
                    act.activation(beta_s[:, PAST:LS], ps[:, 4, 0:NS], ACT.Sigmoid, bias=bias_r[:, :], scale=SCALE)\
                        .then_inc(s.z_read, 1)
                elif what == "AT":
                    for part_ in range(3):
                        bank = 2 + n_kt % 2
                        act.wait_ge(s.kt_done, n_kt + 1)
                        if part_ < 2:
                            act.copy(wgtT_s[:, 4 * part_:4 * part_ + 4], ps[:, bank, :].rearrange("p (k c) -> p k c", c=P))\
                                .then_inc(kt_read[n_kt % 2], 1)
                        else:
                            act.copy(wgtT_s[0:NS, PAGES], ps[0:NS, bank, 0:P]).then_inc(kt_read[n_kt % 2], 1)
                        n_kt += 1
                elif what == "SO":
                    g, = a
                    act.wait_ge(s.attT_done, g + 1)
                    act.copy(acH[:, 0:KC, S + GB * NT * g:S + GB * NT * (g + 1)],
                             ps[:, 4, 0:KC * GB * NT].rearrange("p (k c) -> p k c", k=KC)).then_inc(s.attT_hi, 1)
                elif what == "PS":
                    h, part_ = a
                    if h == part_ == 0:
                        act.wait_ge(s.k_stored, 32)
                    for i in (2 * part_, 2 * part_ + 1):
                        n = 4 * h + i
                        act.wait_ge(s.pscore_done, n + 1)
                        act.activation(beta_p[:, h % 2, POS[i]:POS[i] + WID[i]], ps[:, n % 2, 0:WID[i]], ACT.Sigmoid,
                                       bias=bias_h[:, h:h + 1], scale=SCALE).then_inc(s.pscore_read, 1)
                elif what == "PT":
                    h, part_ = a
                    for f in fills(part_):
                        n = len(FILLS) * h + f
                        at_, w = (sum(S - P * j for j in sum(x, ())) for x in (FILLS[:f], FILLS[f:f + 1]))
                        act.wait_ge(s.ptr_done, n + 1)
                        act.copy(wgtT_p[:, at_:at_ + w], ps[:, 6 + n % 2, 0:w]).then_inc(s.ptr_read, 1)
                elif what == "PO" and a[0] % 2:
                    h, = a
                    act.wait_ge(s.pv_done, h + 1)
                    act.copy(acH[:, h // 2, 0:S], ps[:, 5, :]).then_inc(s.pv_hi, 1)
                elif what == "MW":
                    split_hi(U_MERGE + a[0])
                elif what == "LS":
                    for k in range(KC):
                        act.wait_ge(s.ln_cent, k + 1)
                        act.activation(sq1[:, k], yc[:, k], ACT.Square).then_inc(s.ln_sq, 1)
                elif what == "LQ":
                    std(std1, 6, C, KC, s.ln_sqsum)
                elif what == "LY":
                    k, = a
                    if k == 0:
                        act.wait_ge(s.kv_stored, 16 * (3 + NB))
                    if k < KC:
                        act.wait_ge(s.ln_t, k + 1)
                        if k >= 2:
                            act.wait_ge(s.ln_y, k - 1)
                        act.activation(sig1[:, k % 2], tmp1[:, k % 2], ACT.Sigmoid, bias=cvec(2, k)).then_inc(s.ln_sig, 1)
                    if k >= 1:
                        act.wait_ge(s.ln_y, k)
                        act.copy(acH[:, KC + k - 1], tmp1[:, (k - 1) % 2]).then_inc(s.ln_hi, 1)
                elif what == "MG":
                    gate_sigmoid(0, 0, a[0])
            for mp in range(D // UC):
                for j in range(3):
                    if mp or j:
                        split_hi(U_MERGE + 3 * mp + j + 1)
                    for m in range(MT):
                        if j < 2:
                            if mp or j:
                                gate_sigmoid(mp, j, m)
                        else:
                            act.wait_ge(s.merged_t, 2 * mp + m + 1)
                            act.copy(mH[:, 2 * mp + m], both[:, m]).then_inc(s.merged_hi, 1)

            def square_and_copy(t, a, read, sums):
                if sums is not None:
                    act.wait_ge(s.wo_sum, sums)
                act.activation(halves(sq2[:, t % 2]), a, ACT.Square).then_inc(s.out_sq, 1)
                act.copy(halves(pout[:, t]), a).then_inc(read, 1)

            for j in range(D // UC):
                split_hi(U_WO + j + 1)
                for m in range(MT):
                    t = 2 * j + m
                    act.wait_ge(acc_done[m], (A_WO + t) // 2 + 1)
                    square_and_copy(t, acc(m), acc_read[m], t - 1 if t >= 2 else None)
            std(std2, 4, D, 2)
            for k in range(KD):
                act.wait_ge(s.x1_ready, k + 1)
                if k >= 2:
                    act.wait_ge(s.ssq_done, 2 + k - 1)
                act.activation(hH[:, k], xT[:, k], ACT.Identity, scale=gain(2, k)).then_inc(s.norm_h, 1)
                act.activation(sq2[:, k % 2], xT[:, k], ACT.Square).then_inc(s.sq_ready2, 1)
            split_hi(U_FFI + 1)
            std(rstd, 6, D, KD + 2)

            def ffn_pair(i, peeled):
                for j in range(2):
                    if not peeled or j:
                        n1 = U_FFI + j + 1
                        act.wait_ge(raw_loaded[n1 % 2], i * 32 + 32 * (n1 // 2 + 1))
                        act.wait_ge(acc_done[1], i * 2 + (A_WO // 2 + n1 - 2 - U_WO + 1))
                        act.copy(w_hi[:, n1 % 2], w_raw[:, n1 % 2]).then_inc(s.hi_done, 1)
                    for m in range(MT):
                        if j == 0:
                            act.wait_ge(acc_read[m], i * 2 + (A_FFI // 2 + 1))
                            act.activation(sig_f[:, m], gate_f[:, m], ACT.Sigmoid).then_inc(s.silu_ready, 1)
                        else:
                            act.wait_ge(acc_read[m], i * 2 + (A_FFI // 2 + 2))
                            act.copy(actH[:, bass.ds(i * 2 + m, 1), :], sig_f[:, m:m + 1]).then_inc(s.act_hi, 1)

            ffn_pair(0, True)
            with act.Fori(1, FF // UC) as i:
                ffn_pair(i, False)
            for mp in range(D // UC):
                for j in range(3):
                    n = U_FFO + 3 * mp + j
                    if n + 1 < U_FFO + 12:
                        split_hi(n + 1)
                for m in range(MT):
                    t = 2 * mp + m
                    act.wait_ge(s.out_acc_done, t + 1)
                    if t >= 2:
                        act.wait_ge(s.wo_sum, KD + t - 1)
                    act.activation(halves(sq2[:, t % 2]), acc(m), ACT.Square).then_inc(s.out_sq, 1)
                    act.wait_ge(s.yt_done, tail_order.index(("o", t - 2) if t >= 2 else ("x", t)) + 1)
                    act.activation(halves(o_fm[:, t % 2]), acc(m), ACT.Identity, scale=gain(3, t)).then_inc(s.out_acc_read, 1)
            load_table(ACT.Sqrt)
            act.wait_ge(s.ssq_done, KD + 3)
            act.activation(r_tok[:, 0:NC], ps[:, 4, 0:NC], ACT.Sqrt, bias=eps, scale=1.0 / D)
            act.activation(r_tok[0:NS, NC:NC + 1], ps[0:NS, 4, NC:NC + 1], ACT.Sqrt, bias=eps[0:NS], scale=1.0 / D)\
                .then_inc(s.std_ready, 1)

        @block.vector
        def _(dve):
            step = Count()

            def split_lo(n):
                dve.wait_ge(s.hi_done, n + 1)
                dve.tensor_tensor(w_lo[:, n % 2], w_raw[:, n % 2], w_hi[:, n % 2], ALU.subtract).then_inc(s.split_done, 1)

            def rest_of_h(k, g, first):
                dve.wait_ge(s.norm_h, first + k + 1)
                dve.scalar_tensor_tensor(out=hL[:, k], in0=xT[:, k], scalar=gain(g, k), in1=hH[:, k],
                                         op0=ALU.mult, op1=ALU.subtract).then_inc(s.norm_l, 1)

            dve.wait_ge(s.xt_done, 1)
            dve.tensor_copy(xT[:, :, S:T], ps[:, 3, 0:KD * NS].rearrange("p (k t) -> p k t", t=NS))
            dve.tensor_copy(vec[:, 0:8], ps[:, 3, KD * NS:KD * NS + 8]).then_inc(s.x_copied, 1)
            dve.wait_ge(s.x_copied, 1)
            for k in range(KD + 1):
                if k < KD:
                    dve.wait_ge(s.xt_done, k + 2)
                    dve.tensor_copy(xT[:, k, 0:S], ps[:, 6 + k % 2, :]).then_inc(s.x_copied, 1)
                if k >= 1:
                    rest_of_h(k - 1, 0, 0)
                if k == 3:
                    dve.wait_ge(s.par_done, 1)
                    dve.tensor_copy(vec[:, 8:44], ps[:, 2, 8:44])
                    dve.tensor_copy(dw[:], ps[:, 2, 64:64 + KC * CW].rearrange("p (k w) -> p k w", w=CW))
                    dve.tensor_copy(bias_h[:, :], ps[:, 2, 192:200]).then_inc(s.par_read, 1)
                if k == 3:
                    split_lo(0)

            def reciprocal(a, need):
                dve.wait_ge(s.std_ready, need)
                dve.reciprocal(a[:, :], a[:, :]).then_inc(s.dve_step, step.up())
                dve.wait_ge(s.dve_step, step.n)

            split_lo(1)
            reciprocal(rstd, 1)

            def bias_and_history():
                dve.wait_ge(s.par_read, 1)
                dve.tensor_tensor(bias_own[:, :], bias_h[:, :], headmask, ALU.mult).then_inc(s.dve_step, step.up())
                dve.wait_ge(s.dve_step, step.n)
                dve.tensor_reduce(bias_r[:, :], bias_own[:, :], AX.X, ALU.add).then_inc(s.bias_ready, 1)
                dve.wait_ge(s.st_done, GROUPS)
                for g in range(GROUPS):
                    for k in range(KC):
                        last = dve.tensor_copy(uS[:, k, GB * g:GB * g + GB, 0:HIST],
                                               ps[:, 6 + g, GB * HIST * k:GB * HIST * (k + 1)].rearrange("p (b r) -> p b r", r=HIST))
                    last.then_inc(s.st_read, 1)

            def sample_conv(ct):
                if ct:
                    dve.wait_ge(s.sconv_done, ct)
                for t in range(NT):
                    last = dve.tensor_tensor(prod[:, t], uS[:, ct, :, t:t + CW],
                                             dw[:, ct].unsqueeze(1).to_broadcast([P, NB, CW]), ALU.mult)
                last.then_inc(s.dve_step, step.up())
                dve.wait_ge(s.dve_step, step.n)
                y = yc[:, ct, S:T].rearrange("p (b t) -> p t b", t=NT)
                dve.tensor_reduce(y, prod[:], AX.X, ALU.add).then_inc(s.dve_step, step.up())
                dve.wait_ge(s.dve_step, step.n)
                dve.tensor_scalar(yc[:, ct, S:T], yc[:, ct, S:T], cvec(0, ct), None, ALU.add).then_inc(s.sconv_done, 1)

            conv_at = 0

            def prompt_conv(upto):
                nonlocal conv_at
                while conv_at < min(upto, 2 * CW):
                    w, ct = conv_at // 2, conv_at % 2
                    y, u = yc[:, ct, 0:S], uP[:, ct, w:w + S]
                    if w == 0:
                        dve.tensor_scalar(y, u, dw[:, ct, 0:1], cvec(0, ct), ALU.mult, ALU.add).then_inc(s.dve_step, step.up())
                    else:
                        dve.wait_ge(s.dve_step, step.n - 1 if conv_at < 2 * CW - 1 else step.n)
                        ins = dve.scalar_tensor_tensor(out=y, in0=u, scalar=dw[:, ct, w:w + 1], in1=y, op0=ALU.mult, op1=ALU.add)
                        if w < CW - 1:
                            ins.then_inc(s.dve_step, step.up())
                        else:
                            ins.then_inc(s.dconv_done, 1)
                    conv_at += 1

            for n in range(U_MERGE):
                if 0 < n < U_MERGE - 1:
                    split_lo(n + 1)
                for m in range(MT):
                    a = acc(m)
                    if n not in (1, 3):
                        if n in (2, 4):
                            dve.wait_ge(acc_read[m], n)
                        if n == 5:
                            dve.wait_ge(s.q_copied, m + 1)
                        out = (sig_u[:, m] if n < 6 else kT[:, 2 * (n - 6) + m] if n < 8 else vT[:, 2 * (n - 8) + m])
                        dve.wait_ge(acc_done[m], n + 1)
                        dve.tensor_tensor(halves(out), a, halves(rstd[:]), ALU.mult).then_inc(acc_read[m], 1)
                    else:
                        ct = 2 * (n // 2) + m
                        if n == 1 and m == 0:
                            dve.wait_ge(s.zeroed, 5)
                            dve.wait_ge(s.st_read, GROUPS)
                        dve.wait_ge(s.sig_ready, n + m)
                        dve.tensor_tensor(sig_u[:, m], sig_u[:, m], rstd[:, :], ALU.mult).then_inc(s.dve_step, step.up())
                        dve.wait_ge(acc_done[m], n + 1)
                        dve.wait_ge(s.dve_step, step.n)
                        dve.tensor_tensor(uP[:, ct, HIST:HIST + HT], a[:, 0, :], sig_u[:, m, 0:HT], ALU.mult)
                        dve.tensor_tensor(uP[:, ct, HIST + HT:HIST + S], a[:, 1, 0:S1], sig_u[:, m, HT:S], ALU.mult)
                        dve.tensor_tensor(uS[:, ct, :, HIST:HIST + NT], a[:, 1, S1:HT].rearrange("p (b t) -> p b t", t=NT),
                                          sig_u[:, m, S:T].rearrange("p (b t) -> p b t", t=NT), ALU.mult)
                        dve.tensor_tensor(u_new[:, ct], a[:, 1, S1:HT], sig_u[:, m, S:T], ALU.mult).then_inc(acc_read[m], 1)
                if n == 0:
                    bias_and_history()
                if n >= 2:
                    if n == 2:
                        for m in range(MT):
                            dve.wait_ge(acc_read[m], 2)
                    if n == 4:
                        for m in range(MT):
                            dve.wait_ge(acc_read[m], 4)
                    if 4 <= n < 8:
                        sample_conv(n - 4)
                    prompt_conv((11, 22, 29, 36, 43, 51, 2 * CW, 2 * CW)[n - 2])
            dve.wait_ge(s.zeroed, 5)
            for k in range(KC):
                dve.wait_ge(s.vt_done, k + 1)
                dve.tensor_copy(v_tok[:, :, P * k:P * k + P], ps[:, 4, :].rearrange("p (j c) -> p j c", c=P)).then_inc(s.vt_read, 1)
            dve.wait_ge(s.vt_done, KC + 1)
            dve.tensor_copy(vs_tok[0:NS, :], ps[0:NS, 6, :]).then_inc(s.vt_read, 1)
            dve.wait_ge(s.cout_done, 1)
            dve.tensor_copy(conv_tail[:, :], ps[0:HIST, 0, :]).then_inc(s.cout_read, 1)
            dve.tensor_copy(conv_new[:, :], ps[0:NS, 1, :]).then_inc(s.cout_read, 1)

            def gate_tile(mp, j, m):
                dve.wait_ge(acc_done[m], (A_MERGE + 8 * mp + 2 * j + m) // 2 + 1)
                dve.tensor_tensor(halves((sig_c, sig_a)[j][:, m]), acc(m), halves(rstd[:]), ALU.mult).then_inc(acc_read[m], 1)

            def stick(beta, left, width, out_sem):
                dve.tensor_scalar(left[:, 0:width], beta, -1.0, 1.0, ALU.mult, ALU.add).then_inc(s.dve_step, step.up())
                dve.wait_ge(s.dve_step, step.n)
                back = left[:, 0:width][:, ::-1]
                dve.tensor_tensor_scan(back, back, back, 1.0, ALU.mult, ALU.min).then_inc(s.dve_step, step.up())
                dve.wait_ge(s.dve_step, step.n)
                dve.tensor_tensor(beta, beta, left[:, 1:width + 1], ALU.mult).then_inc(out_sem, 1)

            for st in STEPS:
                what, a = st[0], st[1:]
                if what == "ZN":
                    g, = a
                    dve.wait_ge(s.z_read, 4 * g + 3)
                    if g == 0:
                        dve.memset(stick_s[:, LS:LS + 1], 1.0)
                        dve.memset(wgtT_s[:, PAGES], 0.0)
                    dve.tensor_tensor(beta_s[:, PAST:LS], beta_s[:, PAST:LS], newmask(g), ALU.mult).then_inc(s.dve_step, step.up())
                    dve.wait_ge(s.dve_step, step.n)
                    stick(beta_s[:, :], stick_s, LS, s.weight_s)
                elif what == "PN":
                    g, = a
                    dve.wait_ge(s.own_done, g + 1)
                    dve.tensor_tensor(own_s[:, :].rearrange("p (h d) -> p h d", d=DH), ps[:, 4, :].rearrange("p (h d) -> p h d", d=DH),
                                      headmask.unsqueeze(2).to_broadcast([P, H, DH]), ALU.mult).then_inc(s.own_ready, 1)
                elif what == "SO":
                    g, = a
                    cols = slice(S + GB * NT * g, S + GB * NT * (g + 1))
                    dve.wait_ge(s.attT_hi, g + 1)
                    dve.tensor_tensor(acL[:, 0:KC, cols], ps[:, 4, 0:KC * GB * NT].rearrange("p (k c) -> p k c", k=KC),
                                      acH[:, 0:KC, cols], ALU.subtract).then_inc(s.z_read, 1)
                elif what == "PS":
                    h, part_ = a
                    for i in (2 * part_, 2 * part_ + 1):
                        dve.wait_ge(s.pscore_read, 4 * h + i + 1)
                        left = stick_p[i % 2][:, S - WID[i]:S + 1]
                        if h == 0 and i < 2:
                            dve.memset(left[:, WID[i]:], 1.0)
                        beta = beta_p[:, h % 2, POS[i]:POS[i] + WID[i]]
                        diag = beta[:, P * i:P * i + P]
                        dve.tensor_tensor(diag, diag, tri, ALU.mult).then_inc(s.dve_step, step.up())
                        dve.wait_ge(s.dve_step, step.n)
                        if 4 * h + i >= 2:
                            dve.wait_ge(s.pweight, 4 * h + i - 1)
                        stick(beta, left, WID[i], s.pweight)
                elif what == "PO" and a[0] % 2:
                    h, = a
                    dve.wait_ge(s.pv_hi, h // 2 + 1)
                    dve.tensor_tensor(acL[:, h // 2, 0:S], ps[:, 5, :], acH[:, h // 2, 0:S], ALU.subtract).then_inc(s.pv_read, 1)
                elif what == "MW":
                    split_lo(U_MERGE + a[0])
                elif what == "LS":
                    dve.wait_ge(s.ln_sum, 1)
                    for k in range(KC):
                        dve.scalar_tensor_tensor(out=halves(yc[:, k]), in0=ps[:, 6:8, 0:HT], scalar=-1.0 / C, in1=halves(yc[:, k]),
                                                 op0=ALU.mult, op1=ALU.add).then_inc(s.ln_cent, 1)
                elif what == "LQ":
                    reciprocal(std1, 2)
                elif what == "LY":
                    k, = a
                    if k < KC:
                        if k >= 2:
                            dve.wait_ge(s.ln_lo, k - 1)
                        dve.scalar_tensor_tensor(out=tmp1[:, k % 2], in0=yc[:, k], scalar=cvec(1, k), in1=std1[:, :],
                                                 op0=ALU.mult, op1=ALU.mult).then_inc(s.ln_t, 1)
                    if k >= 1:
                        t = tmp1[:, (k - 1) % 2]
                        dve.wait_ge(s.ln_sig, k)
                        dve.scalar_tensor_tensor(out=t, in0=t, scalar=cvec(2, k - 1), in1=sig1[:, (k - 1) % 2],
                                                 op0=ALU.add, op1=ALU.mult).then_inc(s.ln_y, 1)
                        dve.wait_ge(s.ln_hi, k)
                        dve.tensor_tensor(acL[:, KC + k - 1], t, acH[:, KC + k - 1], ALU.subtract).then_inc(s.ln_lo, 1)
                elif what == "MG":
                    gate_tile(0, 0, a[0])
            for mp in range(D // UC):
                for j in range(2):
                    if mp or j:
                        split_lo(U_MERGE + 3 * mp + j + 1)
                        for m in range(MT):
                            gate_tile(mp, j, m)
                c0 = A_MERGE + 8 * mp + 4
                if mp:
                    dve.wait_ge(s.merged_lo, 2 * mp)
                dve.wait_ge(s.gates_ready, 4 * (mp + 1))
                for m in range(MT):
                    dve.wait_ge(acc_done[m], c0 // 2 + 1)
                    dve.tensor_tensor(halves(part[:, m]), acc(m), halves(sig_c[:, m]), ALU.mult).then_inc(acc_read[m], 1)
                split_lo(U_MERGE + 3 * mp + 3)
                for m in range(MT):
                    dve.wait_ge(acc_done[m], c0 // 2 + 2)
                    dve.tensor_tensor(halves(both[:, m]), acc(m), halves(sig_a[:, m]), ALU.mult).then_inc(acc_read[m], 1)
                    dve.wait_ge(acc_read[m], c0 // 2 + 2)
                    dve.tensor_tensor(both[:, m], both[:, m], part[:, m], ALU.add).then_inc(s.merged_t, 1)
                for m in range(MT):
                    dve.wait_ge(s.merged_hi, 2 * mp + m + 1)
                    dve.tensor_tensor(mL[:, 2 * mp + m], both[:, m], mH[:, 2 * mp + m], ALU.subtract).then_inc(s.merged_lo, 1)

            def add_squares(t, first):
                if t == 0:
                    dve.tensor_copy(ssum[:, :], sq2[:, 0]).then_inc(s.wo_sum, 1)
                else:
                    dve.wait_ge(s.wo_sum, first + t)
                    dve.tensor_tensor(ssum[:, :], ssum[:, :], sq2[:, t % 2], ALU.add).then_inc(s.wo_sum, 1)

            for j in range(D // UC):
                split_lo(U_WO + j + 1)
                for m in range(MT):
                    dve.wait_ge(s.out_sq, 2 * j + m + 1)
                    add_squares(2 * j + m, 0)
            reciprocal(std2, 3)

            for k in range(KD + 1):
                if k < KD:
                    if k >= 2:
                        dve.wait_ge(s.x1_ready, k - 1)
                    dve.scalar_tensor_tensor(out=tmp2[:, k % 2], in0=pout[:, k], scalar=gain(1, k), in1=std2[:, :],
                                             op0=ALU.mult, op1=ALU.mult).then_inc(s.mix_ready, 1)
                if k >= 1:
                    rest_of_h(k - 1, 2, KD)
            split_lo(U_FFI + 1)
            reciprocal(rstd, 4)
            def ffn_pair(i, peeled):
                for j in range(2):
                    n1 = U_FFI + j + 1
                    for m in range(MT):
                        if m == 1 and (not peeled or j):
                            dve.wait_ge(s.hi_done, i * 2 + (n1 + 1))
                            dve.tensor_tensor(w_lo[:, n1 % 2], w_raw[:, n1 % 2], w_hi[:, n1 % 2], ALU.subtract).then_inc(s.split_done, 1)
                        if j == 0:
                            dve.wait_ge(acc_done[m], i * 2 + (A_FFI // 2 + 1))
                            dve.tensor_tensor(halves(gate_f[:, m]), acc(m), halves(rstd[:]), ALU.mult).then_inc(acc_read[m], 1)
                        else:
                            dve.wait_ge(s.silu_scaled, i * 2 + (m + 1))
                            dve.wait_ge(acc_done[m], i * 2 + (A_FFI // 2 + 2))
                            dve.tensor_tensor(halves(sig_f[:, m]), acc(m), halves(sig_f[:, m]), ALU.mult).then_inc(acc_read[m], 1)
                for m in range(MT):
                    dve.wait_ge(s.act_hi, i * 2 + (m + 1))
                    dve.tensor_tensor(actL[:, bass.ds(i * 2 + m, 1), :], sig_f[:, m:m + 1], actH[:, bass.ds(i * 2 + m, 1), :],
                                      ALU.subtract).then_inc(s.act_lo, 1)

            ffn_pair(0, True)
            with dve.Fori(1, FF // UC) as i:
                ffn_pair(i, False)
            n_y = 0
            for mp in range(D // UC):
                for j in range(3):
                    n = U_FFO + 3 * mp + j
                    for m in range(MT):
                        if m == 0 and n + 1 < U_FFO + 12:
                            split_lo(n + 1)
                        if j == 2:
                            dve.wait_ge(s.out_sq, KD + 2 * mp + m + 1)
                            add_squares(2 * mp + m, KD)
                        for kind, t in TAIL[6 * mp + 2 * j + m]:
                            big, small = (x1_tok, x1s_tok) if kind == "x" else (o_tok, os_tok)
                            dve.wait_ge(s.yt_done, n_y + 1)
                            dve.tensor_copy(big[:, :, P * t:P * t + P], ps[:, 6 + n_y % 2, :].rearrange("p (c d) -> p c d", d=P))
                            dve.tensor_copy(small[:, P * t:P * t + P], ps[0:NS, 4 + n_y % 2, 0:P])\
                                .then_inc(s.yt_read, 1)
                            n_y += 1
            dve.wait_ge(s.std_ready, 5)
            dve.reciprocal(r_tok[:, 0:NC], r_tok[:, 0:NC])
            dve.reciprocal(r_tok[0:NS, NC:NC + 1], r_tok[0:NS, NC:NC + 1]).then_inc(s.dve_step, step.up())
            dve.wait_ge(s.dve_step, step.n)
            for c in range(NC):
                dve.scalar_tensor_tensor(out=o_tok[:, c], in0=o_tok[:, c], scalar=r_tok[:, c:c + 1], in1=x1_tok[:, c],
                                         op0=ALU.mult, op1=ALU.add).then_inc(s.y_ready, 1)
            dve.scalar_tensor_tensor(out=os_tok[:, :], in0=os_tok[:, :], scalar=r_tok[0:NS, NC:NC + 1], in1=x1s_tok[:, :],
                                     op0=ALU.mult, op1=ALU.add).then_inc(s.y_ready, 1)

        @block.gpsimd
        def _(pool):
            for n, zero in enumerate((q_even[64:128], q_odd[0:64], q_s[:], vs_tok[:], uP[:, :, 0:HIST])):
                if n:
                    pool.wait_ge(s.zeroed, n)
                pool.memset(zero, 0.0).then_inc(s.zeroed, 1)
            for k in range(KD):
                pool.wait_ge(s.sq_ready, k + 1)
                if k == 0:
                    pool.tensor_copy(ssum0[:, :], sq0[:, 0]).then_inc(s.sq_added, 1)
                else:
                    pool.wait_ge(s.sq_added, k)
                    pool.tensor_tensor(ssum0[:, :], ssum0[:, :], sq0[:, k % 2], ALU.add).then_inc(s.sq_added, 1)
            tap = Count()
            for ct in range(2, KC):
                pool.wait_ge(acc_read[ct % 2], 2 * (ct // 2) + 2)
                y = yc[:, ct, 0:S]
                pool.tensor_scalar(y, uP[:, ct, 0:S], dw[:, ct, 0:1], cvec(0, ct), ALU.mult, ALU.add).then_inc(s.conv_tap, tap.up())
                for w in range(1, CW):
                    product = tap_prod[:, w % 2]
                    pool.tensor_scalar(product, uP[:, ct, w:w + S], dw[:, ct, w:w + 1], None, ALU.mult).then_inc(s.conv_tap, tap.up())
                    pool.wait_ge(s.conv_tap, tap.n)
                    if w < CW - 1:
                        pool.tensor_tensor(y, y, product, ALU.add).then_inc(s.conv_tap, tap.up())
                    else:
                        pool.tensor_tensor(y, y, product, ALU.add).then_inc(s.conv_done, 1)
            pool.wait_ge(s.conv_done, 2)
            pool.wait_ge(s.dconv_done, 2)
            pool.wait_ge(s.sconv_done, KC)
            for k in range(1, KC):
                if k > 1:
                    pool.wait_ge(s.y_added, k - 1)
                pool.tensor_tensor(ysum[:, :], yc[:, 0] if k == 1 else ysum[:, :], yc[:, k], ALU.add).then_inc(s.y_added, 1)
            for k in range(KD):
                pool.wait_ge(s.mix_ready, k + 1)
                pool.tensor_tensor(xT[:, k], xT[:, k], tmp2[:, k % 2], ALU.add).then_inc(s.x1_ready, 1)
            with pool.Fori(0, FF // UC) as i:
                for m in range(MT):
                    pool.wait_ge(s.silu_ready, i * 2 + (m + 1))
                    pool.tensor_tensor(sig_f[:, m], sig_f[:, m], gate_f[:, m], ALU.mult).then_inc(s.silu_times, 1)
                for m in range(MT):
                    pool.wait_ge(s.silu_times, i * 2 + (m + 1))
                    pool.tensor_tensor(sig_f[:, m], sig_f[:, m], rstd[:, :], ALU.mult).then_inc(s.silu_scaled, 1)


_INS = ["x_prompt", "x_sample", "cache_k", "cache_v", "state_conv", "page_table", "norm_pre_mix", "norm_post_mix",
        "norm_pre_ffn", "norm_post_ffn", "w_in", "conv_dw", "conv_b", "conv_ln_g", "conv_ln_b", "w_conv_out",
        "att_bias", "w_att_out", "w_o", "w_ffn_in", "w_ffn_out"]
_OUTS = [(1, S, D), (NB, NT, D), (1, 1, S, H, DH), (1, 1, S, H, DH), (1, 1, HIST, C), (1, NB, NT, H, DH),
         (1, NB, NT, H, DH), (1, NB, HIST, C)]


def kernel(**inputs):
    import concourse.bacc as bacc
    from concourse.bass_utils import run_bass_kernel_spmd

    nc = bacc.Bacc("TRN2", target_bir_lowering=False, num_devices=1)
    arrays, args = {}, []
    for name in _INS + ["consts"]:
        a = constants() if name == "consts" else np.ascontiguousarray(inputs[name])
        arrays[f"in_{name}"] = a
        args.append(nc.dram_tensor(f"in_{name}", a.shape, mybir.dt.from_np(a.dtype), kind="ExternalInput").ap())
    for i, shape in enumerate(_OUTS):
        args.append(nc.dram_tensor(f"out_{i}", shape, F32, kind="ExternalOutput").ap())
    layer_kernel(nc, *args)
    r = run_bass_kernel_spmd(nc, [arrays], core_ids=[0])
    return tuple(r.results[0][f"out_{i}"] for i in range(len(_OUTS)))
```
